# Optimizing a Trainium2 kernel written in Bass

```python
import jax, jax.numpy as jnp
from jax import lax
import numpy as np

D_MODEL = 1024
BATCH = 1
SEQ = 512
DEPTH = 2

CHUNK = 64
Q_BLOCK = 128
NORM_EPS = 1e-6
ROPE_THETA = 500000.0

A_HEADS = 8
A_KV_HEADS = 2
A_HEAD_DIM = 64
IDX_HEADS = 4
IDX_DIM = 64
TOPK_MAX = 256
ROT_DIM = A_HEAD_DIM // 4
B_HEADS = 8
B_HEAD_DIM = 64
B_LEFT_CHUNKS = 8
B_MAX_REL = 128
C_HEADS = 4
C_HEAD_DIM = 128
C_CONV = 4

A_WIDTH = A_HEADS * A_HEAD_DIM
A_KV_WIDTH = A_KV_HEADS * A_HEAD_DIM
B_WIDTH = B_HEADS * B_HEAD_DIM
C_WIDTH = C_HEADS * C_HEAD_DIM
BRANCH_WIDTH = 512
N_BRANCH = 3
IN_SPLITS = (A_WIDTH, A_KV_WIDTH, A_KV_WIDTH, IDX_HEADS * IDX_DIM, IDX_DIM, IDX_HEADS, A_WIDTH,
             B_WIDTH, B_WIDTH, B_WIDTH, B_WIDTH,
             C_WIDTH, C_WIDTH, C_WIDTH, C_HEADS, C_HEADS, C_WIDTH, C_WIDTH,
             N_BRANCH * D_MODEL)
IN_WIDTH = sum(IN_SPLITS)

kernel_name = 'hybrid_dsa_chunkattn_mlstm_block'

def rms_norm(x, g):
    xf = x.astype(jnp.float32)
    y = xf * lax.rsqrt(jnp.mean(xf * xf, axis=-1, keepdims=True) + NORM_EPS)
    return (y * g.astype(jnp.float32)).astype(x.dtype)

def rope_tables(S):
    half = ROT_DIM // 2
    inv_freq = 1.0 / (ROPE_THETA ** (jnp.arange(half, dtype=jnp.float32) * 2.0 / ROT_DIM))
    ang = jnp.arange(S, dtype=jnp.float32)[:, None] * inv_freq[None, :]
    return jnp.cos(ang), jnp.sin(ang)

def partial_rope(x, cos, sin):
    half = ROT_DIM // 2
    xf = x.astype(jnp.float32)
    x1 = xf[..., :half]
    x2 = xf[..., half:ROT_DIM]
    c = cos[:, None, :]
    s = sin[:, None, :]
    return jnp.concatenate([x1 * c - x2 * s, x2 * c + x1 * s, xf[..., ROT_DIM:]], axis=-1).astype(x.dtype)

def causal_depthwise_conv(x, w, b):
    K, C = w.shape
    y = lax.conv_general_dilated(x, w[:, None, :].astype(x.dtype), window_strides=(1,), padding=[(K - 1, 0)],
                                 dimension_numbers=('NWC', 'WIO', 'NWC'), feature_group_count=C)
    return y + b.astype(x.dtype)

def indexer_sparse_attention(q, k, v, iq, ik, iw):
    B, S = q.shape[0], q.shape[1]
    n_sel = min(TOPK_MAX, S // 4)
    nqb = S // Q_BLOCK
    G = A_HEADS // A_KV_HEADS
    scale = A_HEAD_DIM ** -0.5
    key_chunk = jnp.arange(S) // CHUNK
    iw = iw.astype(jnp.float32) * (IDX_DIM ** -0.5 * IDX_HEADS ** -0.5)

    def to_blocks(t):
        return jnp.swapaxes(t.reshape((B, nqb, Q_BLOCK) + t.shape[2:]), 0, 1)

    def one_block(args):
        qb, iqb, iwb, blk = args
        q_chunk = (blk * Q_BLOCK + jnp.arange(Q_BLOCK)) // CHUNK
        logits = jnp.einsum('bqhd,bsd->bqhs', iqb, ik, preferred_element_type=jnp.float32)
        score = jnp.einsum('bqhs,bqh->bqs', jax.nn.relu(logits), iwb)
        admissible = key_chunk[None, :] <= q_chunk[:, None]
        score = jnp.where(admissible[None], score, -jnp.inf)
        _, sel = lax.top_k(score, n_sel)
        sel_valid = key_chunk[sel] <= q_chunk[None, :, None]
        k_sel = jax.vmap(lambda kb, ib: kb[ib])(k, sel)
        v_sel = jax.vmap(lambda vb, ib: vb[ib])(v, sel)
        qg = qb.reshape(B, Q_BLOCK, A_KV_HEADS, G, A_HEAD_DIM)
        s = jnp.einsum('bqhgd,bqnhd->bhgqn', qg, k_sel, preferred_element_type=jnp.float32) * scale
        s = jnp.where(sel_valid[:, None, None], s, -jnp.inf)
        p = jax.nn.softmax(s, axis=-1).astype(v.dtype)
        o = jnp.einsum('bhgqn,bqnhd->bqhgd', p, v_sel)
        return o.reshape(B, Q_BLOCK, A_WIDTH)

    out = lax.map(one_block, (to_blocks(q), to_blocks(iq), to_blocks(iw), jnp.arange(nqb)))
    return jnp.swapaxes(out, 0, 1).reshape(B, S, A_WIDTH)

def chunked_relpos_attention(q, k, v, rel_bias):
    B, S = q.shape[0], q.shape[1]
    nc = S // CHUNK
    pad = B_LEFT_CHUNKS * CHUNK
    band = pad + CHUNK
    scale = B_HEAD_DIM ** -0.5
    kp = jnp.pad(k, ((0, 0), (pad, 0), (0, 0), (0, 0)))
    vp = jnp.pad(v, ((0, 0), (pad, 0), (0, 0), (0, 0)))
    rel = (pad + jnp.arange(CHUNK))[:, None] - jnp.arange(band)[None, :]
    bias = rel_bias.astype(jnp.float32)[:, jnp.clip(rel, -B_MAX_REL, B_MAX_REL) + B_MAX_REL]
    qc = jnp.swapaxes(q.reshape(B, nc, CHUNK, B_HEADS, B_HEAD_DIM), 0, 1)

    def one_chunk(args):
        qb, c = args
        start = c * CHUNK
        kb = lax.dynamic_slice_in_dim(kp, start, band, axis=1)
        vb = lax.dynamic_slice_in_dim(vp, start, band, axis=1)
        key_pos = start - pad + jnp.arange(band)
        s = jnp.einsum('bqhd,bkhd->bhqk', qb, kb, preferred_element_type=jnp.float32) * scale + bias[None]
        s = jnp.where((key_pos >= 0)[None, None, None, :], s, -jnp.inf)
        p = jax.nn.softmax(s, axis=-1).astype(v.dtype)
        o = jnp.einsum('bhqk,bkhd->bqhd', p, vb)
        return o.reshape(B, CHUNK, B_WIDTH)

    out = lax.map(one_chunk, (qc, jnp.arange(nc)))
    return jnp.swapaxes(out, 0, 1).reshape(B, S, B_WIDTH)

def mlstm_chunkwise(q, k, v, i_pre, f_pre, o_pre):
    B, S = q.shape[0], q.shape[1]
    nc = S // CHUNK
    H, d = C_HEADS, C_HEAD_DIM

    def chunks(t):
        t = t.astype(jnp.float32).reshape((B, nc, CHUNK) + t.shape[2:])
        return jnp.moveaxis(t, 3, 1)

    qc = chunks(q) * (d ** -0.5)
    kc = chunks(k)
    vc = chunks(v)
    ig = chunks(i_pre)
    log_f = jax.nn.log_sigmoid(chunks(f_pre))
    b = jnp.cumsum(log_f, axis=-1)
    g = b[..., -1]
    w_log = g[..., None] - b + ig
    m_loc = jnp.max(w_log, axis=-1)
    w = jnp.exp(w_log - m_loc[..., None])
    kv = jnp.einsum('bhcl,bhcld,bhcle->bhcde', w, kc, vc)
    ksum = jnp.einsum('bhcl,bhcld->bhcd', w, kc)

    def step(carry, xs):
        C, n, m = carry
        kv_c, ks_c, g_c, ml_c = xs
        m_new = jnp.maximum(g_c + m, ml_c)
        a = jnp.exp(g_c + m - m_new)
        bb = jnp.exp(ml_c - m_new)
        C_new = a[..., None, None] * C + bb[..., None, None] * kv_c
        n_new = a[..., None] * n + bb[..., None] * ks_c
        return (C_new, n_new, m_new), (C, n, m)

    init = (jnp.zeros((B, H, d, d), jnp.float32), jnp.zeros((B, H, d), jnp.float32), jnp.zeros((B, H), jnp.float32))
    xs = (jnp.moveaxis(kv, 2, 0), jnp.moveaxis(ksum, 2, 0), jnp.moveaxis(g, 2, 0), jnp.moveaxis(m_loc, 2, 0))
    _, (C_prev, n_prev, m_prev) = lax.scan(step, init, xs)
    C_prev = jnp.moveaxis(C_prev, 0, 2)
    n_prev = jnp.moveaxis(n_prev, 0, 2)
    m_prev = jnp.moveaxis(m_prev, 0, 2)

    causal = jnp.tril(jnp.ones((CHUNK, CHUNK), dtype=bool))
    D = jnp.where(causal, b[..., :, None] - b[..., None, :] + ig[..., None, :], -jnp.inf)
    m_inter = b + m_prev[..., None]
    m_row = jnp.maximum(m_inter, jnp.max(D, axis=-1))
    inter_scale = jnp.exp(m_inter - m_row)
    s_qk = jnp.einsum('bhcld,bhcsd->bhcls', qc, kc) * jnp.exp(D - m_row[..., None])
    num = jnp.einsum('bhcls,bhcse->bhcle', s_qk, vc) + inter_scale[..., None] * jnp.einsum('bhcld,bhcde->bhcle', qc, C_prev)
    den = jnp.sum(s_qk, axis=-1) + inter_scale * jnp.einsum('bhcld,bhcd->bhcl', qc, n_prev)
    h = num / jnp.maximum(jnp.abs(den), jnp.exp(-m_row))[..., None]
    h = jnp.moveaxis(h, 1, 3).reshape(B, S, H, d)
    return jax.nn.sigmoid(o_pre.astype(jnp.float32)) * h

def head_layer_norm(h, w):
    mu = jnp.mean(h, axis=-1, keepdims=True)
    hc = h - mu
    y = hc * lax.rsqrt(jnp.mean(hc * hc, axis=-1, keepdims=True) + NORM_EPS)
    return y.reshape(h.shape[0], h.shape[1], -1) * w.astype(jnp.float32)

def hybrid_layer(x, cos, sin, norm_g, w_in, b_in, f_bias, conv_w, conv_b, rel_bias, c_norm_w, w_branch, w_out):
    B, S, _ = x.shape
    h = rms_norm(x, norm_g)
    proj = jnp.einsum('bsd,de->bse', h, w_in) + b_in
    offsets = np.cumsum(IN_SPLITS)[:-1].tolist()
    (a_q, a_k, a_v, i_q, i_k, i_w, a_z, b_q, b_k, b_v, b_z,
     c_q, c_k, c_v, c_i, c_f, c_o, c_z, gates) = jnp.split(proj, offsets, axis=-1)
    a_q = partial_rope(a_q.reshape(B, S, A_HEADS, A_HEAD_DIM), cos, sin)
    a_k = partial_rope(a_k.reshape(B, S, A_KV_HEADS, A_HEAD_DIM), cos, sin)
    a_v = a_v.reshape(B, S, A_KV_HEADS, A_HEAD_DIM)
    i_q = partial_rope(i_q.reshape(B, S, IDX_HEADS, IDX_DIM), cos, sin)
    i_k = partial_rope(i_k.reshape(B, S, 1, IDX_DIM), cos, sin)[:, :, 0]
    y_a = indexer_sparse_attention(a_q, a_k, a_v, i_q, i_k, i_w)
    y_b = chunked_relpos_attention(b_q.reshape(B, S, B_HEADS, B_HEAD_DIM), b_k.reshape(B, S, B_HEADS, B_HEAD_DIM),
                                   b_v.reshape(B, S, B_HEADS, B_HEAD_DIM), rel_bias)
    qk = jax.nn.silu(causal_depthwise_conv(jnp.concatenate([c_q, c_k], axis=-1), conv_w, conv_b))
    c_q, c_k = jnp.split(qk, 2, axis=-1)
    y_c = mlstm_chunkwise(c_q.reshape(B, S, C_HEADS, C_HEAD_DIM), c_k.reshape(B, S, C_HEADS, C_HEAD_DIM),
                          c_v.reshape(B, S, C_HEADS, C_HEAD_DIM), c_i, c_f + f_bias,
                          c_o.reshape(B, S, C_HEADS, C_HEAD_DIM))
    y_c = head_layer_norm(y_c, c_norm_w).astype(x.dtype)
    branches = jnp.stack([y_a * jax.nn.silu(a_z), y_b * jax.nn.silu(b_z), y_c * jax.nn.silu(c_z)], axis=2)
    y = jnp.einsum('bsnw,nwd->bsnd', branches, w_branch)
    gate = jax.nn.sigmoid(gates.reshape(B, S, N_BRANCH, D_MODEL))
    merged = jnp.sum(gate * y, axis=2)
    return x + jnp.einsum('bsd,de->bse', merged, w_out)

def setup_inputs(seed: int = 0) -> dict:
    key = jax.random.key(seed)
    ks = jax.random.split(key, 13)
    f32 = jnp.float32
    x = jax.random.normal(ks[0], (BATCH, SEQ, D_MODEL), f32)
    norm_g = 1.0 + 0.01 * jax.random.normal(ks[1], (DEPTH, D_MODEL), f32)
    w_in = jax.random.normal(ks[2], (DEPTH, D_MODEL, IN_WIDTH), f32) * D_MODEL ** -0.5
    b_in = 0.01 * jax.random.normal(ks[3], (DEPTH, IN_WIDTH), f32)
    f_bias = jax.random.uniform(ks[4], (DEPTH, C_HEADS), f32, 3.0, 6.0)
    conv_w = jax.random.normal(ks[5], (DEPTH, C_CONV, 2 * C_WIDTH), f32) * C_CONV ** -0.5
    conv_b = 0.01 * jax.random.normal(ks[6], (DEPTH, 2 * C_WIDTH), f32)
    rel_bias = 0.1 * jax.random.normal(ks[7], (DEPTH, B_HEADS, 2 * B_MAX_REL + 1), f32)
    c_norm_w = 1.0 + 0.01 * jax.random.normal(ks[8], (DEPTH, C_WIDTH), f32)
    w_branch = jax.random.normal(ks[9], (DEPTH, N_BRANCH, BRANCH_WIDTH, D_MODEL), f32) * BRANCH_WIDTH ** -0.5
    w_out = jax.random.normal(ks[10], (DEPTH, D_MODEL, D_MODEL), f32) * D_MODEL ** -0.5
    final_g = 1.0 + 0.01 * jax.random.normal(ks[11], (D_MODEL,), f32)
    return {'x': x, 'norm_g': norm_g, 'w_in': w_in, 'b_in': b_in, 'f_bias': f_bias, 'conv_w': conv_w,
            'conv_b': conv_b, 'rel_bias': rel_bias, 'c_norm_w': c_norm_w, 'w_branch': w_branch,
            'w_out': w_out, 'final_g': final_g}

def reference(x, norm_g, w_in, b_in, f_bias, conv_w, conv_b, rel_bias, c_norm_w, w_branch, w_out, final_g):
    cos, sin = rope_tables(x.shape[1])
    for l in range(DEPTH):
        x = hybrid_layer(x, cos, sin, norm_g[l], w_in[l], b_in[l], f_bias[l], conv_w[l], conv_b[l],
                         rel_bias[l], c_norm_w[l], w_branch[l], w_out[l])
    return rms_norm(x, final_g)


_drawn_inputs = setup_inputs


def setup_inputs(seed=0):
    import zlib

    import numpy as np

    out = dict(_drawn_inputs(seed))
    spreads = {}
    factors = {'norm_g': 4.762, 'conv_b': 8.0, 'rel_bias': 8.0, 'c_norm_w': 8.0, 'final_g': 5.656}
    for name, (base, spread) in spreads.items():
        noise = np.random.default_rng([zlib.crc32(name.encode()), seed]).standard_normal(out[name].shape)
        drawn = base * np.exp(spread * noise) if base else spread * noise
        out[name] = __import__('jax').numpy.asarray(drawn.astype(out[name].dtype))
    for name, factor in factors.items():
        out[name] = (out[name] * factor).astype(out[name].dtype)
    return out
```

```python
from contextlib import ExitStack

import concourse.bass as bass
from concourse import mybir

F32 = mybir.dt.float32
F32R = mybir.dt.float32r
BF16 = mybir.dt.bfloat16
ALU = mybir.AluOpType
ACT = mybir.ActivationFunctionType

P = 128
DEPTH, SEQ, D = 2, 512, 1024
NT = SEQ // P
DC = D // P
HEADS, HD = 8, 64
IDX_HEADS = 4
TOPK = 128
CH = 4
BR = 4
EPS = 1e-6
NEG = -1.0e30
INADMISSIBLE = -1.0e38
TAKEN = -3.0e38

U_IQ, U_IK, U_SMALL, U_AK, U_AV, U_AQ = 0, 2, 3, 4, 5, 6
U_BQ, U_BK, U_BV, U_AZ, U_CQ, U_CK, U_CV, U_BZ, U_CO, U_CZ = 10, 14, 18, 22, 26, 30, 34, 38, 42, 46
PROJ = 50
MIX = DC * 6
UNITS = PROJ + MIX + DC
U_OUT = PROJ + MIX
FREE = 1
SLOTS = 2
C_GATE, C_NORM, C_CONVB, C_CONVW, C_CNORM, C_FBIAS, PCOLS = PROJ, 74, 82, 90, 122, 126, 128
K_ID, K_CHUNK, K_CAUSAL, K_COS, K_SIN, K_SEL, KCOLS = 0, 128, 256, 384, 896, 1408, 1920


def schedule():
    seq = []

    def units(a, b):
        for u in range(a, b):
            seq.append(("unit", u))
            if u in range(U_IQ, U_IK + 1):
                seq.append(("rope", u))
            if U_CQ <= u < U_CV:
                seq.append(("conv", u - U_CQ))
            if u == U_AV or U_BV <= u < U_AZ or U_CV <= u < U_BZ:
                seq.append(("turn_v", u))
            for name, first in (("z_a", U_AZ), ("z_b", U_BZ)):
                if first <= u < first + BR:
                    seq.append((name, u - first))

    flying = []

    def push(n):
        if n is not None:
            seq.append(("scores", n))
            flying.append(n)
        if len(flying) > 2 or n is None:
            for back in (3, 4):
                if len(flying) >= back and flying[-back] is not None:
                    seq.append(("turn_p" if back == 3 else "values", flying[-back]))

    def flush():
        for _ in range(3):
            flying.append(None)
            for back in (3, 4):
                if len(flying) >= back and flying[-back] is not None:
                    seq.append(("turn_p" if back == 3 else "values", flying[-back]))
        flying.clear()

    units(0, 4)
    seq.append(("turn_iw", 0))
    units(4, 5)
    seq.append(("rope", U_AK))
    seq.extend(("index", (1, h)) for h in range(IDX_HEADS))
    seq.append(("topk", 1))
    units(5, 8)
    seq.extend(("index", (2, h)) for h in range(IDX_HEADS))
    seq.append(("topk", 2))
    units(8, 11)
    seq.extend(("index", (3, h)) for h in range(IDX_HEADS))
    seq.append(("topk", 3))
    units(11, 14)
    seq.extend(("rope", u) for u in range(U_AQ, U_AQ + BR))
    n = 0
    for u in range(14, 22):
        units(u, u + 1)
        for _ in range(4):
            push(n)
            n += 1
    flush()
    seq.append(("rel_bias", 0))
    seq.append(("rel_bias", 1))
    for u in range(22, 37):
        units(u, u + 1)
        for _ in range(3 if u in (23, 36) else 2):
            if n < 64:
                push(n)
                if (n - 32) % NT == NT - 1 and (n - 32) // NT + 2 < HEADS:
                    seq.append(("rel_bias", (n - 32) // NT + 2))
                n += 1
    flush()
    units(37, 38)
    assert n == 64
    seq.append(("rows", 0))
    for u in range(38, 42):
        units(u, u + 1)
        if u == 38:
            seq.append(("turn_c", 0))
        seq.append(("row_max", u - 38))
        for _ in range(NT):
            push(n)
            n += 1
    flush()
    for u in range(42, 46):
        units(u, u + 1)
        seq.append(("out_gate", u - 42))
        if u > 42:
            seq.append(("variance", u - 43))
    units(46, 47)
    seq.append(("variance", 3))
    seq.append(("deviation", 0))
    seq.append(("z_c", 0))
    for u in range(47, 50):
        units(u, u + 1)
        seq.append(("z_c", u - 46))
    return seq


SEQUENCE = schedule()


def order(*kinds):
    steps = [s for s in SEQUENCE if s[0] in kinds]
    return {s: n for n, s in enumerate(steps)}, len(steps)


SCORE_USE, SCORE_USES = order("index", "scores")
SPARE_USE, SPARE_USES = order("turn_iw", "turn_v", "z_a", "z_b", "turn_c", "row_max", "out_gate", "variance")
SPARE_USES += 1
ITEMS = 80
ROPE, ROPES = order("rope")
DVE_STEPS = 328


def item(n):
    if n < 32:
        return "a", n % HEADS, n // HEADS
    if n < 64:
        return "b", (n - 32) // NT, n % NT
    return "c", (n - 64) // NT, n % NT


def build(nc, x_in, w_full, w_mix, params_in, rel_in, final_in, consts_in, out):
    ctx = ExitStack()
    with ctx:
        cursor = [(nc.sbuf_base + 63) // 64 * 64]

        def at(name, shape, dt, offset):
            return nc.alloc_sbuf_tensor_at(name, shape, dt, offset=offset)

        def region(size):
            a = cursor[0]
            cursor[0] += (size + 31) // 32 * 32
            assert cursor[0] <= nc.sbuf_usable_end, cursor[0]
            return a

        def sb(name, shape, dt=F32):
            size = mybir.dt.size(dt)
            for s in shape[1:]:
                size *= s
            return at(name, shape, dt, region(size))

        ROW = SEQ * 4
        xT = sb("xT", [P, DC, SEQ])
        h_hi = sb("h_hi", [P, DC, SEQ], F32R)
        h_lo = sb("h_lo", [P, DC, SEQ], F32R)
        w_raw = sb("w_raw", [P, SLOTS, DC, P])
        w_hi = sb("w_hi", [P, SLOTS, DC, P], F32R)
        w_lo = sb("w_lo", [P, SLOTS, DC, P], F32R)
        r1 = region(9 * ROW)
        aq = at("aq", [P, BR, SEQ], F32, r1)
        ak = at("ak", [P, SEQ], F32, r1 + 4 * ROW)
        av = at("av", [P, NT, P], F32, r1 + 5 * ROW)
        iq = at("iq", [P, 2, SEQ], F32, r1 + 6 * ROW)
        ik = at("ik", [P, SEQ], F32, r1 + 8 * ROW)
        ya_hi = at("ya_hi", [P, BR, SEQ], F32R, r1)
        ya_lo = at("ya_lo", [P, BR, SEQ], F32R, r1 + 4 * ROW)
        r2 = region(24 * ROW)
        bq = at("bq", [P, BR, SEQ], F32, r2)
        bk = at("bk", [P, BR, SEQ], F32, r2 + 4 * ROW)
        bv = at("bv", [P, NT, BR * P], F32, r2 + 8 * ROW)
        yb_hi = at("yb_hi", [P, BR, SEQ], F32R, r2)
        yb_lo = at("yb_lo", [P, BR, SEQ], F32R, r2 + 4 * ROW)
        rstd_c = at("rstd_c", [P, CH, SEQ], F32, r2 + 8 * ROW)
        r3 = r2 + 12 * ROW
        cv = at("cv", [P, NT, BR * P], F32, r3)
        cq = at("cq", [P, CH, SEQ], F32, r3 + 4 * ROW)
        ck = at("ck", [P, CH, SEQ], F32, r3 + 8 * ROW)
        yc_hi = at("yc_hi", [P, BR, SEQ], F32R, r3 + 4 * ROW)
        yc_lo = at("yc_lo", [P, BR, SEQ], F32R, r3 + 8 * ROW)
        merged_lo = at("merged_lo", [P, DC, SEQ], F32R, r2 + 8 * ROW)
        r4 = region(8 * ROW)
        att = {"a": at("att_a", [P, NT, HEADS * HD], F32, r4), "b": at("att_b", [P, NT, HEADS * HD], F32, r4 + 4 * ROW)}
        hc = at("hc", [P, CH, SEQ], F32, r4)
        merged_hi = at("merged_hi", [P, DC, SEQ], F32R, r4)
        stage = at("stage", [P, NT, D], F32, r4)
        MASK_AT = {1: 0, 2: 256, 3: 640}
        r5 = region(1152 * 4 + 4 * ROW)
        key_mask = at("key_mask", [P, 1152], F32, r5)
        score = at("score", [P, 2, SEQ], F32, r5 + 1152 * 4)
        rel = at("rel", [P, 2, SEQ], F32, r5 + 1152 * 4 + 2 * ROW)
        SUM_AT = [0, 512, 896, 1152]
        decay = at("decay", [CH, 1280], F32, r5)
        run_max = at("run_max", [CH, SEQ], F32, r5 + 1280 * 4)
        source = at("source", [CH, SEQ], F32, r5 + 1280 * 4 + ROW)
        log1p = at("log1p", [CH, SEQ], F32, r5 + 1280 * 4 + 2 * ROW)

        consts = sb("consts", [P, KCOLS])
        ones = sb("ones", [P, SEQ])
        ident_b = sb("ident_b", [P, P], BF16)
        causal_b = sb("causal_b", [P, P], BF16)
        par_next = sb("par_next", [P, PCOLS])
        par = sb("par", [P, PCOLS])
        par_half = sb("par_half", [P, PCOLS])
        par_eighth = sb("par_eighth", [P, PCOLS])
        final_g = sb("final_g", [P, DC])
        prob = sb("prob", [P, 3, SEQ])
        prob_t = sb("prob_t", [P, 2, SEQ])
        turn = sb("turn", [P, SEQ])
        norm = sb("norm", [P, SEQ])
        pad = sb("pad", [P, 2, SEQ + 4])
        z_tanh = sb("z_tanh", [P, SEQ])
        z = sb("z", [P, SEQ])
        iw_row = at("iw_row", [IDX_HEADS, SEQ], F32, cursor[0] - ROW)
        gated = sb("gated", [P, SEQ])
        floor = sb("floor", [P, 2, SEQ])
        i_row = sb("i_row", [CH, SEQ])
        f_row = sb("f_row", [CH, SEQ])
        top8 = sb("top8", [P, 8])
        iw = sb("iw", [P, NT, IDX_HEADS])
        source_t = sb("source_t", [P, NT, CH])
        neg_max = sb("neg_max", [P, 4])
        row_sum = sb("row_sum", [P, 4])
        row_inv = sb("row_inv", [P, 1])
        den = sb("den", [P, P])

        ident = consts[:, K_ID:K_ID + P]
        cos, sin = consts[:, K_COS:K_COS + SEQ], consts[:, K_SIN:K_SIN + SEQ]

        def psum(name):
            return ctx.enter_context(nc.psum_tensor(name, [P, SEQ], F32))

        acc = [psum("acc0"), psum("acc1")]
        ps_s = [psum("ps_s0"), psum("ps_s1")]
        ps_t = [psum("ps_t0"), psum("ps_t1")]
        ps_o = psum("ps_o")
        spare = psum("spare")

        def sem(name):
            return ctx.enter_context(nc.semaphore(name))

        consts_in_s, params_in_s, rel_in_s, x_in_s, out_s = (
            sem("consts_loaded"), sem("params_loaded"), [sem("rel_loaded0"), sem("rel_loaded1")], sem("x_loaded"), sem("out_stored"))
        raw_full = [sem("raw_full0"), sem("raw_full1")]
        w_hi_done, split_full, acc_full = sem("w_hi_done"), sem("split_full"), sem("acc_full")
        acc_free = [sem("acc_free0"), sem("acc_free1")]
        const_ready, ones_ready, par_done = sem("const_ready"), sem("ones_ready"), sem("par_done")
        sq_ready, mean_ready, std_ready = sem("sq_ready"), sem("mean_ready"), sem("std_ready")
        hf_ready, h_hi_ready, h_ready = sem("hf_ready"), sem("h_hi_ready"), sem("h_ready")
        spare_full, spare_free = sem("spare_full"), sem("spare_free")
        evac, roped, conv_sum, conv_tanh, conv_done = (
            sem("evac"), sem("roped"), sem("conv_sum"), sem("conv_tanh"), sem("conv_done"))
        score_full, score_free = sem("score_full"), [sem("score_free0"), sem("score_free1")]
        max_ready, prob_ready = sem("max_ready"), sem("prob_ready")
        turn_full, turn_free = sem("turn_full"), [sem("turn_free0"), sem("turn_free1")]
        out_full, out_free = sem("out_full"), sem("out_free")
        z_ready, gated_ready, y_hi_ready, y_ready = sem("z_ready"), sem("gated_ready"), sem("y_hi_ready"), sem("y_ready")
        neg_abs, log_ready, rows_ready, floor_ready = sem("neg_abs"), sem("log_ready"), sem("rows_ready"), sem("floor_ready")
        og_ready, centred, var_ready, dev_ready = sem("og_ready"), sem("centred"), sem("var_ready"), sem("dev_ready")
        og_used, square_ready = sem("og_used"), sem("square_ready")
        gate_ready, mix_f, mix_hi, mix_ready = sem("gate_ready"), sem("mix_f"), sem("mix_hi"), sem("mix_ready")
        x_step = sem("x_step")
        pre_t, pre_x, pre_zero = sem("pre_t"), sem("pre_x"), sem("pre_zero")
        post_f, post_t, post_x = sem("post_f"), sem("post_t"), sem("post_x")
        chain, chain_mix, chain_out = sem("chain"), sem("chain_mix"), sem("chain_out")
        held = {"pe": sem("pe_held"), "dve": sem("dve_held"), "pool": sem("pool_held")}

        def hold(eng, name):
            eng.sem_inc(held[name], 1)

        block = ctx.enter_context(nc.Block())

        @block.sync
        def _(sp):
            sp.dma_start(stage[:], x_in.rearrange("(t p) d -> p t d", p=P)).then_inc(x_in_s, 16)
            sp.dma_start(consts[:], consts_in).then_inc(consts_in_s, 16)
            sp.dma_start(final_g[:], final_in).then_inc(consts_in_s, 16)

            def load(l, u, slot, source, nk):
                sp.wait_ge(split_full, l * UNITS + u + 1)
                sp.dma_start(w_raw[:, slot, 0:nk, :], source).then_inc(raw_full[slot], 16)

            with sp.Fori(0, DEPTH) as l:
                sp.wait_ge(par_done, l * 3 + FREE)
                sp.dma_start(par_next[:], params_in[bass.ds(l, 1), :, :].rearrange("a p c -> (a p) c")).then_inc(params_in_s, 16)
                with sp.Fori(0, PROJ // 2) as i:
                    for b in range(2):
                        load(l, i * 2 + b, b, w_full[bass.ds(l * 82 + i * 2 + b, 1), :, :].rearrange("a p (k c) -> (a p) k c", c=P), DC)
                with sp.Fori(0, DC) as j:
                    for b in range(6):
                        if b < 3:
                            src = w_full[bass.ds(l * 82 + j * 3 + (PROJ + b), 1), :, :].rearrange("a p (k c) -> (a p) k c", c=P)
                        else:
                            src = w_mix[bass.ds(l * 24 + j * 3 + (b - 3), 1), :, :].rearrange("a p (k c) -> (a p) k c", c=P)
                        load(l, j * 6 + (PROJ + b), b % 2, src, DC if b < 3 else BR)
                with sp.Fori(0, DC // 2) as i:
                    for b in range(2):
                        load(l, i * 2 + (U_OUT + b), b, w_full[bass.ds(l * 82 + i * 2 + (74 + b), 1), :, :].rearrange("a p (k c) -> (a p) k c", c=P), DC)
            for t in range(NT):
                sp.wait_ge(post_x, 2 * t + 2)
                sp.dma_start(out[t * P:(t + 1) * P, :], stage[:, t, :]).then_inc(out_s, 16)
            sp.wait_ge(out_s, 16 * NT)

        @block.gpsimd
        def _(pool):
            pool.memset(ones[:], 1.0).then_inc(ones_ready, 1)
            pool.memset(pad[:], 0.0).then_inc(ones_ready, 1)
            pool.sem_inc(split_full, SLOTS)
            for free in (*acc_free, spare_free, *score_free, *turn_free, out_free, mix_f, mix_ready, par_done):
                pool.sem_inc(free, FREE)

            def split(l, u, slot, nk, uses):
                pool.wait_ge(raw_full[slot], (l * (UNITS // 2) + uses) * 16)
                pool.wait_ge(acc_full, l * UNITS + u + 1)
                hold(pool, "pool")
                pool.tensor_copy(w_hi[:, slot, 0:nk, :], w_raw[:, slot, 0:nk, :]).then_inc(w_hi_done, 1)
                pool.wait_ge(w_hi_done, l * UNITS + u + 1)
                pool.tensor_tensor(w_lo[:, slot, 0:nk, :], w_raw[:, slot, 0:nk, :], w_hi[:, slot, 0:nk, :].bitcast(F32),
                                   ALU.subtract).then_inc(split_full, 1)

            with pool.Fori(0, DEPTH) as l:
                with pool.Fori(0, PROJ // 2) as i:
                    for b in range(2):
                        split(l, i * 2 + b, b, DC, i + 1)
                with pool.Fori(0, DC) as j:
                    for b in range(6):
                        split(l, j * 6 + (PROJ + b), b % 2, DC if b < 3 else BR, j * 3 + (PROJ // 2 + b // 2 + 1))
                with pool.Fori(0, DC // 2) as i:
                    for b in range(2):
                        split(l, i * 2 + (U_OUT + b), b, DC, i + (U_OUT // 2 + 1))

        @block.tensor
        def _(pe):
            pe.wait_ge(consts_in_s, 32)
            pe.wait_ge(x_in_s, 16)
            for c in range(DC):
                if c >= 2:
                    pe.wait_ge(pre_x, c - 1)
                for t in range(NT):
                    last = pe.transpose(ps_s[c % 2][:, t * P:(t + 1) * P], stage[:, t, c * P:(c + 1) * P], ident)
                last.then_inc(pre_t, 1)
            pe.wait_ge(pre_x, DC)
            pe.wait_ge(ones_ready, 2)
            pe.wait_ge(const_ready, 2)
            pe.transpose(spare[:, 0:P], ident, ident).then_inc(acc_full, SLOTS)

            def product(l, u, slot, uses, hi, lo, nk, per_chunk=None):
                pe.wait_ge(split_full, l * UNITS + u + (SLOTS + 1))
                pe.wait_ge(acc_free[slot], l * (UNITS // 2) + uses + FREE)
                for k in range(nk):
                    if per_chunk:
                        per_chunk(k)
                    pe.matmul(acc[slot][:, :], w_hi[:, slot, k, :], hi[:, k, :], start=(k == 0), stop=False)
                    pe.matmul(acc[slot][:, :], w_hi[:, slot, k, :], lo[:, k, :], start=False, stop=False)
                    last = pe.matmul(acc[slot][:, :], w_lo[:, slot, k, :], hi[:, k, :], start=False, stop=(k == nk - 1))
                last.then_inc(acc_full, 1)

            def use_spare(l, step):
                pe.wait_ge(spare_free, l * SPARE_USES + SPARE_USE[step] + 1 + FREE)

            def norm_sum(n):
                pe.wait_ge(sq_ready, n + 1)
                pe.matmul(spare[:, :], ones[:, 0:P], norm[:, :], start=True, stop=True).then_inc(spare_full, 1)

            def scores_bank(l, step):
                use = SCORE_USE[step]
                pe.wait_ge(score_free[use % 2], l * (SCORE_USES // 2) + use // 2 + FREE)
                return ps_s[use % 2]

            with pe.Fori(0, DEPTH) as l:
                pe.wait_ge(spare_free, l * SPARE_USES + FREE)
                norm_sum(l)
                for kind, n in SEQUENCE:
                    step = (kind, n)
                    if kind == "unit":
                        product(l, n, n % 2, n // 2, h_hi, h_lo, DC,
                                (lambda k: pe.wait_ge(h_ready, l * DC + k + 1)) if n == 0 else None)
                    elif kind == "turn_iw":
                        use_spare(l, step)
                        pe.wait_ge(evac, l * PROJ + U_SMALL + 1)
                        hold(pe, "pe")
                        for t in range(NT):
                            last = pe.transpose(spare[:, t * IDX_HEADS:(t + 1) * IDX_HEADS],
                                                iw_row[:, t * P:(t + 1) * P], ident[0:IDX_HEADS, 0:IDX_HEADS])
                        last.then_inc(spare_full, 1)
                    elif kind == "turn_v":
                        use_spare(l, step)
                        pe.wait_ge(evac, l * PROJ + n + 1)
                        for t in range(NT):
                            last = pe.transpose(spare[:, t * P:(t + 1) * P], pad[:, n % 2, 3 + t * P:3 + (t + 1) * P], ident)
                        last.then_inc(spare_full, 1)
                    elif kind == "index":
                        t, h = n
                        bank = scores_bank(l, step)
                        pe.wait_ge(roped, l * ROPES + ROPE[("rope", U_IK)] + 1)
                        b = h % 2 * HD
                        pe.matmul(bank[:, 0:(t + 1) * P], iq[b:b + HD, h // 2, t * P:(t + 1) * P],
                                  ik[b:b + HD, 0:(t + 1) * P], start=True, stop=True).then_inc(score_full, 1)
                    elif kind == "scores":
                        branch, h, t = item(n)
                        bank = scores_bank(l, step)
                        w = (t + 1) * P
                        if branch == "a":
                            pe.wait_ge(roped, l * ROPES + ROPES)
                            b = h // BR * HD
                            pe.matmul(bank[:, 0:w], aq[b:b + HD, h % BR, t * P:w], ak[b:b + HD, 0:w],
                                      start=True, stop=True).then_inc(score_full, 1)
                        elif branch == "b":
                            pe.wait_ge(evac, l * PROJ + U_BV)
                            b = h % 2 * HD
                            pe.matmul(bank[:, 0:w], bq[b:b + HD, h // 2, t * P:w], bk[b:b + HD, h // 2, 0:w],
                                      start=True, stop=True).then_inc(score_full, 1)
                        else:
                            pe.wait_ge(rows_ready, l + 1)
                            for s in range(t + 1):
                                o = SUM_AT[s] + (t - s) * P
                                last = pe.matmul(bank[:, s * P:(s + 1) * P], consts[0:CH, K_SEL + h * P:K_SEL + (h + 1) * P],
                                                 decay[:, o:o + P], start=True, stop=(s < t))
                            pe.matmul(bank[:, t * P:w], ident_b[:, :], causal_b[:, :], start=False, stop=True).then_inc(score_full, 1)
                            pe.wait_ge(turn_free[n % 2], l * (ITEMS // 2) + n // 2 + FREE)
                            pe.wait_ge(conv_done, l * 2 * CH + 2 * CH)
                            for s in range(t + 1):
                                last = pe.matmul(ps_t[n % 2][:, s * P:(s + 1) * P], ck[:, h, s * P:(s + 1) * P],
                                                 cq[:, h, t * P:w], start=True, stop=True)
                            last.then_inc(turn_full, 1)
                    elif kind == "turn_p":
                        branch, h, t = item(n)
                        if branch != "c":
                            pe.wait_ge(turn_free[n % 2], l * (ITEMS // 2) + n // 2 + FREE)
                            pe.wait_ge(prob_ready, l * ITEMS + n + 1)
                            for s in range(t + 1):
                                last = pe.transpose(ps_t[n % 2][:, s * P:(s + 1) * P], prob[:, n % 3, s * P:(s + 1) * P], ident)
                            last.then_inc(turn_full, 1)
                    elif kind == "values":
                        branch, h, t = item(n)
                        pe.wait_ge(turn_free[n % 2], l * (ITEMS // 2) + n // 2 + 1 + FREE)
                        pe.wait_ge(out_free, l * ITEMS + n + FREE)
                        if branch != "c":
                            pe.wait_ge(spare_free, l * SPARE_USES + SPARE_USE[("turn_v", U_AV if branch == "a" else U_AZ - 1)] + 2 + FREE)
                            v, f = (av, h // BR * HD) if branch == "a" else (bv, h * HD)
                            o = 0
                            for s in range(t + 1):
                                last = pe.matmul(ps_o[:, o:o + HD], prob_t[:, n % 2, s * P:(s + 1) * P], v[:, s, f:f + HD],
                                                 start=(s == 0), stop=(s == t))
                        else:
                            pe.wait_ge(spare_free, l * SPARE_USES + SPARE_USE[("turn_v", U_BZ - 1)] + 2 + FREE)
                            o = 0
                            for s in range(t + 1):
                                pe.matmul(ps_o[:, o:o + P], cv[:, s, h * P:(h + 1) * P], prob_t[:, n % 2, s * P:(s + 1) * P],
                                          start=(s == 0), stop=(s == t))
                            for s in range(t + 1):
                                last = pe.matmul(ps_o[:, o + P:o + 2 * P], ones[:, 0:P], prob_t[:, n % 2, s * P:(s + 1) * P],
                                                 start=(s == 0), stop=(s == t))
                        last.then_inc(out_full, 1)
                    elif kind in ("z_a", "z_b"):
                        use_spare(l, step)
                        pe.wait_ge(out_free, l * ITEMS + (32 if kind == "z_a" else 64) + FREE)
                        for t in range(NT):
                            last = pe.transpose(spare[:, t * P:(t + 1) * P], att[kind[2]][:, t, n * P:(n + 1) * P], ident)
                        last.then_inc(spare_full, 1)
                    elif kind == "turn_c":
                        use_spare(l, step)
                        pe.wait_ge(rows_ready, l + 1)
                        hold(pe, "pe")
                        for t in range(NT):
                            last = pe.transpose(spare[:, t * CH:(t + 1) * CH], source[:, t * P:(t + 1) * P], ident[0:CH, 0:CH])
                        last.then_inc(spare_full, 1)
                    elif kind == "row_max":
                        use_spare(l, step)
                        pe.matmul(spare[:, :], consts[0:CH, K_SEL + n * P:K_SEL + (n + 1) * P], run_max[:, :],
                                  start=True, stop=True).then_inc(spare_full, 1)
                    elif kind == "out_gate":
                        use_spare(l, step)
                        pe.wait_ge(og_used, l * CH + n + 1)
                        pe.matmul(spare[:, :], ones[:, 0:P], hc[:, n, :], start=True, stop=True).then_inc(spare_full, 1)
                    elif kind == "variance":
                        use_spare(l, step)
                        pe.wait_ge(square_ready, l * CH + n + 1)
                        pe.matmul(spare[:, :], ones[:, 0:P], gated[:, :], start=True, stop=True).then_inc(spare_full, 1)
                with pe.Fori(0, DC) as j:
                    for b in range(3):
                        product(l, j * 6 + (PROJ + b), b % 2, j * 3 + (PROJ // 2 + b // 2), h_hi, h_lo, DC)
                    for b, (hi, lo) in enumerate(((ya_hi, ya_lo), (yb_hi, yb_lo), (yc_hi, yc_lo))):
                        pe.wait_ge(y_ready, l * 12 + 4 * b + 4)
                        product(l, j * 6 + (PROJ + 3 + b), (3 + b) % 2, j * 3 + (PROJ // 2 + (3 + b) // 2), hi, lo, BR)
                pe.wait_ge(mix_ready, l * DC + DC + FREE)
                hold(pe, "pe")
                with pe.Fori(0, DC // 2) as i:
                    for b in range(2):
                        product(l, i * 2 + (U_OUT + b), b, i + U_OUT // 2, merged_hi, merged_lo, DC)
            pe.wait_ge(spare_free, DEPTH * SPARE_USES + FREE)
            norm_sum(DEPTH)
            pe.wait_ge(post_f, DC)
            for n in range(2 * NT):
                if n >= 2:
                    pe.wait_ge(post_x, n - 1)
                t, half = n // 2, n % 2
                for c in range(4):
                    last = pe.transpose(ps_s[n % 2][:, c * P:(c + 1) * P], xT[:, half * 4 + c, t * P:(t + 1) * P], ident)
                last.then_inc(post_t, 1)

        @block.scalar
        def _(act):
            for c in range(DC):
                act.wait_ge(pre_t, c + 1)
                act.activation(xT[:, c, :], ps_s[c % 2][:, :], ACT.Copy).then_inc(pre_x, 1)
            act.wait_ge(consts_in_s, 32)
            act.activation(ident_b[:, :], ident, ACT.Copy).then_inc(const_ready, 1)
            act.activation(causal_b[:, :], consts[:, K_CAUSAL:K_CAUSAL + P], ACT.Copy).then_inc(const_ready, 1)

            def std():
                act.activation(norm[:, :], norm[:, :], ACT.Sqrt).then_inc(std_ready, 1)

            with act.Fori(0, DEPTH) as l:
                act.wait_ge(params_in_s, l * 16 + 16)
                act.wait_ge(mean_ready, l + 1)
                act.activation(norm[:, :], norm[:, :], ACT.Sqrt).then_inc(std_ready, 1)
                act.activation(par[:, :], par_next[:, :], ACT.Copy).then_inc(par_done, 1)
                act.activation(par_half[:, :], par_next[:, :], ACT.Copy, scale=0.5).then_inc(par_done, 1)
                act.activation(par_eighth[:, :], par_next[:, :], ACT.Copy, scale=HD ** -0.5).then_inc(par_done, 1)
                for c in range(DC):
                    act.wait_ge(hf_ready, l * DC + c + 1)
                    act.activation(h_hi[:, c, :], pad[:, c % 2, 3:3 + SEQ], ACT.Copy).then_inc(h_hi_ready, 1)
                act.wait_ge(par_done, l * 3 + 3 + FREE)

                for kind, n in SEQUENCE:
                    step = (kind, n)
                    if kind == "unit" and n != U_SMALL:
                        act.wait_ge(acc_full, l * UNITS + n + (SLOTS + 1))
                        src, free = acc[n % 2][:, :], acc_free[n % 2]
                        bias, half = par[:, n:n + 1], par_half[:, n:n + 1]
                        if U_AZ <= n < U_AZ + BR or U_BZ <= n < U_BZ + BR or n >= U_CZ:
                            zn = (n - U_AZ) if n < U_CQ else (n - U_BZ + BR) if n < U_CO else (n - U_CZ + 2 * BR)
                            if zn:
                                act.wait_ge(gated_ready, l * 12 + zn)
                            act.activation(z_tanh[:, :], src, ACT.Tanh, bias=half, scale=0.5)
                            act.activation(z[:, :], src, ACT.Identity, bias=bias).then_inc(z_ready, 1)
                            act.wait_ge(z_ready, l * 12 + zn + 1)
                            act.sem_inc(free, 1)
                            act.sem_inc(evac, 1)
                            continue
                        if U_CO <= n < U_CZ:
                            act.wait_ge(gated_ready, l * 12 + 8)
                            if n > U_CO:
                                act.wait_ge(og_used, l * CH + n - U_CO)
                            act.activation(z_tanh[:, :], src, ACT.Tanh, bias=half, scale=0.5).then_inc(og_ready, 1)
                            act.wait_ge(og_ready, l * CH + n - U_CO + 1)
                            act.sem_inc(free, 1)
                            act.sem_inc(evac, 1)
                            continue
                        scale = 1.0
                        if n < U_IK:
                            dst = iq[:, n, :]
                        elif n == U_IK:
                            dst = ik[:, :]
                        elif n == U_AK:
                            dst = ak[:, :]
                        elif U_AQ <= n < U_BQ:
                            dst, scale, bias = aq[:, n - U_AQ, :], HD ** -0.5, par_eighth[:, n:n + 1]
                        elif U_BQ <= n < U_BK:
                            dst, scale, bias = bq[:, n - U_BQ, :], HD ** -0.5, par_eighth[:, n:n + 1]
                        elif U_BK <= n < U_BV:
                            dst = bk[:, n - U_BK, :]
                        else:
                            dst = pad[:, n % 2, 3:3 + SEQ]
                            if n == U_AV:
                                act.wait_ge(h_ready, l * DC + DC)
                            elif U_BV <= n < U_AZ or n >= U_CV:
                                if n not in (U_BV, U_CV):
                                    act.wait_ge(spare_full, l * SPARE_USES + SPARE_USE[("turn_v", n - 1)] + 1)
                                else:
                                    if n == U_CV:
                                        act.wait_ge(conv_sum, l * 8 + 8)
                            else:
                                if n > U_CQ + 1:
                                    act.wait_ge(conv_sum, l * 8 + n - U_CQ - 1)
                                act.wait_ge(spare_full, l * SPARE_USES + SPARE_USE[("turn_v", U_AZ - 1)] + 2)
                        act.activation(dst, src, ACT.Identity, bias=bias, scale=scale).then_inc(evac, 1)
                        act.wait_ge(evac, l * PROJ + n + 1)
                        act.sem_inc(free, 1)
                    elif kind == "turn_v":
                        act.wait_ge(spare_full, l * SPARE_USES + SPARE_USE[step] + 2)
                        if n == U_AV:
                            dst = av[:, :, :]
                        else:
                            c = (n - U_BV) if n < U_AZ else (n - U_CV)
                            dst = (bv if n < U_AZ else cv)[:, :, c * P:(c + 1) * P]
                        act.activation(dst, spare[:, :].rearrange("p (t c) -> p t c", t=NT), ACT.Copy).then_inc(spare_free, 1)
                    elif kind == "conv":
                        act.wait_ge(conv_sum, l * 8 + n + 1)
                        act.activation(z_tanh[:, :], turn[:, :], ACT.Tanh, scale=0.5).then_inc(conv_tanh, 1)
                    elif kind == "rel_bias":
                        act.wait_ge(max_ready, l * 64 + (32 + 4 * (n - 1) if n >= 2 else 32))
                        act.dma_start(rel[:, n % 2, :], rel_in[bass.ds(l * HEADS + n, 1), :, :].rearrange("a p k -> (a p) k"))\
                           .then_inc(rel_in_s[n % 2], 16)
                    elif kind == "scores":
                        branch, h, t = item(n)
                        if branch != "c":
                            act.wait_ge(max_ready, l * 64 + n + 1)
                            act.activation(prob[:, n % 3, 0:(t + 1) * P], prob[:, n % 3, 0:(t + 1) * P], ACT.Exp,
                                           bias=neg_max[:, n % 4:n % 4 + 1], scale=-1.0,
                                           accum_out=row_sum[:, n % 4:n % 4 + 1]).then_inc(prob_ready, 1)
                        else:
                            use = SCORE_USE[step]
                            act.wait_ge(score_full, l * SCORE_USES + use + 1)
                            if n < 67:
                                act.wait_ge(turn_full, l * ITEMS + n - 2)
                            else:
                                act.wait_ge(turn_free[(n - 3) % 2], l * (ITEMS // 2) + (n - 3) // 2 + 1 + FREE)
                            if n == 64:
                                act.wait_ge(spare_free, l * SPARE_USES + SPARE_USE[("turn_c", 0)] + 2 + FREE)
                            for s in range(t + 1):
                                last = act.activation(prob[:, n % 3, s * P:(s + 1) * P], ps_s[use % 2][:, s * P:(s + 1) * P],
                                                      ACT.Exp, bias=source_t[:, s, h:h + 1])
                            last.then_inc(prob_ready, 1)
                            act.wait_ge(prob_ready, l * ITEMS + n + 1)
                            act.sem_inc(score_free[use % 2], 1)
                    elif kind == "turn_p":
                        branch, h, t = item(n)
                        if branch != "c":
                            act.wait_ge(turn_full, l * ITEMS + n + 1)
                            if n >= 2:
                                act.wait_ge(out_full, l * ITEMS + n - 1)
                            act.activation(prob_t[:, n % 2, 0:(t + 1) * P], ps_t[n % 2][:, 0:(t + 1) * P], ACT.Copy)\
                               .then_inc(turn_free[n % 2], 1)
                    elif kind in ("z_a", "z_b", "z_c"):
                        zn = "abc".index(kind[2]) * BR + n
                        act.wait_ge(gated_ready, l * 12 + zn + 1)
                        act.activation((ya_hi, yb_hi, yc_hi)[zn // BR][:, n, :], gated[:, :], ACT.Copy).then_inc(y_hi_ready, 1)
                    elif kind == "rows":
                        act.wait_ge(neg_abs, l + 1)
                        act.activation(log1p[:, :], log1p[:, :], ACT.Exp).then_inc(log_ready, 1)
                        act.wait_ge(log_ready, l * 2 + 1)
                        act.activation(log1p[:, :], log1p[:, :], ACT.Ln, bias=ones[0:CH, 0:1]).then_inc(log_ready, 1)
                    elif kind == "row_max":
                        act.wait_ge(spare_full, l * SPARE_USES + SPARE_USE[step] + 2)
                        act.wait_ge(out_free, l * ITEMS + (64 + NT * (n - 1) if n >= 2 else 64) + FREE)
                        act.activation(floor[:, n % 2, :], spare[:, :], ACT.Exp).then_inc(floor_ready, 1)
                        act.wait_ge(floor_ready, l * CH + n + 1)
                        act.sem_inc(spare_free, 1)
                    elif kind == "out_gate":
                        act.wait_ge(centred, l * CH + n + 1)
                        if n:
                            act.wait_ge(spare_full, l * SPARE_USES + SPARE_USE[("variance", n - 1)] + 2)
                        act.activation(gated[:, :], hc[:, n, :], ACT.Square).then_inc(square_ready, 1)
                    elif kind == "deviation":
                        act.wait_ge(var_ready, l * CH + CH)
                        act.activation(rstd_c[:, :, :], rstd_c[:, :, :], ACT.Sqrt).then_inc(dev_ready, 1)

                with act.Fori(0, DC) as j:
                    for b in range(3):
                        act.wait_ge(acc_full, l * UNITS + j * 6 + (PROJ + b + SLOTS + 1))
                        act.wait_ge(mix_f, l * DC + j + FREE)
                        act.wait_ge(y_ready, l * 12 + 12)
                        act.activation((floor[:, 0, :], floor[:, 1, :], z_tanh[:, :])[b], acc[b % 2][:, :], ACT.Tanh,
                                       bias=par_half[:, bass.ds(j + (C_GATE + DC * b), 1)], scale=0.5).then_inc(gate_ready, 1)
                        act.wait_ge(gate_ready, l * 24 + j * 3 + (b + 1))
                        act.sem_inc(acc_free[b % 2], 1)
                    act.wait_ge(mix_f, l * DC + j + 1 + FREE)
                    act.activation(merged_hi[:, bass.ds(j, 1), :], gated[:, :].rearrange("p (a n) -> p a n", a=1), ACT.Copy,
                                   scale=0.5).then_inc(mix_hi, 1)
            act.wait_ge(mean_ready, DEPTH + 1)
            std()
            for n in range(2 * NT):
                act.wait_ge(post_t, n + 1)
                act.activation(stage[:, n // 2, n % 2 * SEQ:(n % 2 + 1) * SEQ], ps_s[n % 2][:, :], ACT.Copy).then_inc(post_x, 1)

        @block.vector
        def _(dve):
            count = [0]

            def link(ins):
                count[0] += 1
                ins.then_inc(chain, 1)
                dve.wait_ge(chain, base[0] + count[0])

            base = [0]
            dve.wait_ge(ones_ready, 2)
            for c in range(DC):
                dve.wait_ge(pre_x, c + 1)
                if c == 0:
                    link(dve.tensor_tensor(norm[:, :], xT[:, c, :], xT[:, c, :], ALU.mult))
                else:
                    link(dve.tensor_tensor(turn[:, :], xT[:, c, :], xT[:, c, :], ALU.mult))
                    ins = dve.tensor_tensor(norm[:, :], norm[:, :], turn[:, :], ALU.add)
                    link(ins) if c < DC - 1 else ins.then_inc(sq_ready, 1)
            PRE = count[0]
            count[0] = 0

            def mean_square(n):
                dve.wait_ge(spare_full, n * SPARE_USES + 1)
                dve.tensor_scalar(norm[:, :], spare[:, :], 1.0 / D, EPS, ALU.mult, ALU.add).then_inc(mean_ready, 1)
                dve.wait_ge(mean_ready, n + 1)
                dve.sem_inc(spare_free, 1)

            with dve.Fori(0, DEPTH) as l:
                base[0] = l * DVE_STEPS + PRE
                mean_square(l)
                dve.wait_ge(std_ready, l + 1)
                link(dve.reciprocal(norm[:, :], norm[:, :]))
                dve.wait_ge(par_done, l * 3 + 1 + FREE)

                def h_lo_part(c):
                    dve.wait_ge(h_hi_ready, l * DC + c + 1)
                    dve.tensor_tensor(h_lo[:, c, :], pad[:, c % 2, 3:3 + SEQ], h_hi[:, c, :].bitcast(F32),
                                      ALU.subtract).then_inc(h_ready, 1)

                for c in range(DC):
                    if c >= 2:
                        dve.wait_ge(h_ready, l * DC + c - 1)
                    dve.scalar_tensor_tensor(pad[:, c % 2, 3:3 + SEQ], xT[:, c, :], par[:, C_NORM + c:C_NORM + c + 1], norm[:, :],
                                             ALU.mult, ALU.mult).then_inc(hf_ready, 1)
                    if c:
                        h_lo_part(c - 1)
                h_lo_part(DC - 1)

                for kind, n in SEQUENCE:
                    step = (kind, n)
                    if kind == "unit" and n == U_SMALL:
                        dve.wait_ge(acc_full, l * UNITS + n + (SLOTS + 1))
                        src = acc[n % 2]
                        dve.wait_ge(par_done, l * 3 + 3 + FREE)
                        dve.tensor_scalar(i_row[:, :], src[32:32 + CH, :], par[32:32 + CH, n:n + 1], None, ALU.add)
                        dve.tensor_scalar(f_row[:, :], src[64:64 + CH, :], par[64:64 + CH, n:n + 1],
                                          par[64:64 + CH, C_FBIAS:C_FBIAS + 1], ALU.add, ALU.add)
                        link(dve.tensor_scalar(iw_row[:, :], src[0:IDX_HEADS, :], par[0:IDX_HEADS, n:n + 1],
                                               HD ** -0.5 * IDX_HEADS ** -0.5, ALU.add, ALU.mult))
                        dve.sem_inc(acc_free[n % 2], 1)
                        dve.wait_ge(evac, l * PROJ + n)
                        dve.sem_inc(evac, 1)
                    elif kind == "turn_iw":
                        dve.wait_ge(spare_full, l * SPARE_USES + SPARE_USE[step] + 2)
                        link(dve.tensor_copy(iw[:, :, :], spare[:, 0:NT * IDX_HEADS].rearrange("p (t h) -> p t h", t=NT)))
                        dve.sem_inc(spare_free, 1)
                    elif kind == "rope":
                        dve.wait_ge(evac, l * PROJ + n + 1)
                        t = (iq[:, n, :] if n < U_IK else ik[:, :] if n == U_IK else ak[:, :] if n == U_AK else aq[:, n - U_AQ, :])
                        swap = [i + 8 if i < 8 else i - 8 if i < 16 else i for i in range(32)]
                        hold(dve, "dve")
                        link(dve.stream_shuffle(turn[:, :], t, swap))
                        link(dve.tensor_tensor(turn[:, :], turn[:, :], sin, ALU.mult))
                        link(dve.tensor_tensor(t, t, cos, ALU.mult))
                        dve.tensor_tensor(t, t, turn[:, :], ALU.add).then_inc(roped, 1)
                        dve.wait_ge(roped, l * ROPES + ROPE[step] + 1)
                    elif kind == "index":
                        t, h = n
                        use = SCORE_USE[step]
                        w = (t + 1) * P
                        dve.wait_ge(score_full, l * SCORE_USES + use + 1)
                        dst = score[:, t % 2, 0:w] if h == 0 else turn[:, 0:w]
                        link(dve.tensor_scalar(dst, ps_s[use % 2][:, 0:w], 0.0, iw[:, t, h:h + 1], ALU.max, ALU.mult))
                        dve.sem_inc(score_free[use % 2], 1)
                        if h:
                            link(dve.tensor_tensor(score[:, t % 2, 0:w], score[:, t % 2, 0:w], turn[:, 0:w], ALU.add))
                        if h == IDX_HEADS - 1:
                            link(dve.memset(score[0:P // 2, t % 2, w - P // 2:w], INADMISSIBLE))
                    elif kind == "topk":
                        s = score[:, n % 2, 0:(n + 1) * P]
                        for _ in range(TOPK // 8):
                            hold(dve, "dve")
                            link(dve.max(top8[:, :], s))
                            hold(dve, "dve")
                            link(dve.match_replace(s, top8[:, :], s, TAKEN))
                        link(dve.tensor_scalar(key_mask[:, MASK_AT[n]:MASK_AT[n] + (n + 1) * P], s, 0.5 * (TAKEN + INADMISSIBLE), NEG,
                                               ALU.is_gt, ALU.mult))
                    elif kind == "conv":
                        dve.wait_ge(evac, l * PROJ + U_CQ + n + 1)
                        x = pad[:, n % 2, :]
                        for tap in (3, 2, 1, 0):
                            w = par[:, C_CONVW + tap * 8 + n:C_CONVW + tap * 8 + n + 1]
                            if tap == 3:
                                link(dve.tensor_scalar(turn[:, :], x[:, tap:tap + SEQ], w, par[:, C_CONVB + n:C_CONVB + n + 1],
                                                       ALU.mult, ALU.add))
                            else:
                                ins = dve.scalar_tensor_tensor(turn[:, :], x[:, tap:tap + SEQ], w, turn[:, :], ALU.mult, ALU.add)
                                link(ins) if tap else ins.then_inc(conv_sum, 1)
                        dve.wait_ge(conv_tanh, l * 8 + n + 1)
                        dst = cq[:, n, :] if n < CH else ck[:, n - CH, :]
                        dve.scalar_tensor_tensor(dst, z_tanh[:, :], 1.0, turn[:, :], ALU.add, ALU.mult).then_inc(conv_done, 1)
                        dve.wait_ge(conv_done, l * 8 + n + 1)
                    elif kind == "rel_bias":
                        dve.wait_ge(rel_in_s[n % 2], l * 64 + 16 * (n // 2 + 1))
                        link(dve.memset(rel[0:P // 2, n % 2, SEQ - P // 2:SEQ], NEG))
                    elif kind == "scores":
                        branch, h, t = item(n)
                        use = SCORE_USE[step]
                        w = (t + 1) * P
                        if branch != "c":
                            dve.wait_ge(score_full, l * SCORE_USES + use + 1)
                            if n >= 3:
                                dve.wait_ge(turn_full, l * ITEMS + n - 2)
                            if branch == "b":
                                mask = rel[:, h % 2, SEQ - w:SEQ]
                            else:
                                mask = key_mask[:, MASK_AT[t]:MASK_AT[t] + w] if t else consts[:, K_CHUNK:K_CHUNK + P]
                            hold(dve, "dve")
                            dve.tensor_tensor_reduce(out=prob[:, n % 3, 0:w], in0=ps_s[use % 2][:, 0:w], in1=mask, scale=-1.0,
                                                     scalar=3.0e38, op0=ALU.add, op1=ALU.min,
                                                     accum_out=neg_max[:, n % 4:n % 4 + 1]).then_inc(max_ready, 1)
                            dve.wait_ge(max_ready, l * 64 + n + 1)
                            dve.sem_inc(score_free[use % 2], 1)
                    elif kind == "turn_p":
                        branch, h, t = item(n)
                        if branch == "c":
                            dve.wait_ge(turn_full, l * ITEMS + n + 1)
                            dve.wait_ge(prob_ready, l * ITEMS + n + 1)
                            dve.wait_ge(out_full, l * ITEMS + n - 1)
                            w = (t + 1) * P
                            dve.scalar_tensor_tensor(prob_t[:, n % 2, 0:w], ps_t[n % 2][:, 0:w], 0.25 * P ** -0.5, prob[:, n % 3, 0:w],
                                                     ALU.mult, ALU.mult).then_inc(turn_free[n % 2], 1)
                    elif kind == "values":
                        branch, h, t = item(n)
                        dve.wait_ge(out_full, l * ITEMS + n + 1)
                        dve.wait_ge(out_free, l * ITEMS + n + FREE)
                        if branch != "c":
                            o = 0
                            link(dve.reciprocal(row_inv[:, :], row_sum[:, n % 4:n % 4 + 1]))
                            dve.tensor_scalar(att[branch][:, t, h * HD:(h + 1) * HD], ps_o[:, o:o + HD], row_inv[:, 0:1], None,
                                              ALU.mult).then_inc(out_free, 1)
                        else:
                            o = 0
                            dve.wait_ge(floor_ready, l * CH + h + 1)
                            link(dve.scalar_tensor_tensor(den[:, :], ps_o[:, o + P:o + 2 * P], -1.0, floor[:, h % 2, t * P:(t + 1) * P],
                                                          ALU.mult, ALU.max))
                            link(dve.tensor_tensor(den[:, :], den[:, :], ps_o[:, o + P:o + 2 * P], ALU.max))
                            link(dve.reciprocal(den[:, :], den[:, :]))
                            dve.tensor_tensor(hc[:, h, t * P:(t + 1) * P], ps_o[:, o:o + P], den[:, :], ALU.mult).then_inc(out_free, 1)
                    elif kind in ("z_a", "z_b", "z_c"):
                        zn = "abc".index(kind[2]) * BR + n
                        dve.wait_ge(z_ready, l * 12 + zn + 1)
                        link(dve.scalar_tensor_tensor(z[:, :], z_tanh[:, :], 1.0, z[:, :], ALU.add, ALU.mult))
                        if kind != "z_c":
                            dve.wait_ge(spare_full, l * SPARE_USES + SPARE_USE[step] + 2)
                            dve.scalar_tensor_tensor(gated[:, :], z[:, :], 0.5, spare[:, :], ALU.mult, ALU.mult).then_inc(gated_ready, 1)
                            dve.wait_ge(gated_ready, l * 12 + zn + 1)
                            dve.sem_inc(spare_free, 1)
                        else:
                            link(dve.reciprocal(rstd_c[:, n, :], rstd_c[:, n, :]))
                            link(dve.scalar_tensor_tensor(turn[:, :], hc[:, n, :], par[:, C_CNORM + n:C_CNORM + n + 1], rstd_c[:, n, :],
                                                          ALU.mult, ALU.mult))
                            dve.scalar_tensor_tensor(gated[:, :], z[:, :], 0.5, turn[:, :], ALU.mult, ALU.mult).then_inc(gated_ready, 1)
                        dve.wait_ge(y_hi_ready, l * 12 + zn + 1)
                        dve.tensor_tensor((ya_lo, yb_lo, yc_lo)[zn // BR][:, n, :], gated[:, :],
                                          (ya_hi, yb_hi, yc_hi)[zn // BR][:, n, :].bitcast(F32), ALU.subtract).then_inc(y_ready, 1)
                        dve.wait_ge(y_ready, l * 12 + zn + 1)
                    elif kind == "rows":
                        dve.scalar_tensor_tensor(log1p[:, :], f_row[:, :], -1.0, f_row[:, :], ALU.mult, ALU.min).then_inc(neg_abs, 1)
                        dve.wait_ge(log_ready, l * 2 + 2)
                        link(dve.scalar_tensor_tensor(f_row[:, :], f_row[:, :], 0.0, log1p[:, :], ALU.min, ALU.subtract))
                        link(dve.tensor_tensor_scan(run_max[:, :], f_row[:, :], i_row[:, :], 0.0, ALU.add, ALU.max))
                        for s in range(NT):
                            w = SEQ - s * P
                            link(dve.tensor_tensor_scan(decay[:, SUM_AT[s]:SUM_AT[s] + w], ones[0:CH, 0:w], f_row[:, s * P:SEQ], 0.0,
                                                        ALU.mult, ALU.add))
                            link(dve.tensor_tensor(source[:, s * P:(s + 1) * P], i_row[:, s * P:(s + 1) * P],
                                                   decay[:, SUM_AT[s]:SUM_AT[s] + P], ALU.subtract))
                            link(dve.tensor_tensor(decay[:, SUM_AT[s]:SUM_AT[s] + w], decay[:, SUM_AT[s]:SUM_AT[s] + w],
                                                   run_max[:, s * P:SEQ], ALU.subtract))
                        dve.tensor_scalar(run_max[:, :], run_max[:, :], -1.0, None, ALU.mult).then_inc(rows_ready, 1)
                    elif kind == "turn_c":
                        dve.wait_ge(spare_full, l * SPARE_USES + SPARE_USE[step] + 2)
                        dve.tensor_copy(source_t[:, :, :], spare[:, 0:NT * CH].rearrange("p (t h) -> p t h", t=NT)).then_inc(spare_free, 1)
                    elif kind == "out_gate":
                        dve.wait_ge(og_ready, l * CH + n + 1)
                        dve.scalar_tensor_tensor(hc[:, n, :], z_tanh[:, :], 1.0, hc[:, n, :], ALU.add, ALU.mult).then_inc(og_used, 1)
                        dve.wait_ge(spare_full, l * SPARE_USES + SPARE_USE[step] + 2)
                        dve.scalar_tensor_tensor(hc[:, n, :], spare[:, :], -1.0 / P, hc[:, n, :], ALU.mult, ALU.add).then_inc(centred, 1)
                        dve.wait_ge(centred, l * CH + n + 1)
                        dve.sem_inc(spare_free, 1)
                    elif kind == "variance":
                        dve.wait_ge(spare_full, l * SPARE_USES + SPARE_USE[step] + 2)
                        dve.tensor_scalar(rstd_c[:, n, :], spare[:, :], 1.0 / P, 4.0 * EPS, ALU.mult, ALU.add).then_inc(var_ready, 1)
                        dve.wait_ge(var_ready, l * CH + n + 1)
                        dve.sem_inc(spare_free, 1)
                    elif kind == "deviation":
                        dve.wait_ge(dev_ready, l + 1)
                assert count[0] == DVE_STEPS, count[0]
                hold(dve, "dve")

                with dve.Fori(0, DC) as j:
                    for b in range(3):
                        dve.wait_ge(acc_full, l * UNITS + j * 6 + (PROJ + 3 + b + SLOTS + 1))
                        dve.wait_ge(gate_ready, l * 24 + j * 3 + (b + 1))
                        if b == 0:
                            dve.wait_ge(mix_ready, l * DC + j + FREE)
                        gate = (floor[:, 0, :], floor[:, 1, :], z_tanh[:, :])[b]
                        dve.scalar_tensor_tensor((gated, z, z)[b][:, :], gate, 1.0, acc[(3 + b) % 2][:, :], ALU.add, ALU.mult)\
                           .then_inc(chain_mix, 1)
                        dve.wait_ge(chain_mix, l * (4 * DC) + j * 4 + ((1, 2, 4)[b]))
                        dve.sem_inc(acc_free[(3 + b) % 2], 1)
                        if b == 1:
                            dve.tensor_tensor(gated[:, :], gated[:, :], z[:, :], ALU.add).then_inc(chain_mix, 1)
                            dve.wait_ge(chain_mix, l * (4 * DC) + j * 4 + 3)
                    dve.tensor_tensor(gated[:, :], gated[:, :], z[:, :], ALU.add).then_inc(mix_f, 1)
                    dve.wait_ge(mix_hi, l * DC + j + 1)
                    dve.scalar_tensor_tensor(merged_lo[:, bass.ds(j, 1), :], gated[:, :].rearrange("p (a n) -> p a n", a=1), 0.5,
                                             merged_hi[:, bass.ds(j, 1), :].bitcast(F32), ALU.mult, ALU.subtract).then_inc(mix_ready, 1)

                dve.memset(norm[:, :], 0.0).then_inc(chain_out, 1)
                dve.wait_ge(chain_out, l * (3 * DC + 1) + 1)
                hold(dve, "dve")
                with dve.Fori(0, DC // 2) as i:
                    for b in range(2):
                        xc = xT[:, bass.ds(i * 2 + b, 1), :]
                        dve.wait_ge(acc_full, l * UNITS + i * 2 + (U_OUT + b + SLOTS + 1))
                        dve.tensor_tensor(xc, xc, acc[b][:, :].rearrange("p (a n) -> p a n", a=1), ALU.add).then_inc(chain_out, 1)
                        dve.wait_ge(chain_out, l * (3 * DC + 1) + i * 6 + (3 * b + 2))
                        dve.sem_inc(acc_free[b], 1)
                        dve.tensor_tensor(turn[:, :].rearrange("p (a n) -> p a n", a=1), xc, xc, ALU.mult).then_inc(chain_out, 1)
                        dve.wait_ge(chain_out, l * (3 * DC + 1) + i * 6 + (3 * b + 3))
                        dve.tensor_tensor(norm[:, :], norm[:, :], turn[:, :], ALU.add).then_inc(chain_out, 1)
                        dve.wait_ge(chain_out, l * (3 * DC + 1) + i * 6 + (3 * b + 4))
                dve.sem_inc(sq_ready, 1)

            mean_square(DEPTH)
            dve.wait_ge(std_ready, DEPTH + 1)
            dve.reciprocal(norm[:, :], norm[:, :]).then_inc(pre_zero, 1)
            dve.wait_ge(pre_zero, 1)
            for c in range(DC):
                dve.scalar_tensor_tensor(xT[:, c, :], xT[:, c, :], final_g[:, c:c + 1], norm[:, :], ALU.mult, ALU.mult).then_inc(post_f, 1)


def kernel(**inputs):
    import numpy as np
    import concourse.bacc as bacc
    from concourse.bass_utils import run_bass_kernel_spmd

    a = {k: np.ascontiguousarray(v) for k, v in inputs.items()}
    f32 = a["x"].dtype
    w, b = a["w_in"], a["b_in"]
    half = np.arange(HD)

    def cols(start):
        return np.arange(start, start + P)

    offs = {"aq": 0, "ak": 512, "av": 640, "iq": 768, "ik": 1024, "iw": 1088, "az": 1092, "bq": 1604, "bk": 2116, "bv": 2628,
            "bz": 3140, "cq": 3652, "ck": 4164, "cv": 4676, "ci": 5188, "cf": 5192, "co": 5196, "cz": 5708, "gates": 6220}
    small = np.full(P, -1)
    for at_, name in ((0, "iw"), (32, "ci"), (64, "cf")):
        small[at_:at_ + 4] = offs[name] + np.arange(4)
    units = [cols(offs["iq"]), cols(offs["iq"] + P), np.concatenate([offs["ik"] + half] * 2), small, cols(offs["ak"]), cols(offs["av"])]
    units += [np.concatenate([offs["aq"] + j * HD + half, offs["aq"] + (j + 4) * HD + half]) for j in range(4)]
    for name in ("bq", "bk", "bv", "az", "cq", "ck", "cv", "bz", "co", "cz"):
        units += [cols(offs[name] + j * P) for j in range(4)]
    gate_units = [cols(offs["gates"] + n * D + j * P) for j in range(DC) for n in range(3)]

    def take(m, c):
        padded = np.concatenate([m, np.zeros(m.shape[:-1] + (1,), f32)], axis=-1)
        return padded[..., c]

    def unit(m, c):
        t = take(m, c)
        return t.reshape(DEPTH, -1, P, P).transpose(0, 2, 1, 3).reshape(DEPTH, P, -1)

    wo_units = [unit(a["w_out"], cols(j * P)) for j in range(DC)]
    w_full = np.stack([unit(w, c) for c in units + gate_units] + wo_units, axis=1).reshape(-1, P, D)
    wb = a["w_branch"]
    w_mix = np.stack([unit(wb[:, n], cols(j * P)) for j in range(DC) for n in range(3)], axis=1).reshape(-1, P, BR * P)

    def chunks(m):
        return m.reshape(DEPTH, -1, P).transpose(0, 2, 1)

    fcol = np.zeros((DEPTH, P, 2), f32)
    fcol[:, 64:68, 0] = a["f_bias"]
    params = np.concatenate([np.stack([take(b, c) for c in units], axis=2), chunks(b[:, offs["gates"]:]), chunks(a["norm_g"]),
                             chunks(a["conv_b"]), chunks(a["conv_w"].reshape(DEPTH, -1)), chunks(a["c_norm_w"]), fcol], axis=2)
    dist = np.clip(SEQ - P + np.arange(P)[:, None] - np.arange(SEQ)[None, :], -128, 128) + 128
    rel = a["rel_bias"][:, :, dist].reshape(-1, P, SEQ)

    consts = np.zeros((P, KCOLS), f32)
    consts[:, K_ID:K_ID + P] = np.eye(P)
    p, q = np.arange(P)[:, None], np.arange(P)[None, :]
    consts[:, K_CHUNK:K_CHUNK + P] = np.where(q // 64 <= p // 64, 0.0, NEG)
    consts[:, K_CAUSAL:K_CAUSAL + P] = np.where(p <= q, 0.0, NEG)
    inv = (1.0 / (np.float32(500000.0) ** (np.arange(8, dtype=f32) * np.float32(2.0) / np.float32(16)))).astype(f32)
    ang = np.arange(SEQ, dtype=f32)[None, :] * inv[:, None]
    for s in (0, 64):
        consts[s:s + 64, K_COS:K_COS + SEQ] = 1.0
        for r, sign in ((0, -1.0), (8, 1.0)):
            consts[s + r:s + r + 8, K_COS:K_COS + SEQ] = np.cos(ang)
            consts[s + r:s + r + 8, K_SIN:K_SIN + SEQ] = sign * np.sin(ang)
    for h in range(4):
        consts[h, K_SEL + h * P:K_SEL + (h + 1) * P] = 1.0

    arrays = {"x": a["x"].reshape(SEQ, D), "w_full": w_full, "w_mix": w_mix, "params": params, "rel": rel,
              "final_g": a["final_g"].reshape(DC, P).T, "consts": consts}
    arrays = {k: np.ascontiguousarray(v) for k, v in arrays.items()}
    nc = bacc.Bacc("TRN2", target_bir_lowering=False, num_devices=1, dynamic_dma_scratch_size=1024)
    args = [nc.dram_tensor(k, v.shape, mybir.dt.from_np(v.dtype), kind="ExternalInput").ap() for k, v in arrays.items()]
    out = nc.dram_tensor("out", (SEQ, D), F32, kind="ExternalOutput").ap()
    build(nc, *args, out)
    got = run_bass_kernel_spmd(nc, [arrays], core_ids=[0])
    return got.results[0]["out"].reshape(1, SEQ, D)
```

```python
from contextlib import ExitStack

import concourse.bass as bass
from concourse import mybir

F32 = mybir.dt.float32
F32R = mybir.dt.float32r
BF16 = mybir.dt.bfloat16
ALU = mybir.AluOpType
ACT = mybir.ActivationFunctionType

P = 128
DEPTH, SEQ, D = 2, 512, 1024
NT = SEQ // P
DC = D // P
HEADS, HD = 8, 64
IDX_HEADS = 4
TOPK = 128
CH = 4
BR = 4
EPS = 1e-6
NEG = -1.0e30
INADMISSIBLE = -1.0e38
TAKEN = -3.0e38

U_IQ, U_IK, U_SMALL, U_AK, U_AV, U_AQ = 0, 2, 3, 4, 5, 6
U_BQ, U_BK, U_BV, U_CQ, U_CK, U_CV, U_AZ, U_BZ, U_CO, U_CZ = 10, 14, 18, 22, 26, 30, 34, 38, 42, 46
PROJ = 50
MIX = DC * 6
UNITS = PROJ + MIX + DC
U_OUT = PROJ + MIX
PASSES = 3 * DC
FREE = 1
SLOTS = 2
RAW = 4
RAW_USES = [(UNITS - s + RAW - 1) // RAW for s in range(RAW)]
C_GATE, C_NORM, C_CONVB, C_CONVW, C_CNORM, C_FBIAS, PCOLS = PROJ, 74, 82, 90, 122, 126, 128
K_ID, K_CHUNK, K_CAUSAL, K_COS, K_SIN, K_SEL, KCOLS = 0, 128, 256, 384, 896, 1408, 1920


def schedule():
    seq = []
    flying = []

    def push(n):
        seq.append(CUT)
        if n is not None:
            seq.append(("scores", n))
        flying.append(n)
        mlstm = any(m is not None and m >= 64 for m in flying[-4:])
        for back, kind in ((1, "exp"), (2, "turn_p"), (3, "values")) if mlstm else ((3, "turn_p"), (2, "exp"), (4, "values")):
            if len(flying) >= back and flying[-back] is not None:
                seq.append((kind, flying[-back]))

    def flush():
        for _ in range(3):
            push(None)
        flying.clear()

    def units(a, b):
        seq.extend(("unit", u) for u in range(a, b))

    def index(t):
        for h in range(IDX_HEADS):
            seq.extend((CUT, ("index", (t, h))))

    def topk(t, a=0, b=TOPK // 8):
        seq.append(("topk", (t, a, b)))

    units(0, 1)
    seq.append(("rope", 0))
    units(1, 2)
    seq.append(("rope", 1))
    units(2, 3)
    seq.append(("rope", 2))
    units(3, 5)
    seq.append(("turn_iw", 0))
    seq.append(("rope", U_AK))
    index(1)
    topk(1)
    units(5, 7)
    seq.append(("turn_v", U_AV))
    units(7, 8)
    seq.append(("rope", U_AQ))
    seq.append(("rope", U_AQ + 1))
    index(2)
    topk(2)
    units(8, 13)
    seq.append(("rope", U_AQ + 2))
    seq.append(("rope", U_AQ + 3))
    index(3)
    seq.append(("rel_bias", 0))
    seq.append(("rel_bias", 1))
    first = 17
    units(13, first)
    n, late, rows = 0, [], -1
    for u in range(first, 38):
        units(u, u + 1)
        upto = -(-64 * (u + 1 - first) // (38 - first))
        k = 0
        while n < upto:
            push(n)
            if n < TOPK // 8:
                topk(3, n, n + 1)
            if n == 31:
                flush()
                rows = 0
            if n >= 32 and n % NT == NT - 1 and (n - 32) // NT + 2 < HEADS:
                seq.append(("rel_bias", (n - 32) // NT + 2))
            n += 1
            if k == 1:
                seq.extend(late)
                late = []
            k += 1
        if 0 <= rows < 6:
            seq.append(("rows", rows))
            rows += 1
        if U_BV <= u < U_CQ or U_CV <= u < U_AZ:
            late.append(("turn_v", u))
        if U_CQ <= u < U_CV:
            seq.append(("conv", u - U_CQ))
            late.append(("conv_gate", u - U_CQ))
        if U_AZ <= u:
            seq.extend((CUT, ("z_a", u - U_AZ)))
            late.append(("y_split", u - U_AZ))
    assert rows == 6
    flush()
    assert n == 64
    seq.append(("turn_c", 0))
    for u in range(38, 42):
        units(u, u + 1)
        for k in range(NT):
            push(n)
            n += 1
            if k == 2:
                seq.extend(late)
                late = []
        seq.extend((CUT, ("z_b", u - U_BZ)))
        late.append(("y_split", u - U_BZ + BR))
    flush()
    units(42, 43)
    seq.extend(late)
    for u in range(43, 46):
        units(u, u + 1)
        seq.extend((CUT, ("out_gate", u - 43)))
    seq.append(("out_gate", 3))
    units(46, 47)
    seq.append(("deviation", 0))
    units(47, 48)
    seq.append(("z_c", 0))
    seq.append(("y_split", 8))
    units(48, 49)
    seq.append(("z_c", 1))
    seq.append(("y_split", 9))
    units(49, 50)
    seq.append(("z_c", 2))
    seq.append(("y_split", 10))
    seq.append(("z_c", 3))
    seq.append(("y_split", 11))
    return interleave(seq)


CUT = ("cut", None)


def interleave(steps):
    seq, groups = [], [[]]
    for step in steps:
        if step == CUT:
            groups.append([])
        elif step[0] == "unit":
            groups = [g for g in groups if g]
            at = 0
            for i, g in enumerate(groups):
                to = (2 * i + 1) * PASSES // (2 * len(groups))
                if to > at:
                    seq.append(("passes", (step[1], at, to)))
                    at = to
                seq.extend(g)
            seq.append(("passes", (step[1], at, PASSES)))
            seq.append(step)
            groups = [[]]
        else:
            groups[-1].append(step)
    return seq + [step for g in groups for step in g]


SEQUENCE = schedule()


def order(*kinds):
    steps = [s for s in SEQUENCE if s[0] in kinds]
    return {s: n for n, s in enumerate(steps)}, len(steps)


SCORE_USE, SCORE_USES = order("index", "scores")
SPARE_USE, SPARE_USES = order("turn_iw", "turn_v", "z_a", "z_b", "z_c", "turn_c", "out_gate")
SPARE_USES += 2
ITEMS = 80
GROUPS = 24
ROPE, ROPES = order("rope")
DVE_STEPS = 261


def item(n):
    if n < 32:
        return "a", n % HEADS, n // HEADS
    if n < 64:
        return "b", (n - 32) // NT, n % NT
    return "c", (n - 64) // NT, n % NT


def group(n):
    return (n // 4, n % 4, 4) if n < 64 else (n // 2 - 16, n % 2, 2)


def evacs(l, n):
    return l * (PROJ - 1) + (n + 1 if n < U_SMALL else n)


def build(nc, x_in, w_full, w_mix, params_in, rel_in, final_in, consts_in, out):
    ctx = ExitStack()
    with ctx:
        cursor = [(nc.sbuf_base + 63) // 64 * 64]

        def at(name, shape, dt, offset):
            return nc.alloc_sbuf_tensor_at(name, shape, dt, offset=offset)

        def region(size):
            a = cursor[0]
            cursor[0] += (size + 31) // 32 * 32
            assert cursor[0] <= nc.sbuf_usable_end, cursor[0]
            return a

        def sb(name, shape, dt=F32):
            size = mybir.dt.size(dt)
            for s in shape[1:]:
                size *= s
            return at(name, shape, dt, region(size))

        ROW = SEQ * 4
        xT = sb("xT", [P, DC, SEQ])
        h_hi = sb("h_hi", [P, DC, SEQ], F32R)
        h_lo = sb("h_lo", [P, DC, SEQ], F32R)
        w_raw = sb("w_raw", [P, RAW, DC, P])
        w_hi = sb("w_hi", [P, SLOTS, DC, P], F32R)
        w_lo = sb("w_lo", [P, SLOTS, DC, P], F32R)
        r1 = region(9 * ROW)
        aq = at("aq", [P, BR, SEQ], F32, r1)
        ak = at("ak", [P, SEQ], F32, r1 + 4 * ROW)
        av = at("av", [P, NT, P], F32, r1 + 5 * ROW)
        iq = at("iq", [P, 2, SEQ], F32, r1 + 6 * ROW)
        ik = at("ik", [P, SEQ], F32, r1 + 8 * ROW)
        ya_hi = at("ya_hi", [P, BR, SEQ], F32R, r1)
        ya_lo = at("ya_lo", [P, BR, SEQ], F32R, r1 + 4 * ROW)
        r2 = region(24 * ROW + 64)
        bq = at("bq", [P, BR, SEQ], F32, r2)
        bk = at("bk", [P, BR, SEQ], F32, r2 + 4 * ROW)
        bv = at("bv", [P, NT, BR * P], F32, r2 + 8 * ROW)
        yb_hi = at("yb_hi", [P, BR, SEQ], F32R, r2)
        yb_lo = at("yb_lo", [P, BR, SEQ], F32R, r2 + 4 * ROW)
        r3 = r2 + 12 * ROW
        cv = at("cv", [P, NT, CH, P + 1], F32, r3)
        cq = at("cq", [P, CH, SEQ], F32, r3 + 4 * ROW + 64)
        ck = at("ck", [P, CH, SEQ], F32, r3 + 8 * ROW + 64)
        yc_hi = at("yc_hi", [P, BR, SEQ], F32R, r3 + 4 * ROW + 64)
        yc_lo = at("yc_lo", [P, BR, SEQ], F32R, r3 + 8 * ROW + 64)
        merged_lo = at("merged_lo", [P, DC, SEQ], F32R, r2 + 8 * ROW)
        r4 = region(8 * ROW)
        att = {"a": at("att_a", [P, NT, HEADS * HD], F32, r4), "b": at("att_b", [P, NT, HEADS * HD], F32, r4 + 4 * ROW)}
        att["c"] = at("att_c", [P, NT, CH * P], F32, r4)
        merged_hi = at("merged_hi", [P, DC, SEQ], F32R, r4)
        stage = at("stage", [P, NT, D], F32, r4)
        MASK_AT = {1: 0, 2: 256, 3: 640}
        r5 = region(1152 * 4 + 4 * ROW)
        key_mask = at("key_mask", [P, 1152], F32, r5)
        score = at("score", [P, 2, SEQ], F32, r5 + 1152 * 4)
        rel = at("rel", [P, 2, SEQ], F32, r5 + 1152 * 4 + 2 * ROW)
        SUM_AT = [0, 512, 896, 1152]
        decay = at("decay", [CH, 1280], F32, r5)
        run_max = at("run_max", [CH, SEQ], F32, r5 + 1280 * 4)
        assert 1280 * 4 + ROW <= 1152 * 4 + 2 * ROW

        consts = sb("consts", [P, KCOLS])
        ones = sb("ones", [P, SEQ])
        ident_b = sb("ident_b", [P, P], BF16)
        causal_b = sb("causal_b", [P, P], BF16)
        par_next = sb("par_next", [P, PCOLS])
        par = sb("par", [P, PCOLS])
        par_half = sb("par_half", [P, PCOLS])
        par_eighth = sb("par_eighth", [P, PCOLS])
        final_g = sb("final_g", [P, DC])
        prob = sb("prob", [P, 3, SEQ])
        prob_t = sb("prob_t", [P, 2, SEQ])
        turn = sb("turn", [P, SEQ])
        norm = sb("norm", [P, SEQ])
        log1p = source = norm[0:CH, :]
        sel_r = sb("sel_r", [36, CH * P], F32R)
        decay_r = sb("decay_r", [36, 1280], F32R)
        pad = sb("pad", [P, 2, SEQ + 4])
        z_tanh = sb("z_tanh", [P, SEQ])
        z = sb("z", [P, SEQ])
        iw_row = at("iw_row", [IDX_HEADS, SEQ], F32, cursor[0] - ROW)
        gated = sb("gated", [P, SEQ])
        i_row = sb("i_row", [CH, SEQ])
        f_row = sb("f_row", [CH, SEQ])
        top8 = sb("top8", [P, 8])
        iw = sb("iw", [P, NT, IDX_HEADS])
        source_t = sb("source_t", [P, NT, CH])
        neg_max = sb("neg_max", [P, 4])
        row_sum = sb("row_sum", [P, 8])
        row_inv = sb("row_inv", [P, 4])
        floor_t = sb("floor_t", [P, NT, CH])
        tok = sb("tok", [P, NT])
        stats = sb("stats", [P, NT, 6])
        moments = sb("moments", [P, NT, CH, 2])
        dev = sb("dev", [P, NT, CH])

        ident = consts[:, K_ID:K_ID + P]
        cos, sin = consts[:, K_COS:K_COS + SEQ], consts[:, K_SIN:K_SIN + SEQ]

        def psum(name):
            return ctx.enter_context(nc.psum_tensor(name, [P, SEQ], F32))

        acc = [psum("acc0"), psum("acc1")]
        ps_s = [psum("ps_s0"), psum("ps_s1")]
        ps_t = [psum("ps_t0"), psum("ps_t1")]
        ps_o = psum("ps_o")
        spare = psum("spare")

        def sem(name):
            return ctx.enter_context(nc.semaphore(name))

        consts_in_s, params_in_s, rel_in_s, x_in_s, out_s = (
            sem("consts_loaded"), sem("params_loaded"), [sem("rel_loaded0"), sem("rel_loaded1")], sem("x_loaded"), sem("out_stored"))
        raw_full = [sem(f"raw_full{s}") for s in range(RAW)]
        w_hi_done, split_full, acc_full = sem("w_hi_done"), sem("split_full"), sem("acc_full")
        acc_free = [sem("acc_free0"), sem("acc_free1")]
        const_ready, ones_ready, par_done = sem("const_ready"), sem("ones_ready"), sem("par_done")
        sq_ready, mean_ready, std_ready = sem("sq_ready"), sem("mean_ready"), sem("std_ready")
        hf_ready, h_hi_ready, h_even, h_odd = sem("hf_ready"), sem("h_hi_ready"), sem("h_even"), sem("h_odd")
        tok_ready, spread_ready = sem("tok_ready"), sem("spread_ready")
        spare_full, spare_free = sem("spare_full"), sem("spare_free")
        evac, roped, conv_sum, conv_tanh, conv_done = (
            sem("evac"), sem("roped"), sem("conv_sum"), sem("conv_tanh"), sem("conv_done"))
        small_ready, score_part = sem("small_ready"), sem("score_part")
        score_full, score_free = sem("score_full"), [sem("score_free0"), sem("score_free1")]
        max_ready, prob_ready = sem("max_ready"), sem("prob_ready")
        turn_full, turn_free = sem("turn_full"), [sem("turn_free0"), sem("turn_free1")]
        out_full, out_free = sem("out_full"), sem("out_free")
        z_ready, gated_ready, y_hi_ready, y_ready = sem("z_ready"), sem("gated_ready"), sem("y_hi_ready"), sem("y_ready")
        neg_abs, log_ready, rows_ready, rows_hi = sem("neg_abs"), sem("log_ready"), sem("rows_ready"), sem("rows_hi")
        decay_ready, floor_ready, ones_col = sem("decay_ready"), sem("floor_ready"), sem("ones_col")
        og_used, var_ready, dev_ready, normed = sem("og_used"), sem("var_ready"), sem("dev_ready"), sem("normed")
        gate_ready, mix_f, mix_hi, mix_ready = sem("gate_ready"), sem("mix_f"), sem("mix_hi"), sem("mix_ready")
        x_step = sem("x_step")
        pre_t, pre_x = sem("pre_t"), sem("pre_x")
        post_f, post_t, post_x = sem("post_f"), sem("post_t"), sem("post_x")
        chain, chain_mix, chain_out = sem("chain"), sem("chain_mix"), sem("chain_out")
        held = {"pe": sem("pe_held"), "dve": sem("dve_held"), "pool": sem("pool_held")}

        def hold(eng, name):
            eng.sem_inc(held[name], 1)

        block = ctx.enter_context(nc.Block())

        @block.sync
        def _(sp):
            sp.dma_start(stage[:], x_in.rearrange("(t p) d -> p t d", p=P)).then_inc(x_in_s, 16)
            sp.dma_start(consts[:], consts_in).then_inc(consts_in_s, 16)
            sp.dma_start(final_g[:], final_in).then_inc(consts_in_s, 16)

            def load(l, u, slot, source, nk, back=RAW):
                sp.wait_ge(split_full, l * UNITS + u + (RAW + 1 - back))
                sp.dma_start(w_raw[:, slot, 0:nk, :], source).then_inc(raw_full[slot], 16)

            def full(n):
                return w_full[bass.ds(n, 1), :, :].rearrange("a p (k c) -> (a p) k c", c=P)

            with sp.Fori(0, DEPTH) as l:
                sp.wait_ge(par_done, l * 3 + FREE)
                sp.dma_start(par_next[:], params_in[bass.ds(l, 1), :, :].rearrange("a p c -> (a p) c")).then_inc(params_in_s, 16)
                for u in range(2):
                    load(l, u, u, full(l * 82 + u), DC, back=2)
                with sp.Fori(0, (PROJ - 2) // RAW) as i:
                    for b in range(2, RAW + 2):
                        load(l, i * RAW + b, b % RAW, full(l * 82 + i * RAW + b), DC)
                with sp.Fori(0, DC // 2) as i:
                    for b in range(12):
                        j, b6 = b // 6, b % 6
                        if b6 < 3:
                            src = full(l * 82 + i * 6 + (PROJ + j * 3 + b6))
                        else:
                            src = w_mix[bass.ds(l * 24 + i * 6 + (j * 3 + b6 - 3), 1), :, :].rearrange("a p (k c) -> (a p) k c", c=P)
                        load(l, i * 12 + (PROJ + b), (PROJ + b) % RAW, src, DC if b6 < 3 else BR)
                with sp.Fori(0, DC // RAW) as i:
                    for b in range(RAW):
                        load(l, i * RAW + (U_OUT + b), (U_OUT + b) % RAW, full(l * 82 + i * RAW + (74 + b)), DC)
            for t in range(NT):
                sp.wait_ge(post_x, 2 * t + 2)
                sp.dma_start(out[t * P:(t + 1) * P, :], stage[:, t, :]).then_inc(out_s, 16)
            sp.wait_ge(out_s, 16 * NT)

        @block.gpsimd
        def _(pool):
            pool.memset(ones[:], 1.0).then_inc(ones_ready, 1)
            pool.memset(pad[:], 0.0).then_inc(ones_ready, 1)
            pool.memset(decay_r[:].bitcast(F32), 0.0).then_inc(ones_ready, 1)
            pool.sem_inc(split_full, RAW)
            for free in (*acc_free, spare_free, *score_free, *turn_free, out_free, mix_f, mix_ready, par_done):
                pool.sem_inc(free, FREE)

            def split(l, u, slot, raw, nk):
                pool.wait_ge(w_hi_done, l * UNITS + u + 1)
                pool.tensor_tensor(w_lo[:, slot, 0:nk, :], w_raw[:, raw, 0:nk, :], w_hi[:, slot, 0:nk, :].bitcast(F32),
                                   ALU.subtract).then_inc(split_full, 1)

            with pool.Fori(0, DEPTH) as l:
                for u in range(2):
                    split(l, u, u, u, DC)
                for c in range(1, DC, 2):
                    pool.wait_ge(h_hi_ready, l * DC + c + 1)
                    pool.tensor_tensor(h_lo[:, c, :], pad[:, 1, 3:3 + SEQ], h_hi[:, c, :].bitcast(F32), ALU.subtract).then_inc(h_odd, 1)
                with pool.Fori(0, (PROJ - 2) // RAW) as i:
                    for b in range(2, RAW + 2):
                        split(l, i * RAW + b, b % SLOTS, b % RAW, DC)
                with pool.Fori(0, DC // 2) as i:
                    for b in range(12):
                        split(l, i * 12 + (PROJ + b), b % SLOTS, (PROJ + b) % RAW, DC if b % 6 < 3 else BR)
                with pool.Fori(0, DC // RAW) as i:
                    for b in range(RAW):
                        split(l, i * RAW + (U_OUT + b), b % SLOTS, (U_OUT + b) % RAW, DC)

        @block.tensor
        def _(pe):
            pe.wait_ge(consts_in_s, 32)
            pe.wait_ge(x_in_s, 16)
            for c in range(DC):
                if c >= 2:
                    pe.wait_ge(pre_x, c - 1)
                for t in range(NT):
                    last = pe.transpose(ps_s[c % 2][:, t * P:(t + 1) * P], stage[:, t, c * P:(c + 1) * P], ident)
                last.then_inc(pre_t, 1)
            pe.wait_ge(pre_x, DC)
            pe.wait_ge(ones_ready, 3)
            pe.wait_ge(const_ready, 3)
            pe.transpose(spare[:, 0:P], ident, ident).then_inc(acc_full, SLOTS)

            def product(l, u, slot, uses, hi, lo, nk, first=0, to=PASSES, per_chunk=None):
                if first == 0:
                    pe.wait_ge(w_hi_done, l * UNITS + u + 1)
                    pe.wait_ge(acc_free[slot], l * (UNITS // 2) + uses + FREE)
                for i in range(first, min(to, 3 * nk)):
                    if i == 2 * nk:
                        pe.wait_ge(split_full, l * UNITS + u + (RAW + 1))
                    k = i // 2 if i < 2 * nk else i - 2 * nk
                    if per_chunk and i < 2 * nk and i % 2 == 0:
                        per_chunk(k)
                    w, x = (w_lo, hi) if i >= 2 * nk else (w_hi, lo if i % 2 else hi)
                    last = pe.matmul(acc[slot][:, :], w[:, slot, k, :], x[:, k, :], start=(i == 0), stop=(i == 3 * nk - 1))
                if to == PASSES:
                    last.then_inc(acc_full, 1)

            def use_spare(l, step):
                pe.wait_ge(spare_free, l * SPARE_USES + SPARE_USE[step] + 2 + FREE)

            def norm_sum(n):
                pe.wait_ge(sq_ready, n + 1)
                for t in range(NT):
                    last = pe.matmul(spare[:, t:t + 1], norm[:, t * P:(t + 1) * P], ones[:, 0:1], start=True, stop=True)
                last.then_inc(spare_full, 1)
                pe.wait_ge(spread_ready, n + 1)
                pe.matmul(spare[:, :], ones[:, 0:P], turn[:, :], start=True, stop=True).then_inc(spare_full, 1)

            def scores_bank(l, step):
                use = SCORE_USE[step]
                pe.wait_ge(score_free[use % 2], l * (SCORE_USES // 2) + use // 2 + FREE)
                return ps_s[use % 2]

            with pe.Fori(0, DEPTH) as l:
                pe.wait_ge(spare_free, l * SPARE_USES + FREE)
                norm_sum(l)
                for kind, n in SEQUENCE:
                    step = (kind, n)
                    if kind == "passes":
                        n, first, to = n
                        product(l, n, n % 2, n // 2, h_hi, h_lo, DC, first, to,
                                (lambda k: pe.wait_ge((h_even, h_odd)[k % 2], l * (DC // 2) + k // 2 + 1)) if n == 0 else None)
                    elif kind == "turn_iw":
                        use_spare(l, step)
                        pe.wait_ge(small_ready, l + 1)
                        hold(pe, "pe")
                        for t in range(NT):
                            last = pe.transpose(spare[:, t * IDX_HEADS:(t + 1) * IDX_HEADS],
                                                iw_row[:, t * P:(t + 1) * P], ident[0:IDX_HEADS, 0:IDX_HEADS])
                        last.then_inc(spare_full, 1)
                    elif kind == "turn_v":
                        use_spare(l, step)
                        pe.wait_ge(evac, evacs(l, n))
                        for t in range(NT):
                            last = pe.transpose(spare[:, t * P:(t + 1) * P], pad[:, n % 2, 3 + t * P:3 + (t + 1) * P], ident)
                        last.then_inc(spare_full, 1)
                    elif kind == "index":
                        t, h = n
                        bank = scores_bank(l, step)
                        pe.wait_ge(roped, l * ROPES + ROPE[("rope", U_IK)] + 1)
                        b = h % 2 * HD
                        pe.matmul(bank[:, 0:(t + 1) * P], iq[b:b + HD, h // 2, t * P:(t + 1) * P],
                                  ik[b:b + HD, 0:(t + 1) * P], start=True, stop=True).then_inc(score_full, 1)
                    elif kind == "scores":
                        branch, h, t = item(n)
                        bank = scores_bank(l, step)
                        w = (t + 1) * P
                        if branch == "a":
                            pe.wait_ge(roped, l * ROPES + ROPES)
                            b = h // BR * HD
                            pe.matmul(bank[:, 0:w], aq[b:b + HD, h % BR, t * P:w], ak[b:b + HD, 0:w],
                                      start=True, stop=True).then_inc(score_full, 1)
                        elif branch == "b":
                            pe.wait_ge(evac, evacs(l, U_BV - 1))
                            b = h % 2 * HD
                            pe.matmul(bank[:, 0:w], bq[b:b + HD, h // 2, t * P:w], bk[b:b + HD, h // 2, 0:w],
                                      start=True, stop=True).then_inc(score_full, 1)
                        else:
                            pe.wait_ge(decay_ready, l + 1)
                            for s in range(t + 1):
                                o = SUM_AT[s] + (t - s) * P
                                pe.matmul(bank[:, s * P:(s + 1) * P], sel_r[:, h * P:(h + 1) * P], decay_r[:, o:o + P],
                                          start=True, stop=(s < t))
                            pe.matmul(bank[:, t * P:w], ident_b[:, :], causal_b[:, :], start=False, stop=True).then_inc(score_full, 1)
                            pe.wait_ge(turn_free[n % 2], l * (ITEMS // 2) + n // 2 + FREE)
                            pe.wait_ge(conv_done, l * 2 * CH + 2 * CH)
                            for s in range(t + 1):
                                last = pe.matmul(ps_t[n % 2][:, s * P:(s + 1) * P], ck[:, h, s * P:(s + 1) * P],
                                                 cq[:, h, t * P:w], start=True, stop=True)
                            last.then_inc(turn_full, 1)
                    elif kind == "turn_p":
                        branch, h, t = item(n)
                        if branch != "c":
                            pe.wait_ge(turn_free[n % 2], l * (ITEMS // 2) + n // 2 + FREE)
                            pe.wait_ge(prob_ready, l * ITEMS + n + 1)
                            for s in range(t + 1):
                                last = pe.transpose(ps_t[n % 2][:, s * P:(s + 1) * P], prob[:, n % 3, s * P:(s + 1) * P], ident)
                            last.then_inc(turn_full, 1)
                    elif kind == "values":
                        branch, h, t = item(n)
                        pe.wait_ge(turn_free[n % 2], l * (ITEMS // 2) + n // 2 + 1 + FREE)
                        g, place, size = group(n)
                        if place == 0:
                            pe.wait_ge(out_free, l * GROUPS + g + FREE)
                        if branch != "c":
                            pe.wait_ge(spare_free, l * SPARE_USES + SPARE_USE[("turn_v", U_AV if branch == "a" else U_CQ - 1)] + 3 + FREE)
                            v, f = (av, h // BR * HD) if branch == "a" else (bv, h * HD)
                            for s in range(t + 1):
                                last = pe.matmul(ps_o[:, place * HD:(place + 1) * HD], prob_t[:, n % 2, s * P:(s + 1) * P],
                                                 v[:, s, f:f + HD], start=(s == 0), stop=(s == t))
                        else:
                            pe.wait_ge(spare_free, l * SPARE_USES + SPARE_USE[("turn_v", U_AZ - 1)] + 3 + FREE)
                            pe.wait_ge(ones_col, l + 1)
                            for s in range(t + 1):
                                last = pe.matmul(ps_o[:, place * 2 * P:place * 2 * P + P + 1], prob_t[:, n % 2, s * P:(s + 1) * P],
                                                 cv[:, s, h, :], start=(s == 0), stop=(s == t))
                        last.then_inc(out_full, 1)
                    elif kind in ("z_a", "z_b", "z_c"):
                        use_spare(l, step)
                        if kind == "z_c":
                            pe.wait_ge(normed, l + 1)
                        else:
                            pe.wait_ge(out_free, l * GROUPS + (8 if kind == "z_a" else 16) + FREE)
                        for t in range(NT):
                            last = pe.transpose(spare[:, t * P:(t + 1) * P], att[kind[2]][:, t, n * P:(n + 1) * P], ident)
                        last.then_inc(spare_full, 1)
                    elif kind == "turn_c":
                        use_spare(l, step)
                        pe.wait_ge(floor_ready, l + 1)
                        hold(pe, "pe")
                        for t in range(NT):
                            pe.transpose(spare[:, t * CH:(t + 1) * CH], source[:, t * P:(t + 1) * P], ident[0:CH, 0:CH])
                            last = pe.transpose(spare[:, (NT + t) * CH:(NT + t + 1) * CH], run_max[:, t * P:(t + 1) * P],
                                                ident[0:CH, 0:CH])
                        last.then_inc(spare_full, 1)
                    elif kind == "out_gate":
                        use_spare(l, step)
                        pe.wait_ge(evac, evacs(l, U_CO + n))
                        for t in range(NT):
                            last = pe.transpose(spare[:, t * P:(t + 1) * P], (z_tanh, z)[n % 2][:, t * P:(t + 1) * P], ident)
                        last.then_inc(spare_full, 1)
                with pe.Fori(0, DC) as j:
                    for b in range(3):
                        product(l, j * 6 + (PROJ + b), b % 2, j * 3 + (PROJ // 2 + b // 2), h_hi, h_lo, DC)
                    for b, (hi, lo) in enumerate(((ya_hi, ya_lo), (yb_hi, yb_lo), (yc_hi, yc_lo))):
                        pe.wait_ge(y_ready, l * 12 + 4 * b + 4)
                        product(l, j * 6 + (PROJ + 3 + b), (3 + b) % 2, j * 3 + (PROJ // 2 + (3 + b) // 2), hi, lo, BR)
                product(l, U_OUT, 0, U_OUT // 2, merged_hi, merged_lo, DC, per_chunk=
                        lambda k: pe.wait_ge(mix_ready, l * DC + (k + 1 + FREE)))
                product(l, U_OUT + 1, 1, U_OUT // 2, merged_hi, merged_lo, DC)
                with pe.Fori(1, DC // 2) as i:
                    for b in range(2):
                        product(l, i * 2 + (U_OUT + b), b, i + U_OUT // 2, merged_hi, merged_lo, DC)
            pe.wait_ge(spare_free, DEPTH * SPARE_USES + FREE)
            norm_sum(DEPTH)
            pe.wait_ge(post_f, DC)
            for n in range(2 * NT):
                if n >= 2:
                    pe.wait_ge(post_x, n - 1)
                t, half = n // 2, n % 2
                for c in range(4):
                    last = pe.transpose(ps_s[n % 2][:, c * P:(c + 1) * P], xT[:, half * 4 + c, t * P:(t + 1) * P], ident)
                last.then_inc(post_t, 1)

        @block.scalar
        def _(act):
            for c in range(DC):
                act.wait_ge(pre_t, c + 1)
                act.activation(xT[:, c, :], ps_s[c % 2][:, :], ACT.Copy).then_inc(pre_x, 1)
            act.wait_ge(consts_in_s, 32)
            act.activation(ident_b[:, :], ident, ACT.Copy).then_inc(const_ready, 1)
            act.activation(causal_b[:, :], consts[:, K_CAUSAL:K_CAUSAL + P], ACT.Copy).then_inc(const_ready, 1)

            act.activation(sel_r[:, :], consts[0:36, K_SEL:K_SEL + CH * P], ACT.Copy).then_inc(const_ready, 1)

            def high_part(l, first, b, nk=DC):
                raw, slot = b % RAW, b % SLOTS
                act.wait_ge(raw_full[raw], (l * RAW_USES[raw] + first // RAW + (b // RAW + 1)) * 16 if isinstance(first, int)
                            else (l * RAW_USES[raw] + first[1] + (b // RAW + 1)) * 16)
                at_u = first if isinstance(first, int) else first[0]
                act.wait_ge(acc_full, l * UNITS + at_u + (b + 1))
                act.activation(w_hi[:, slot, 0:nk, :], w_raw[:, raw, 0:nk, :], ACT.Copy).then_inc(w_hi_done, 1)

            with act.Fori(0, DEPTH) as l:
                high_part(l, 0, 0)
                high_part(l, 0, 1)
                act.wait_ge(params_in_s, l * 16 + 16)
                act.wait_ge(mean_ready, l + 1)
                act.activation(tok[:, :], tok[:, :], ACT.Sqrt).then_inc(std_ready, 1)
                act.activation(par[:, :], par_next[:, :], ACT.Copy).then_inc(par_done, 1)
                act.activation(par_half[:, :], par_next[:, :], ACT.Copy, scale=0.5).then_inc(par_done, 1)
                act.activation(par_eighth[:, :], par_next[:, :], ACT.Copy, scale=HD ** -0.5).then_inc(par_done, 1)
                for c in range(DC):
                    act.wait_ge(hf_ready, l * DC + c + 1)
                    act.activation(h_hi[:, c, :], pad[:, c % 2, 3:3 + SEQ], ACT.Copy).then_inc(h_hi_ready, 1)
                act.wait_ge(par_done, l * 3 + 3 + FREE)

                def z_tile(zn, which):
                    return ((z_tanh[:, :], z[:, :]) if zn < 8 or zn % 2 == 0 else (prob[:, 0, :], prob[:, 1, :]))[which]

                def read_sums(n):
                    act.wait_ge(acc_full, l * UNITS + n + (SLOTS + 1))
                    src, free = acc[n % 2][:, :], acc_free[n % 2]
                    bias, half = par[:, n:n + 1], par_half[:, n:n + 1]
                    if U_AZ <= n < U_CO or n >= U_CZ:
                        zn = n - U_AZ if n < U_CO else n - U_CZ + 2 * BR
                        before = zn - (1 if n <= U_CZ else 2)
                        if before >= 0:
                            act.wait_ge(gated_ready, l * 12 + before + 1)
                        if n == U_CZ:
                            act.wait_ge(og_used, l * CH + CH)
                        act.activation(z_tile(zn, 0), src, ACT.Tanh, bias=half, scale=0.5)
                        act.activation(z_tile(zn, 1), src, ACT.Identity, bias=bias).then_inc(z_ready, 1)
                        act.wait_ge(z_ready, l * 12 + zn + 1)
                        act.sem_inc(free, 1)
                        act.sem_inc(evac, 1)
                        return
                    if U_CO <= n < U_CZ:
                        act.wait_ge(gated_ready, l * 12 + 8)
                        if n >= U_CO + 2:
                            act.wait_ge(og_used, l * CH + n - U_CO - 1)
                        act.activation((z_tanh, z)[n % 2][:, :], src, ACT.Tanh, bias=half, scale=0.5).then_inc(evac, 1)
                        act.wait_ge(evac, evacs(l, n))
                        act.sem_inc(free, 1)
                        return
                    scale = 1.0
                    if n < U_IK:
                        dst = iq[:, n, :]
                    elif n == U_IK:
                        dst = ik[:, :]
                    elif n == U_AK:
                        dst = ak[:, :]
                    elif U_AQ <= n < U_BQ:
                        dst, scale, bias = aq[:, n - U_AQ, :], HD ** -0.5, par_eighth[:, n:n + 1]
                    elif U_BQ <= n < U_BK:
                        dst, scale, bias = bq[:, n - U_BQ, :], HD ** -0.5, par_eighth[:, n:n + 1]
                    elif U_BK <= n < U_BV:
                        dst = bk[:, n - U_BK, :]
                    else:
                        dst = pad[:, n % 2, 3:3 + SEQ]
                        if n == U_AV:
                            act.wait_ge(h_even, (l + 1) * (DC // 2))
                            act.wait_ge(h_odd, (l + 1) * (DC // 2))
                        elif U_CQ <= n - 2 < U_CV:
                            act.wait_ge(conv_sum, l * 8 + n - 2 - U_CQ + 1)
                        elif n - 2 >= U_BV:
                            act.wait_ge(spare_full, l * SPARE_USES + SPARE_USE[("turn_v", n - 2)] + 3)
                    act.activation(dst, src, ACT.Identity, bias=bias, scale=scale).then_inc(evac, 1)
                    act.wait_ge(evac, evacs(l, n))
                    act.sem_inc(free, 1)

                for kind, n in SEQUENCE:
                    step = (kind, n)
                    if kind == "unit":
                        if n != U_SMALL:
                            read_sums(n)
                        high_part(l, 0, n + 2)
                    elif kind == "turn_v":
                        act.wait_ge(spare_full, l * SPARE_USES + SPARE_USE[step] + 3)
                        if n == U_AV:
                            dst = av[:, :, :]
                        else:
                            dst = bv[:, :, (n - U_BV) * P:(n - U_BV + 1) * P] if n < U_CQ else cv[:, :, n - U_CV, 0:P]
                        act.activation(dst, spare[:, :].rearrange("p (t c) -> p t c", t=NT), ACT.Copy).then_inc(spare_free, 1)
                    elif kind == "conv_gate":
                        act.wait_ge(conv_sum, l * 8 + n + 1)
                        act.activation(z_tanh[:, :], turn[:, :], ACT.Tanh, scale=0.5).then_inc(conv_tanh, 1)
                    elif kind == "index":
                        t, h = n
                        use = SCORE_USE[step]
                        act.wait_ge(score_full, l * SCORE_USES + use + 1)
                        if (t, h) > (1, 1):
                            act.wait_ge(score_part, l * 12 + (t - 1) * 4 + h - 1)
                        act.activation(prob[:, h % 2, 0:(t + 1) * P], ps_s[use % 2][:, 0:(t + 1) * P], ACT.Relu)\
                           .then_inc(score_free[use % 2], 1)
                    elif kind == "rel_bias":
                        if n >= 2:
                            act.wait_ge(max_ready, l * 64 + 32 + 4 * (n - 1))
                        act.dma_start(rel[:, n % 2, :], rel_in[bass.ds(l * HEADS + n, 1), :, :].rearrange("a p k -> (a p) k"))\
                           .then_inc(rel_in_s[n % 2], 16)
                    elif kind == "exp":
                        branch, h, t = item(n)
                        if branch != "c":
                            act.wait_ge(max_ready, l * 64 + n + 1)
                            act.activation(prob[:, n % 3, 0:(t + 1) * P], prob[:, n % 3, 0:(t + 1) * P], ACT.Exp,
                                           bias=neg_max[:, n % 4:n % 4 + 1], scale=-1.0,
                                           accum_out=row_sum[:, n % 8:n % 8 + 1]).then_inc(prob_ready, 1)
                        else:
                            use = SCORE_USE[("scores", n)]
                            act.wait_ge(score_full, l * SCORE_USES + use + 1)
                            if n < 67:
                                act.wait_ge(turn_full, l * ITEMS + n - 2)
                            else:
                                act.wait_ge(turn_free[(n - 3) % 2], l * (ITEMS // 2) + (n - 3) // 2 + 1 + FREE)
                            if n == 64:
                                act.wait_ge(spare_free, l * SPARE_USES + SPARE_USE[("turn_c", 0)] + 3 + FREE)
                            for s in range(t + 1):
                                last = act.activation(prob[:, n % 3, s * P:(s + 1) * P], ps_s[use % 2][:, s * P:(s + 1) * P],
                                                      ACT.Exp, bias=source_t[:, s, h:h + 1])
                            last.then_inc(prob_ready, 1)
                            act.wait_ge(prob_ready, l * ITEMS + n + 1)
                            act.sem_inc(score_free[use % 2], 1)
                    elif kind == "turn_p":
                        branch, h, t = item(n)
                        if branch != "c":
                            act.wait_ge(turn_full, l * ITEMS + n + 1)
                            if n >= 2:
                                act.wait_ge(out_full, l * ITEMS + n - 1)
                            act.activation(prob_t[:, n % 2, 0:(t + 1) * P], ps_t[n % 2][:, 0:(t + 1) * P], ACT.Copy)\
                               .then_inc(turn_free[n % 2], 1)
                    elif kind == "y_split":
                        act.wait_ge(gated_ready, l * 12 + n + 1)
                        act.activation((ya_hi, yb_hi, yc_hi)[n // BR][:, n % BR, :], gated[:, :], ACT.Copy).then_inc(y_hi_ready, 1)
                    elif step == ("rows", 0):
                        act.wait_ge(neg_abs, l + 1)
                        act.activation(log1p, log1p, ACT.Exp).then_inc(log_ready, 1)
                        act.wait_ge(log_ready, l * 2 + 1)
                        act.activation(log1p, log1p, ACT.Ln, bias=ones[0:CH, 0:1]).then_inc(log_ready, 1)
                    elif kind == "turn_c":
                        act.wait_ge(rows_ready, l + 1)
                        act.activation(decay_r[0:CH, :], decay[:, :], ACT.Copy).then_inc(rows_hi, 1)
                        act.activation(run_max[:, :], run_max[:, :], ACT.Exp, scale=-1.0).then_inc(floor_ready, 1)
                    elif kind == "deviation":
                        act.wait_ge(var_ready, l + 1)
                        act.activation(dev[:, :, :], dev[:, :, :], ACT.Sqrt).then_inc(dev_ready, 1)

                act.wait_ge(y_ready, l * 12 + 12)
                with act.Fori(0, DC // 2) as i:
                    for j in range(2):
                        for b in range(3):
                            act.wait_ge(acc_full, l * UNITS + i * 12 + (PROJ + 6 * j + b + SLOTS + 1))
                            if b == 0:
                                act.wait_ge(mix_f, l * DC + i * 2 + (j + FREE))
                            act.activation(prob[:, b, :], acc[b % 2][:, :], ACT.Tanh,
                                           bias=par_half[:, bass.ds(i * 2 + (C_GATE + DC * b + j), 1)], scale=0.5).then_inc(gate_ready, 1)
                            act.wait_ge(gate_ready, l * 24 + i * 6 + (3 * j + b + 1))
                            act.sem_inc(acc_free[b % 2], 1)
                            high_part(l, (i * 12, i * 3), PROJ + 6 * j + b + 2, DC if b == 0 else BR)
                        high_part(l, (i * 12, i * 3), PROJ + 6 * j + 5, BR)
                        high_part(l, (i * 12, i * 3), PROJ + 6 * j + 6)
                        act.wait_ge(mix_f, l * DC + i * 2 + (j + 1 + FREE))
                        act.activation(merged_hi[:, bass.ds(i * 2 + j, 1), :], gated[:, :].rearrange("p (a n) -> p a n", a=1), ACT.Copy,
                                       scale=0.5).then_inc(mix_hi, 1)
                        high_part(l, (i * 12, i * 3), PROJ + 6 * j + 7)
                act.activation(tok[:, 0:1], ones[:, 0:1], ACT.Sqrt)
                for u in range(U_OUT + 2, UNITS):
                    high_part(l, 0, u)
            act.wait_ge(mean_ready, DEPTH + 1)
            act.activation(tok[:, :], tok[:, :], ACT.Sqrt).then_inc(std_ready, 1)
            for n in range(2 * NT):
                act.wait_ge(post_t, n + 1)
                act.activation(stage[:, n // 2, n % 2 * SEQ:(n % 2 + 1) * SEQ], ps_s[n % 2][:, :], ACT.Copy).then_inc(post_x, 1)

        @block.vector
        def _(dve):
            count = [0]

            def link(ins):
                count[0] += 1
                ins.then_inc(chain, 1)
                dve.wait_ge(chain, base[0] + count[0])

            base = [0]
            dve.wait_ge(ones_ready, 3)
            for c in range(DC):
                dve.wait_ge(pre_x, c + 1)
                if c == 0:
                    link(dve.tensor_tensor(norm[:, :], xT[:, c, :], xT[:, c, :], ALU.mult))
                else:
                    link(dve.tensor_tensor(turn[:, :], xT[:, c, :], xT[:, c, :], ALU.mult))
                    ins = dve.tensor_tensor(norm[:, :], norm[:, :], turn[:, :], ALU.add)
                    link(ins) if c < DC - 1 else ins.then_inc(sq_ready, 1)
            PRE = count[0]
            count[0] = 0

            def norms(n):
                dve.wait_ge(spare_full, n * SPARE_USES + 1)
                dve.tensor_scalar(tok[:, :], spare[:, 0:NT], 1.0 / D, EPS, ALU.mult, ALU.add).then_inc(mean_ready, 1)
                dve.wait_ge(std_ready, n + 1)
                dve.reciprocal(tok[:, :], tok[:, :]).then_inc(tok_ready, 1)
                dve.wait_ge(tok_ready, n + 1)
                dve.tensor_tensor(turn[:, :].rearrange("p (t q) -> p t q", t=NT), ident.unsqueeze(1).broadcast_to([P, NT, P]),
                                  tok[:, :].unsqueeze(2).broadcast_to([P, NT, P]), ALU.mult).then_inc(spread_ready, 1)
                dve.sem_inc(spare_free, 1)
                dve.wait_ge(spare_full, n * SPARE_USES + 2)

            with dve.Fori(0, DEPTH) as l:
                base[0] = l * DVE_STEPS + PRE
                norms(l)
                dve.wait_ge(par_done, l * 3 + 1 + FREE)

                def h_lo_part(c):
                    dve.wait_ge(h_hi_ready, l * DC + c + 1)
                    dve.tensor_tensor(h_lo[:, c, :], pad[:, 0, 3:3 + SEQ], h_hi[:, c, :].bitcast(F32), ALU.subtract).then_inc(h_even, 1)

                for c in range(DC):
                    if c >= 2:
                        dve.wait_ge((h_even, h_odd)[c % 2], l * (DC // 2) + c // 2)
                    dve.scalar_tensor_tensor(pad[:, c % 2, 3:3 + SEQ], xT[:, c, :], par[:, C_NORM + c:C_NORM + c + 1], spare[:, :],
                                             ALU.mult, ALU.mult).then_inc(hf_ready, 1)
                    if c % 2:
                        h_lo_part(c - 1)
                dve.wait_ge(hf_ready, l * DC + DC)
                dve.sem_inc(spare_free, 1)

                for kind, n in SEQUENCE:
                    step = (kind, n)
                    if kind == "unit" and n == U_SMALL:
                        dve.wait_ge(acc_full, l * UNITS + n + (SLOTS + 1))
                        src = acc[n % 2]
                        dve.wait_ge(par_done, l * 3 + 3 + FREE)
                        dve.tensor_scalar(i_row[:, :], src[32:32 + CH, :], par[32:32 + CH, n:n + 1], None, ALU.add)
                        dve.tensor_scalar(f_row[:, :], src[64:64 + CH, :], par[64:64 + CH, n:n + 1],
                                          par[64:64 + CH, C_FBIAS:C_FBIAS + 1], ALU.add, ALU.add)
                        link(dve.tensor_scalar(iw_row[:, :], src[0:IDX_HEADS, :], par[0:IDX_HEADS, n:n + 1],
                                               HD ** -0.5 * IDX_HEADS ** -0.5, ALU.add, ALU.mult))
                        dve.sem_inc(acc_free[n % 2], 1)
                        dve.sem_inc(small_ready, 1)
                    elif kind == "turn_iw":
                        dve.wait_ge(spare_full, l * SPARE_USES + SPARE_USE[step] + 3)
                        link(dve.tensor_copy(iw[:, :, :], spare[:, 0:NT * IDX_HEADS].rearrange("p (t h) -> p t h", t=NT)))
                        dve.sem_inc(spare_free, 1)
                    elif kind == "rope":
                        dve.wait_ge(evac, evacs(l, n))
                        t = (iq[:, n, :] if n < U_IK else ik[:, :] if n == U_IK else ak[:, :] if n == U_AK else aq[:, n - U_AQ, :])
                        swap = [i + 8 if i < 8 else i - 8 if i < 16 else i for i in range(32)]
                        hold(dve, "dve")
                        link(dve.stream_shuffle(turn[:, :], t, swap))
                        link(dve.tensor_tensor(turn[:, :], turn[:, :], sin, ALU.mult))
                        link(dve.tensor_tensor(t, t, cos, ALU.mult))
                        dve.tensor_tensor(t, t, turn[:, :], ALU.add).then_inc(roped, 1)
                        dve.wait_ge(roped, l * ROPES + ROPE[step] + 1)
                    elif kind == "index":
                        t, h = n
                        use = SCORE_USE[step]
                        w = (t + 1) * P
                        dve.wait_ge(score_free[use % 2], l * (SCORE_USES // 2) + use // 2 + 1 + FREE)
                        dst = score[:, t % 2, 0:w]
                        if h == 0:
                            dve.tensor_scalar(dst, prob[:, h % 2, 0:w], iw[:, t, h:h + 1], None, ALU.mult).then_inc(score_part, 1)
                        else:
                            dve.scalar_tensor_tensor(dst, prob[:, h % 2, 0:w], iw[:, t, h:h + 1], dst, ALU.mult, ALU.add)\
                               .then_inc(score_part, 1)
                        dve.wait_ge(score_part, l * 12 + (t - 1) * 4 + h + 1)
                        if h == IDX_HEADS - 1:
                            link(dve.memset(score[0:P // 2, t % 2, w - P // 2:w], INADMISSIBLE))
                    elif kind == "topk":
                        t, a, b = n
                        s = score[:, t % 2, 0:(t + 1) * P]
                        for _ in range(a, b):
                            hold(dve, "dve")
                            link(dve.max(top8[:, :], s))
                            hold(dve, "dve")
                            link(dve.match_replace(s, top8[:, :], s, TAKEN))
                        if b == TOPK // 8:
                            link(dve.tensor_scalar(key_mask[:, MASK_AT[t]:MASK_AT[t] + (t + 1) * P], s,
                                                   0.5 * (TAKEN + INADMISSIBLE), NEG, ALU.is_gt, ALU.mult))
                    elif kind == "conv":
                        dve.wait_ge(evac, evacs(l, U_CQ + n))
                        x = pad[:, n % 2, :]
                        for tap in (3, 2, 1, 0):
                            w = par[:, C_CONVW + tap * 8 + n:C_CONVW + tap * 8 + n + 1]
                            if tap == 3:
                                link(dve.tensor_scalar(turn[:, :], x[:, tap:tap + SEQ], w, par[:, C_CONVB + n:C_CONVB + n + 1],
                                                       ALU.mult, ALU.add))
                            else:
                                ins = dve.scalar_tensor_tensor(turn[:, :], x[:, tap:tap + SEQ], w, turn[:, :], ALU.mult, ALU.add)
                                link(ins) if tap else ins.then_inc(conv_sum, 1)
                    elif kind == "conv_gate":
                        dve.wait_ge(conv_tanh, l * 8 + n + 1)
                        dst = cq[:, n, :] if n < CH else ck[:, n - CH, :]
                        dve.scalar_tensor_tensor(dst, z_tanh[:, :], 1.0, turn[:, :], ALU.add, ALU.mult).then_inc(conv_done, 1)
                        dve.wait_ge(conv_done, l * 8 + n + 1)
                    elif kind == "rel_bias":
                        dve.wait_ge(rel_in_s[n % 2], l * 64 + 16 * (n // 2 + 1))
                        link(dve.memset(rel[0:P // 2, n % 2, SEQ - P // 2:SEQ], NEG))
                    elif kind == "scores":
                        branch, h, t = item(n)
                        use = SCORE_USE[step]
                        w = (t + 1) * P
                        if branch != "c":
                            dve.wait_ge(score_full, l * SCORE_USES + use + 1)
                            if n >= 3:
                                dve.wait_ge(turn_full, l * ITEMS + n - 2)
                            if branch == "b":
                                mask = rel[:, h % 2, SEQ - w:SEQ]
                            else:
                                mask = key_mask[:, MASK_AT[t]:MASK_AT[t] + w] if t else consts[:, K_CHUNK:K_CHUNK + P]
                            hold(dve, "dve")
                            dve.tensor_tensor_reduce(out=prob[:, n % 3, 0:w], in0=ps_s[use % 2][:, 0:w], in1=mask, scale=-1.0,
                                                     scalar=3.0e38, op0=ALU.add, op1=ALU.min,
                                                     accum_out=neg_max[:, n % 4:n % 4 + 1]).then_inc(max_ready, 1)
                            dve.wait_ge(max_ready, l * 64 + n + 1)
                            dve.sem_inc(score_free[use % 2], 1)
                    elif kind == "turn_p":
                        branch, h, t = item(n)
                        if branch == "c":
                            dve.wait_ge(turn_full, l * ITEMS + n + 1)
                            dve.wait_ge(prob_ready, l * ITEMS + n + 1)
                            dve.wait_ge(out_full, l * ITEMS + n - 1)
                            w = (t + 1) * P
                            dve.scalar_tensor_tensor(prob_t[:, n % 2, 0:w], ps_t[n % 2][:, 0:w], 0.25 * P ** -0.5, prob[:, n % 3, 0:w],
                                                     ALU.mult, ALU.mult).then_inc(turn_free[n % 2], 1)
                    elif kind == "values":
                        branch, h, t = item(n)
                        dve.wait_ge(out_full, l * ITEMS + n + 1)
                        g, place, size = group(n)
                        if place < size - 1:
                            continue
                        dve.wait_ge(out_free, l * GROUPS + g + FREE)
                        if branch != "c":
                            o = n % 8 - 3
                            link(dve.reciprocal(row_inv[:, :], row_sum[:, o:o + 4]))
                            dst = (att["a"][:, t, (h - 3) * HD:(h + 1) * HD].rearrange("p (g d) -> p g d", g=4) if branch == "a"
                                   else att["b"][:, :, h * HD:(h + 1) * HD])
                            dve.tensor_tensor(dst, ps_o[:, 0:4 * HD].rearrange("p (g d) -> p g d", g=4),
                                              row_inv[:, :].unsqueeze(2).broadcast_to([P, 4, HD]), ALU.mult).then_inc(out_free, 1)
                        else:
                            pair = ps_o[:, :].rearrange("p (g c) -> p g c", g=2)
                            inv = row_inv[:, 0:2].unsqueeze(2)
                            link(dve.scalar_tensor_tensor(inv, pair[:, :, P:P + 1], -1.0, floor_t[:, t - 1:t + 1, h:h + 1],
                                                          ALU.mult, ALU.max))
                            link(dve.tensor_tensor(inv, inv, pair[:, :, P:P + 1], ALU.max))
                            link(dve.reciprocal(inv, inv))
                            dve.tensor_tensor(att["c"][:, t - 1:t + 1, h * P:(h + 1) * P], pair[:, :, 0:P],
                                              inv.broadcast_to([P, 2, P]), ALU.mult).then_inc(out_free, 1)
                    elif kind in ("z_a", "z_b", "z_c"):
                        zn = "abc".index(kind[2]) * BR + n
                        tanh, zt = (z_tanh[:, :], z[:, :]) if zn < 8 or zn % 2 == 0 else (prob[:, 0, :], prob[:, 1, :])
                        dve.wait_ge(z_ready, l * 12 + zn + 1)
                        link(dve.scalar_tensor_tensor(zt, tanh, 1.0, zt, ALU.add, ALU.mult))
                        half = par_half[:, C_CNORM + n:C_CNORM + n + 1] if kind == "z_c" else 0.5
                        dve.wait_ge(spare_full, l * SPARE_USES + SPARE_USE[step] + 3)
                        dve.scalar_tensor_tensor(gated[:, :], zt, half, spare[:, :], ALU.mult, ALU.mult).then_inc(gated_ready, 1)
                        dve.wait_ge(gated_ready, l * 12 + zn + 1)
                        dve.sem_inc(spare_free, 1)
                    elif kind == "y_split":
                        dve.wait_ge(y_hi_ready, l * 12 + n + 1)
                        dve.tensor_tensor((ya_lo, yb_lo, yc_lo)[n // BR][:, n % BR, :], gated[:, :],
                                          (ya_hi, yb_hi, yc_hi)[n // BR][:, n % BR, :].bitcast(F32), ALU.subtract).then_inc(y_ready, 1)
                        dve.wait_ge(y_ready, l * 12 + n + 1)
                    elif step == ("rows", 0):
                        dve.scalar_tensor_tensor(log1p, f_row[:, :], -1.0, f_row[:, :], ALU.mult, ALU.min).then_inc(neg_abs, 1)
                    elif step == ("rows", 1):
                        dve.wait_ge(log_ready, l * 2 + 2)
                        link(dve.scalar_tensor_tensor(f_row[:, :], f_row[:, :], 0.0, log1p, ALU.min, ALU.subtract))
                        link(dve.tensor_tensor_scan(run_max[:, :], f_row[:, :], i_row[:, :], 0.0, ALU.add, ALU.max))
                    elif kind == "rows":
                        s = n - 2
                        w = SEQ - s * P
                        link(dve.tensor_tensor_scan(decay[:, SUM_AT[s]:SUM_AT[s] + w], ones[0:CH, 0:w], f_row[:, s * P:SEQ], 0.0,
                                                    ALU.mult, ALU.add))
                        link(dve.tensor_tensor(source[:, s * P:(s + 1) * P], i_row[:, s * P:(s + 1) * P],
                                               decay[:, SUM_AT[s]:SUM_AT[s] + P], ALU.subtract))
                        link(dve.tensor_tensor(decay[:, SUM_AT[s]:SUM_AT[s] + w], decay[:, SUM_AT[s]:SUM_AT[s] + w],
                                               run_max[:, s * P:SEQ], ALU.subtract))
                        if s == NT - 1:
                            dve.sem_inc(rows_ready, 1)
                            dve.memset(cv[:, :, :, P:P + 1], 1.0).then_inc(ones_col, 1)
                    elif kind == "turn_c":
                        dve.wait_ge(spare_full, l * SPARE_USES + SPARE_USE[step] + 3)
                        link(dve.tensor_copy(source_t[:, :, :], spare[:, 0:NT * CH].rearrange("p (t h) -> p t h", t=NT)))
                        link(dve.tensor_copy(floor_t[:, :, :], spare[:, NT * CH:2 * NT * CH].rearrange("p (t h) -> p t h", t=NT)))
                        dve.sem_inc(spare_free, 1)
                        dve.wait_ge(rows_hi, l + 1)
                        dve.tensor_tensor(decay_r[32:32 + CH, :], decay[:, :], decay_r[0:CH, :].bitcast(F32), ALU.subtract)\
                           .then_inc(decay_ready, 1)
                    elif kind == "out_gate":
                        dve.wait_ge(spare_full, l * SPARE_USES + SPARE_USE[step] + 3)
                        y = att["c"][:, :, n * P:(n + 1) * P]
                        dve.scalar_tensor_tensor(y, spare[:, :].rearrange("p (t q) -> p t q", t=NT), 1.0, y, ALU.add, ALU.mult)\
                           .then_inc(og_used, 1)
                        dve.wait_ge(og_used, l * CH + n + 1)
                        dve.sem_inc(spare_free, 1)
                        for t in range(NT):
                            link(dve.bn_stats(stats[:, t, :], y[:, t, :]))
                            hold(dve, "dve")
                            link(dve.bn_aggr(moments[:, t, n, :], stats[:, t, :]))
                    elif kind == "deviation":
                        dve.tensor_scalar(dev[:, :, :], moments[:, :, :, 1], 4.0 * EPS, None, ALU.add).then_inc(var_ready, 1)
                        dve.wait_ge(dev_ready, l + 1)
                        link(dve.reciprocal(dev[:, :, :], dev[:, :, :]))
                        for t in range(NT):
                            for h in range(CH):
                                y = att["c"][:, t, h * P:(h + 1) * P]
                                last = dve.tensor_scalar(y, y, moments[:, t, h, 0:1], dev[:, t, h:h + 1], ALU.subtract, ALU.mult)
                        last.then_inc(normed, 1)
                assert count[0] == DVE_STEPS, count[0]
                hold(dve, "dve")

                with dve.Fori(0, DC) as j:
                    for b in range(3):
                        dve.wait_ge(acc_full, l * UNITS + j * 6 + (PROJ + 3 + b + SLOTS + 1))
                        dve.wait_ge(gate_ready, l * 24 + j * 3 + (b + 1))
                        if b == 0:
                            dve.wait_ge(mix_ready, l * DC + j + FREE)
                        dve.scalar_tensor_tensor((gated, z, z)[b][:, :], prob[:, b, :], 1.0, acc[(3 + b) % 2][:, :], ALU.add, ALU.mult)\
                           .then_inc(chain_mix, 1)
                        dve.wait_ge(chain_mix, l * (4 * DC) + j * 4 + ((1, 2, 4)[b]))
                        dve.sem_inc(acc_free[(3 + b) % 2], 1)
                        if b == 1:
                            dve.tensor_tensor(gated[:, :], gated[:, :], z[:, :], ALU.add).then_inc(chain_mix, 1)
                            dve.wait_ge(chain_mix, l * (4 * DC) + j * 4 + 3)
                    dve.tensor_tensor(gated[:, :], gated[:, :], z[:, :], ALU.add).then_inc(mix_f, 1)
                    dve.wait_ge(mix_hi, l * DC + j + 1)
                    dve.scalar_tensor_tensor(merged_lo[:, bass.ds(j, 1), :], gated[:, :].rearrange("p (a n) -> p a n", a=1), 0.5,
                                             merged_hi[:, bass.ds(j, 1), :].bitcast(F32), ALU.mult, ALU.subtract).then_inc(mix_ready, 1)

                dve.memset(norm[:, :], 0.0).then_inc(chain_out, 1)
                dve.wait_ge(chain_out, l * (3 * DC + 1) + 1)
                hold(dve, "dve")
                with dve.Fori(0, DC // 2) as i:
                    for b in range(2):
                        xc = xT[:, bass.ds(i * 2 + b, 1), :]
                        dve.wait_ge(acc_full, l * UNITS + i * 2 + (U_OUT + b + SLOTS + 1))
                        dve.tensor_tensor(xc, xc, acc[b][:, :].rearrange("p (a n) -> p a n", a=1), ALU.add).then_inc(chain_out, 1)
                        dve.wait_ge(chain_out, l * (3 * DC + 1) + i * 6 + (3 * b + 2))
                        dve.sem_inc(acc_free[b], 1)
                        dve.tensor_tensor(turn[:, :].rearrange("p (a n) -> p a n", a=1), xc, xc, ALU.mult).then_inc(chain_out, 1)
                        dve.wait_ge(chain_out, l * (3 * DC + 1) + i * 6 + (3 * b + 3))
                        dve.tensor_tensor(norm[:, :], norm[:, :], turn[:, :], ALU.add).then_inc(chain_out, 1)
                        dve.wait_ge(chain_out, l * (3 * DC + 1) + i * 6 + (3 * b + 4))
                dve.sem_inc(sq_ready, 1)
            norms(DEPTH)
            for c in range(DC):
                dve.scalar_tensor_tensor(xT[:, c, :], xT[:, c, :], final_g[:, c:c + 1], spare[:, :], ALU.mult, ALU.mult).then_inc(post_f, 1)


def kernel(**inputs):
    import numpy as np
    import concourse.bacc as bacc
    from concourse.bass_utils import run_bass_kernel_spmd

    a = {k: np.ascontiguousarray(v) for k, v in inputs.items()}
    f32 = a["x"].dtype
    w, b = a["w_in"], a["b_in"]
    half = np.arange(HD)

    def cols(start):
        return np.arange(start, start + P)

    offs = {"aq": 0, "ak": 512, "av": 640, "iq": 768, "ik": 1024, "iw": 1088, "az": 1092, "bq": 1604, "bk": 2116, "bv": 2628,
            "bz": 3140, "cq": 3652, "ck": 4164, "cv": 4676, "ci": 5188, "cf": 5192, "co": 5196, "cz": 5708, "gates": 6220}
    small = np.full(P, -1)
    for at_, name in ((0, "iw"), (32, "ci"), (64, "cf")):
        small[at_:at_ + 4] = offs[name] + np.arange(4)
    units = [cols(offs["iq"]), cols(offs["iq"] + P), np.concatenate([offs["ik"] + half] * 2), small, cols(offs["ak"]), cols(offs["av"])]
    units += [np.concatenate([offs["aq"] + j * HD + half, offs["aq"] + (j + 4) * HD + half]) for j in range(4)]
    for name in ("bq", "bk", "bv", "cq", "ck", "cv", "az", "bz", "co", "cz"):
        units += [cols(offs[name] + j * P) for j in range(4)]
    gate_units = [cols(offs["gates"] + n * D + j * P) for j in range(DC) for n in range(3)]

    def take(m, c):
        padded = np.concatenate([m, np.zeros(m.shape[:-1] + (1,), f32)], axis=-1)
        return padded[..., c]

    def unit(m, c):
        t = take(m, c)
        return t.reshape(DEPTH, -1, P, P).transpose(0, 2, 1, 3).reshape(DEPTH, P, -1)

    wo_units = [unit(a["w_out"], cols(j * P)) for j in range(DC)]
    w_full = np.stack([unit(w, c) for c in units + gate_units] + wo_units, axis=1).reshape(-1, P, D)
    wb = a["w_branch"]
    w_mix = np.stack([unit(wb[:, n], cols(j * P)) for j in range(DC) for n in range(3)], axis=1).reshape(-1, P, BR * P)

    def chunks(m):
        return m.reshape(DEPTH, -1, P).transpose(0, 2, 1)

    fcol = np.zeros((DEPTH, P, 2), f32)
    fcol[:, 64:68, 0] = a["f_bias"]
    params = np.concatenate([np.stack([take(b, c) for c in units], axis=2), chunks(b[:, offs["gates"]:]), chunks(a["norm_g"]),
                             chunks(a["conv_b"]), chunks(a["conv_w"].reshape(DEPTH, -1)), chunks(a["c_norm_w"]), fcol], axis=2)
    dist = np.clip(SEQ - P + np.arange(P)[:, None] - np.arange(SEQ)[None, :], -128, 128) + 128
    rel = a["rel_bias"][:, :, dist].reshape(-1, P, SEQ)

    consts = np.zeros((P, KCOLS), f32)
    consts[:, K_ID:K_ID + P] = np.eye(P)
    p, q = np.arange(P)[:, None], np.arange(P)[None, :]
    consts[:, K_CHUNK:K_CHUNK + P] = np.where(q // 64 <= p // 64, 0.0, NEG)
    consts[:, K_CAUSAL:K_CAUSAL + P] = np.where(p <= q, 0.0, NEG)
    inv = (1.0 / (np.float32(500000.0) ** (np.arange(8, dtype=f32) * np.float32(2.0) / np.float32(16)))).astype(f32)
    ang = np.arange(SEQ, dtype=f32)[None, :] * inv[:, None]
    for s in (0, 64):
        consts[s:s + 64, K_COS:K_COS + SEQ] = 1.0
        for r, sign in ((0, -1.0), (8, 1.0)):
            consts[s + r:s + r + 8, K_COS:K_COS + SEQ] = np.cos(ang)
            consts[s + r:s + r + 8, K_SIN:K_SIN + SEQ] = sign * np.sin(ang)
    for h in range(CH):
        for r in (0, 32):
            consts[r + h, K_SEL + h * P:K_SEL + (h + 1) * P] = 1.0

    arrays = {"x": a["x"].reshape(SEQ, D), "w_full": w_full, "w_mix": w_mix, "params": params, "rel": rel,
              "final_g": a["final_g"].reshape(DC, P).T, "consts": consts}
    arrays = {k: np.ascontiguousarray(v) for k, v in arrays.items()}
    nc = bacc.Bacc("TRN2", target_bir_lowering=False, num_devices=1, dynamic_dma_scratch_size=1024)
    args = [nc.dram_tensor(k, v.shape, mybir.dt.from_np(v.dtype), kind="ExternalInput").ap() for k, v in arrays.items()]
    out = nc.dram_tensor("out", (SEQ, D), F32, kind="ExternalOutput").ap()
    build(nc, *args, out)
    got = run_bass_kernel_spmd(nc, [arrays], core_ids=[0])
    return got.results[0]["out"].reshape(1, SEQ, D)
```

```python
from contextlib import ExitStack

import concourse.bass as bass
from concourse import mybir

F32 = mybir.dt.float32
F32R = mybir.dt.float32r
BF16 = mybir.dt.bfloat16
ALU = mybir.AluOpType
ACT = mybir.ActivationFunctionType

P = 128
DEPTH, SEQ, D = 2, 512, 1024
NT = SEQ // P
DC = D // P
HEADS, HD = 8, 64
IDX_HEADS = 4
TOPK = 128
CH = 4
BR = 4
EPS = 1e-6
NEG = -1.0e30
INADMISSIBLE = -1.0e38
TAKEN = -3.0e38

U_IQ, U_IK, U_SMALL, U_AK, U_AV, U_AQ = 0, 2, 3, 4, 5, 6
U_BQ, U_BK, U_BV, U_CQ, U_CK, U_CV, U_AZ, U_BZ, U_CO, U_CZ = 10, 14, 18, 22, 26, 30, 34, 38, 42, 46
PROJ = 50
MIX = DC * 6
UNITS = PROJ + MIX + DC
U_OUT = PROJ + MIX
PASSES = 3 * DC
XG_UNITS = 3
FREE = 1
SLOTS = 2
RAW = 4
RAW_USES = [(UNITS - s + RAW - 1) // RAW for s in range(RAW)]
C_GATE, C_NORM, C_CONVB, C_CONVW, C_CNORM, C_FBIAS, PCOLS = PROJ, 74, 82, 90, 122, 126, 128
K_ID, K_CHUNK, K_CAUSAL, K_COS, K_SIN, K_SEL, KCOLS = 0, 128, 256, 384, 896, 1408, 1920


INDEX_AT = {12: 2, 14: 3}
CUT = ("cut", None)


ROUNDS = {7: 4, 8: 4, 9: 4, 10: 4, 11: 0, 12: 2, 13: 2, 14: 2, 15: 2, 16: 2}


def schedule():
    seq = []
    flying = []

    def push(n):
        seq.append(CUT)
        if n is not None:
            seq.append(("scores", n))
        flying.append(n)
        mlstm = any(m is not None and m >= 64 for m in flying[-4:])
        for back, kind in ((1, "exp"), (2, "turn_p"), (3, "values")) if mlstm else ((2, "exp"), (3, "turn_p"), (4, "values")):
            if len(flying) >= back and flying[-back] is not None:
                seq.append((kind, flying[-back]))

    def flush():
        for _ in range(3):
            push(None)
        flying.clear()

    def units(a, b):
        seq.extend(("unit", u) for u in range(a, b))

    def index(t):
        for h in range(IDX_HEADS):
            seq.extend((CUT, ("index", (t, h))))

    def topk(t, a=0, b=TOPK // 8):
        seq.append(("topk", (t, a, b)))

    seq.extend((("passes", (0, 0, 2 * DC - 2)), ("norm_sum", 0), ("passes", (0, 2 * DC - 2, PASSES)), ("unit", 0)))
    seq.extend((("passes", (1, 0, 2)), ("norm_spread", 0), ("passes", (1, 2, PASSES))))
    seq.extend(("h", c) for c in range(6))
    seq.append(("unit", 1))
    seq.extend(("h", c) for c in range(6, DC))
    seq.extend((("passes", (2, 0, PASSES)), ("unit", 2)))
    seq.extend((("passes", (3, 0, PASSES)), ("unit", 3)))
    seq.extend(("rope", u) for u in range(XG_UNITS))
    units(4, 7)
    seq.append(("turn_iw", 0))
    seq.append(("rope", U_AK))
    index(1)
    work = [("topk", (t, r, r + 1)) for t in (1, 2, 3) for r in range(TOPK // 8)]
    for u in range(7, 17):
        units(u, u + 1)
        if u == U_AV + 2:
            seq.append(("turn_v", U_AV))
        if U_AQ <= u - 2 < U_BQ:
            seq.append(("rope", u - 2))
        if u in INDEX_AT:
            index(INDEX_AT[u])
        for half in range(2):
            seq.append(CUT)
            for _ in range(ROUNDS[u] // 2):
                seq.append(work.pop(0))
    seq.append(("rel_bias", 0))
    seq.append(("rel_bias", 1))
    first = 17
    n, soon, late, rows = 0, [], [], -1
    for u in range(first, 38):
        units(u, u + 1)
        upto = -(-64 * (u + 1 - first) // (38 - first))
        k = 0
        while n < upto:
            push(n)
            if work:
                seq.append(work.pop(0))
            if n == 31:
                rows = 0
            if n >= 32 and n % NT == NT - 1 and (n - 32) // NT + 2 < HEADS:
                seq.append(("rel_bias", (n - 32) // NT + 2))
            n += 1
            if k == 0:
                seq.extend(soon)
                soon = []
            if k == 1:
                seq.extend(late)
                late = []
                if rows == 6:
                    seq.append(("row_parts", 0))
                    rows += 1
                if u == U_AZ + 1:
                    seq.append(("turn_c", 0))
            k += 1
        if 0 <= rows < 6:
            seq.append(("rows", rows))
            rows += 1
        if U_BV <= u < U_CQ or U_CV <= u < U_AZ:
            late.append(("turn_v", u))
        if U_CQ <= u < U_CV:
            seq.append(("conv", (u - U_CQ, 0)))
            soon.append(("conv", (u - U_CQ, 1)))
            late.append(("conv_gate", u - U_CQ))
        if U_AZ <= u:
            seq.extend((CUT, ("z_a", u - U_AZ)))
            late.append(("y_split", u - U_AZ))
    assert rows == 7 and not work
    flush()
    assert n == 64
    for u in range(38, 42):
        units(u, u + 1)
        for k in range(NT):
            push(n)
            n += 1
            if k == 2:
                seq.extend(late)
                late = []
        seq.extend((CUT, ("z_b", u - U_BZ)))
        late.append(("y_split", u - U_BZ + BR))
    flush()
    units(42, 43)
    seq.extend(late)
    for u in range(43, 46):
        units(u, u + 1)
        seq.extend((CUT, ("out_gate", u - 43)))
    seq.extend((CUT, ("out_gate", 3)))
    units(46, 47)
    seq.append(("deviation", 0))
    units(47, 48)
    seq.extend((("z_c", 0), ("y_split", 8)))
    units(48, 49)
    for n in (1, 2):
        seq.extend((CUT, ("z_c", n), ("y_split", 8 + n)))
    units(49, 50)
    seq.extend((("z_c", 3), ("y_split", 11)))
    return interleave(seq)


def interleave(steps):
    seq, groups = [], [[]]
    for step in steps:
        if step == CUT:
            groups.append([])
        elif step[0] == "unit" and step[1] <= XG_UNITS:
            seq.extend(groups[0] + [step])
            groups = [[]]
        elif step[0] == "unit":
            groups = [g for g in groups if g]
            at = 0
            for i, g in enumerate(groups):
                to = (i + 1) * PASSES // (len(groups) + 1)
                if to > at:
                    seq.append(("passes", (step[1], at, to)))
                    at = to
                seq.extend(g)
            seq.append(("passes", (step[1], at, PASSES)))
            seq.append(step)
            groups = [[]]
        else:
            groups[-1].append(step)
    return seq + [step for g in groups for step in g]


SEQUENCE = schedule()


def order(*kinds):
    steps = [s for s in SEQUENCE if s[0] in kinds]
    return {s: n for n, s in enumerate(steps)}, len(steps)


SCORE_USE, SCORE_USES = order("index", "scores")
SPARE_USE, SPARE_USES = order("turn_iw", "turn_v", "z_a", "z_b", "z_c", "turn_c", "out_gate")
SPARE_USES += 2
ITEMS = 80
GROUPS = 24
ROPE, ROPES = order("rope")
DVE_STEPS = 267


def item(n):
    if n < 32:
        return "a", n % HEADS, n // HEADS
    if n < 64:
        return "b", (n - 32) // NT, n % NT
    return "c", (n - 64) // NT, n % NT


def group(n):
    return (n // 4, n % 4, 4) if n < 64 else (n // 2 - 16, n % 2, 2)


def evacs(l, n):
    return l * (PROJ - 1) + (n + 1 if n < U_SMALL else n)


def build(nc, x_in, w_full, w_mix, params_in, rel_in, gains_in, consts_in, out):
    ctx = ExitStack()
    with ctx:
        cursor = [(nc.sbuf_base + 63) // 64 * 64]

        def at(name, shape, dt, offset):
            return nc.alloc_sbuf_tensor_at(name, shape, dt, offset=offset)

        def region(size):
            a = cursor[0]
            cursor[0] += (size + 31) // 32 * 32
            assert cursor[0] <= nc.sbuf_usable_end, cursor[0]
            return a

        def sb(name, shape, dt=F32):
            size = mybir.dt.size(dt)
            for s in shape[1:]:
                size *= s
            return at(name, shape, dt, region(size))

        ROW = SEQ * 4
        xT = sb("xT", [P, DC, SEQ])
        h_hi = sb("h_hi", [P, DC, SEQ], F32R)
        h_lo = sb("h_lo", [P, DC, SEQ], F32R)
        w_raw = sb("w_raw", [P, RAW, DC, P])
        w_hi = sb("w_hi", [P, SLOTS, DC, P], F32R)
        w_lo = sb("w_lo", [P, SLOTS, DC, P], F32R)
        r1 = region(9 * ROW)
        aq = at("aq", [P, BR, SEQ], F32, r1)
        ak = at("ak", [P, SEQ], F32, r1 + 4 * ROW)
        av = at("av", [P, NT, P], F32, r1 + 5 * ROW)
        iq = at("iq", [P, 2, SEQ], F32, r1 + 6 * ROW)
        ik = at("ik", [P, SEQ], F32, r1 + 8 * ROW)
        ya_hi = at("ya_hi", [P, BR, SEQ], F32R, r1)
        ya_lo = at("ya_lo", [P, BR, SEQ], F32R, r1 + 4 * ROW)
        r2 = region(24 * ROW + 64)
        bq = at("bq", [P, BR, SEQ], F32, r2)
        bk = at("bk", [P, BR, SEQ], F32, r2 + 4 * ROW)
        bv = at("bv", [P, NT, BR * P], F32, r2 + 8 * ROW)
        yb_hi = at("yb_hi", [P, BR, SEQ], F32R, r2)
        yb_lo = at("yb_lo", [P, BR, SEQ], F32R, r2 + 4 * ROW)
        r3 = r2 + 12 * ROW
        cv = at("cv", [P, NT, CH, P + 1], F32, r3)
        cq = at("cq", [P, CH, SEQ], F32, r3 + 4 * ROW + 64)
        ck = at("ck", [P, CH, SEQ], F32, r3 + 8 * ROW + 64)
        yc_hi = at("yc_hi", [P, BR, SEQ], F32R, r3 + 4 * ROW + 64)
        yc_lo = at("yc_lo", [P, BR, SEQ], F32R, r3 + 8 * ROW + 64)
        xg_hi = at("xg_hi", [P, DC, SEQ], F32R, r2)
        xg_lo = at("xg_lo", [P, DC, SEQ], F32R, r2 + 16 * ROW + 64)
        merged_lo = at("merged_lo", [P, DC, SEQ], F32R, r2 + 8 * ROW)
        r4 = region(8 * ROW)
        att = {"a": at("att_a", [P, NT, HEADS * HD], F32, r4), "b": at("att_b", [P, NT, HEADS * HD], F32, r4 + 4 * ROW)}
        att["c"] = at("att_c", [P, NT, CH * P], F32, r4)
        merged_hi = at("merged_hi", [P, DC, SEQ], F32R, r4)
        stage = at("stage", [P, NT, D], F32, r4)
        MASK_AT = {1: 0, 2: 256, 3: 640}
        r5 = region(1152 * 4 + 4 * ROW)
        key_mask = at("key_mask", [P, 1152], F32, r5)
        score = at("score", [P, 2, SEQ], F32, r5 + 1152 * 4)
        rel = at("rel", [P, 2, SEQ], F32, r5 + 1152 * 4 + 2 * ROW)
        SUM_AT = [0, 512, 896, 1152]
        decay = at("decay", [CH, 1280], F32, r5)
        run_max = at("run_max", [CH, SEQ], F32, r5 + 1280 * 4)
        assert 1280 * 4 + ROW <= 1152 * 4 + 2 * ROW

        consts = sb("consts", [P, KCOLS])
        ones = sb("ones", [P, SEQ])
        ident_b = sb("ident_b", [P, P], BF16)
        causal_b = sb("causal_b", [P, P], BF16)
        par_next = sb("par_next", [P, PCOLS])
        par = sb("par", [P, PCOLS])
        par_half = sb("par_half", [P, PCOLS])
        par_eighth = sb("par_eighth", [P, PCOLS])
        gains = sb("gains", [P, (DEPTH + 1) * DC])
        prob = sb("prob", [P, 3, SEQ])
        prob_t = sb("prob_t", [P, 2, SEQ])
        turn = sb("turn", [P, SEQ])
        norm = sb("norm", [P, SEQ])
        log1p = source = norm[0:CH, :]
        sel_r = sb("sel_r", [36, CH * P], F32R)
        decay_r = sb("decay_r", [36, 1280], F32R)
        pad = sb("pad", [P, 2, SEQ + 4])
        z_tanh = sb("z_tanh", [P, SEQ])
        z = sb("z", [P, SEQ])
        iw_row = at("iw_row", [IDX_HEADS, SEQ], F32, cursor[0] - ROW)
        gated = sb("gated", [P, SEQ])
        i_row = sb("i_row", [CH, SEQ])
        f_row = sb("f_row", [CH, SEQ])
        top8 = sb("top8", [P, 8])
        iw = sb("iw", [P, NT, IDX_HEADS])
        source_t = sb("source_t", [P, NT, CH])
        neg_max = sb("neg_max", [P, 4])
        row_sum = sb("row_sum", [P, 8])
        row_inv = sb("row_inv", [P, 4])
        floor_t = sb("floor_t", [P, NT, CH])
        tok = sb("tok", [P, NT])
        stats = sb("stats", [P, NT, 6])
        moments = sb("moments", [P, NT, CH, 2])
        dev = sb("dev", [P, NT, CH])

        ident = consts[:, K_ID:K_ID + P]
        cos, sin = consts[:, K_COS:K_COS + SEQ], consts[:, K_SIN:K_SIN + SEQ]

        def psum(name):
            return ctx.enter_context(nc.psum_tensor(name, [P, SEQ], F32))

        acc = [psum("acc0"), psum("acc1")]
        ps_s = [psum("ps_s0"), psum("ps_s1")]
        ps_t = [psum("ps_t0"), psum("ps_t1")]
        ps_o = psum("ps_o")
        spare = psum("spare")

        def sem(name):
            return ctx.enter_context(nc.semaphore(name))

        consts_in_s, params_in_s, rel_in_s, x_in_s, out_s = (
            [sem("ident_loaded"), sem("consts_loaded"), sem("gains_loaded")], sem("params_loaded"),
            [sem("rel_loaded0"), sem("rel_loaded1")], [sem(f"x_loaded{c}") for c in range(0, DC, 2)], sem("out_stored"))
        raw_full = [sem(f"raw_full{s}") for s in range(RAW)]
        w_hi_done, split_full, acc_full = sem("w_hi_done"), sem("split_full"), sem("acc_full")
        acc_free = [sem("acc_free0"), sem("acc_free1")]
        const_ready, ones_ready, par_done = sem("const_ready"), sem("ones_ready"), sem("par_done")
        sq_ready, mean_ready, std_ready = sem("sq_ready"), sem("mean_ready"), sem("std_ready")
        hf_ready, h_hi_ready, h_even, h_odd = sem("hf_ready"), sem("h_hi_ready"), sem("h_even"), sem("h_odd")
        tok_ready, spread_ready = sem("tok_ready"), sem("spread_ready")
        spare_full, spare_free = sem("spare_full"), sem("spare_free")
        evac, roped, conv_sum, conv_tanh, conv_done = (
            sem("evac"), sem("roped"), sem("conv_sum"), sem("conv_tanh"), sem("conv_done"))
        small_ready, score_part = sem("small_ready"), sem("score_part")
        score_full, score_free = sem("score_full"), [sem("score_free0"), sem("score_free1")]
        max_ready, prob_ready = sem("max_ready"), sem("prob_ready")
        turn_full, turn_free = sem("turn_full"), [sem("turn_free0"), sem("turn_free1")]
        out_full, out_free = sem("out_full"), sem("out_free")
        z_ready, gated_ready, y_hi_ready, y_ready = sem("z_ready"), sem("gated_ready"), sem("y_hi_ready"), sem("y_ready")
        neg_abs, log_ready, rows_ready, rows_hi = sem("neg_abs"), sem("log_ready"), sem("rows_ready"), sem("rows_hi")
        decay_ready, floor_ready, ones_col = sem("decay_ready"), sem("floor_ready"), sem("ones_col")
        og_used, var_ready, dev_ready, normed = sem("og_used"), sem("var_ready"), sem("dev_ready"), sem("normed")
        gate_ready, mix_f, mix_hi, mix_ready = sem("gate_ready"), sem("mix_f"), sem("mix_hi"), sem("mix_ready")
        x_step, xg_hi_done, xg_ready = sem("x_step"), sem("xg_hi_done"), sem("xg_ready")
        pre_t = sem("pre_t")
        post_t = sem("post_t")
        post_f, post_x = [sem("post_f0"), sem("post_f1")], [sem("post_x0"), sem("post_x1")]
        chain, chain_mix, chain_out = sem("chain"), sem("chain_mix"), sem("chain_out")
        held = {"pe": sem("pe_held"), "dve": sem("dve_held"), "pool": sem("pool_held")}

        def hold(eng, name):
            eng.sem_inc(held[name], 1)

        block = ctx.enter_context(nc.Block())

        @block.sync
        def _(sp):
            sp.dma_start(ident, consts_in[:, K_ID:K_ID + P]).then_inc(consts_in_s[0], 16)
            for c in range(0, DC, 2):
                sp.dma_start(stage[:, :, c * P:(c + 2) * P], x_in[:, c * P:(c + 2) * P].rearrange("(t p) d -> p t d", p=P))\
                    .then_inc(x_in_s[c // 2], 16)
                if c == 0:
                    sp.dma_start(gains[:], gains_in).then_inc(consts_in_s[2], 16)

            def load(l, u, slot, source, nk, back=RAW):
                sp.wait_ge(split_full, l * UNITS + u + (RAW + 1 - back))
                sp.dma_start(w_raw[:, slot, 0:nk, :], source).then_inc(raw_full[slot], 16)

            def full(n):
                return w_full[bass.ds(n, 1), :, :].rearrange("a p (k c) -> (a p) k c", c=P)

            with sp.Fori(0, DEPTH) as l:
                sp.wait_ge(par_done, l * 3 + FREE)
                sp.dma_start(par_next[:], params_in[bass.ds(l, 1), :, :].rearrange("a p c -> (a p) c")).then_inc(params_in_s, 16)
                for u in range(2):
                    load(l, u, u, full(l * 82 + u), DC, back=2)
                with sp.Fori(0, (PROJ - 2) // RAW) as i:
                    for b in range(2, RAW + 2):
                        load(l, i * RAW + b, b % RAW, full(l * 82 + i * RAW + b), DC)
                with sp.Fori(0, DC // 2) as i:
                    for b in range(12):
                        j, b6 = b // 6, b % 6
                        if b6 < 3:
                            src = full(l * 82 + i * 6 + (PROJ + j * 3 + b6))
                        else:
                            src = w_mix[bass.ds(l * 24 + i * 6 + (j * 3 + b6 - 3), 1), :, :].rearrange("a p (k c) -> (a p) k c", c=P)
                        load(l, i * 12 + (PROJ + b), (PROJ + b) % RAW, src, DC if b6 < 3 else BR)
                with sp.Fori(0, DC // RAW) as i:
                    for b in range(RAW):
                        load(l, i * RAW + (U_OUT + b), (U_OUT + b) % RAW, full(l * 82 + i * RAW + (74 + b)), DC)
            for t in range(NT):
                for half in range(2):
                    sp.wait_ge(post_x[half], t + 1)
                sp.dma_start(out[t * P:(t + 1) * P, :], stage[:, t, :]).then_inc(out_s, 16)
            sp.wait_ge(out_s, 16 * NT)

        @block.gpsimd
        def _(pool):
            pool.memset(ones[:], 1.0).then_inc(ones_ready, 1)
            pool.memset(pad[:], 0.0).then_inc(ones_ready, 1)
            pool.memset(decay_r[:].bitcast(F32), 0.0).then_inc(ones_ready, 1)
            pool.sem_inc(split_full, RAW)
            for free in (*acc_free, spare_free, *score_free, *turn_free, out_free, mix_f, mix_ready, par_done):
                pool.sem_inc(free, FREE)

            def split(l, u, slot, raw, nk):
                pool.wait_ge(w_hi_done, l * UNITS + u + 1)
                pool.tensor_tensor(w_lo[:, slot, 0:nk, :], w_raw[:, raw, 0:nk, :], w_hi[:, slot, 0:nk, :].bitcast(F32),
                                   ALU.subtract).then_inc(split_full, 1)

            with pool.Fori(0, DEPTH) as l:
                for u in range(3):
                    split(l, u, u % SLOTS, u, DC)
                for c in range(1, DC, 2):
                    pool.wait_ge(h_hi_ready, l * DC + c + 1)
                    pool.tensor_tensor(h_lo[:, c, :], pad[:, 1, 3:3 + SEQ], h_hi[:, c, :].bitcast(F32), ALU.subtract).then_inc(h_odd, 1)
                with pool.Fori(0, (PROJ - 3) // RAW) as i:
                    for b in range(3, RAW + 3):
                        split(l, i * RAW + b, b % SLOTS, b % RAW, DC)
                for u in range(3 + (PROJ - 3) // RAW * RAW, PROJ):
                    split(l, u, u % SLOTS, u % RAW, DC)
                with pool.Fori(0, DC // 2) as i:
                    for b in range(12):
                        split(l, i * 12 + (PROJ + b), b % SLOTS, (PROJ + b) % RAW, DC if b % 6 < 3 else BR)
                with pool.Fori(0, DC // RAW) as i:
                    for b in range(RAW):
                        split(l, i * RAW + (U_OUT + b), b % SLOTS, (U_OUT + b) % RAW, DC)

        @block.tensor
        def _(pe):
            pe.wait_ge(consts_in_s[0], 16)
            for c in range(DC):
                if c % 2 == 0:
                    pe.wait_ge(x_in_s[c // 2], 16)
                if c >= 2:
                    pe.wait_ge(x_step, c - 1)
                for t in range(NT):
                    last = pe.transpose(ps_s[c % 2][:, t * P:(t + 1) * P], stage[:, t, c * P:(c + 1) * P], ident)
                last.then_inc(pre_t, 1)
            pe.wait_ge(x_step, DC)
            pe.wait_ge(ones_ready, 3)
            pe.wait_ge(const_ready, 3)
            pe.transpose(spare[:, 0:P], ident, ident).then_inc(acc_full, SLOTS)

            def product(l, u, slot, uses, hi, lo, nk, first=0, to=PASSES, per_chunk=None):
                if first == 0:
                    pe.wait_ge(w_hi_done, l * UNITS + u + 1)
                    pe.wait_ge(acc_free[slot], l * (UNITS // 2) + uses + FREE)
                for i in range(first, min(to, 3 * nk)):
                    if i == 2 * nk:
                        pe.wait_ge(split_full, l * UNITS + u + (RAW + 1))
                    k = i // 2 if i < 2 * nk else i - 2 * nk
                    if per_chunk and i < 2 * nk and i % 2 == 0:
                        per_chunk(k)
                    w, x = (w_lo, hi) if i >= 2 * nk else (w_hi, lo if i % 2 else hi)
                    last = pe.matmul(acc[slot][:, :], w[:, slot, k, :], x[:, k, :], start=(i == 0), stop=(i == 3 * nk - 1))
                if to == PASSES:
                    last.then_inc(acc_full, 1)

            def use_spare(l, step):
                pe.wait_ge(spare_free, l * SPARE_USES + SPARE_USE[step] + 2 + FREE)

            def norm_sum(n):
                pe.wait_ge(spare_free, n * SPARE_USES + FREE)
                pe.wait_ge(sq_ready, n + 1)
                for t in range(NT):
                    last = pe.matmul(spare[:, t:t + 1], norm[:, t * P:(t + 1) * P], ones[:, 0:1], start=True, stop=True)
                last.then_inc(spare_full, 1)

            def norm_spread(n):
                pe.wait_ge(spread_ready, n + 1)
                pe.matmul(spare[:, :], ones[:, 0:P], turn[:, :], start=True, stop=True).then_inc(spare_full, 1)

            def scores_bank(l, step):
                use = SCORE_USE[step]
                pe.wait_ge(score_free[use % 2], l * (SCORE_USES // 2) + use // 2 + FREE)
                return ps_s[use % 2]

            with pe.Fori(0, DEPTH) as l:
                for kind, n in SEQUENCE:
                    step = (kind, n)
                    if kind == "passes":
                        n, first, to = n
                        product(l, n, n % 2, n // 2, h_hi if n >= XG_UNITS else xg_hi, h_lo if n >= XG_UNITS else xg_lo, DC, first, to,
                                (lambda k: pe.wait_ge(xg_ready, l * DC + k + 1)) if n == 0 else
                                (lambda k: pe.wait_ge((h_even, h_odd)[k % 2], l * (DC // 2) + k // 2 + 1)) if n == XG_UNITS else None)
                    elif kind == "norm_sum":
                        norm_sum(l)
                    elif kind == "norm_spread":
                        norm_spread(l)
                    elif kind == "turn_iw":
                        use_spare(l, step)
                        pe.wait_ge(small_ready, l + 1)
                        hold(pe, "pe")
                        for t in range(NT):
                            last = pe.transpose(spare[:, t * IDX_HEADS:(t + 1) * IDX_HEADS],
                                                iw_row[:, t * P:(t + 1) * P], ident[0:IDX_HEADS, 0:IDX_HEADS])
                        last.then_inc(spare_full, 1)
                    elif kind == "turn_v":
                        use_spare(l, step)
                        pe.wait_ge(evac, evacs(l, n))
                        for t in range(NT):
                            last = pe.transpose(spare[:, t * P:(t + 1) * P], pad[:, n % 2, 3 + t * P:3 + (t + 1) * P], ident)
                        last.then_inc(spare_full, 1)
                    elif kind == "index":
                        t, h = n
                        bank = scores_bank(l, step)
                        pe.wait_ge(roped, l * ROPES + ROPE[("rope", U_IK)] + 1)
                        b = h % 2 * HD
                        pe.matmul(bank[:, 0:(t + 1) * P], iq[b:b + HD, h // 2, t * P:(t + 1) * P],
                                  ik[b:b + HD, 0:(t + 1) * P], start=True, stop=True).then_inc(score_full, 1)
                    elif kind == "scores":
                        branch, h, t = item(n)
                        bank = scores_bank(l, step)
                        w = (t + 1) * P
                        if branch == "a":
                            pe.wait_ge(roped, l * ROPES + ROPES)
                            b = h // BR * HD
                            pe.matmul(bank[:, 0:w], aq[b:b + HD, h % BR, t * P:w], ak[b:b + HD, 0:w],
                                      start=True, stop=True).then_inc(score_full, 1)
                        elif branch == "b":
                            pe.wait_ge(evac, evacs(l, U_BV - 1))
                            b = h % 2 * HD
                            pe.matmul(bank[:, 0:w], bq[b:b + HD, h // 2, t * P:w], bk[b:b + HD, h // 2, 0:w],
                                      start=True, stop=True).then_inc(score_full, 1)
                        else:
                            pe.wait_ge(decay_ready, l + 1)
                            for s in range(t + 1):
                                o = SUM_AT[s] + (t - s) * P
                                pe.matmul(bank[:, s * P:(s + 1) * P], sel_r[:, h * P:(h + 1) * P], decay_r[:, o:o + P],
                                          start=True, stop=(s < t))
                            pe.matmul(bank[:, t * P:w], ident_b[:, :], causal_b[:, :], start=False, stop=True).then_inc(score_full, 1)
                            pe.wait_ge(turn_free[n % 2], l * (ITEMS // 2) + n // 2 + FREE)
                            pe.wait_ge(conv_done, l * 2 * CH + 2 * CH)
                            for s in range(t + 1):
                                last = pe.matmul(ps_t[n % 2][:, s * P:(s + 1) * P], ck[:, h, s * P:(s + 1) * P],
                                                 cq[:, h, t * P:w], start=True, stop=True)
                            last.then_inc(turn_full, 1)
                    elif kind == "turn_p":
                        branch, h, t = item(n)
                        if branch != "c":
                            pe.wait_ge(turn_free[n % 2], l * (ITEMS // 2) + n // 2 + FREE)
                            pe.wait_ge(prob_ready, l * ITEMS + n + 1)
                            for s in range(t + 1):
                                last = pe.transpose(ps_t[n % 2][:, s * P:(s + 1) * P], prob[:, n % 3, s * P:(s + 1) * P], ident)
                            last.then_inc(turn_full, 1)
                    elif kind == "values":
                        branch, h, t = item(n)
                        pe.wait_ge(turn_free[n % 2], l * (ITEMS // 2) + n // 2 + 1 + FREE)
                        g, place, size = group(n)
                        if place == 0:
                            pe.wait_ge(out_free, l * GROUPS + g + FREE)
                        if branch != "c":
                            pe.wait_ge(spare_free, l * SPARE_USES + SPARE_USE[("turn_v", U_AV if branch == "a" else U_CQ - 1)] + 3 + FREE)
                            v, f = (av, h // BR * HD) if branch == "a" else (bv, h * HD)
                            for s in range(t + 1):
                                last = pe.matmul(ps_o[:, place * HD:(place + 1) * HD], prob_t[:, n % 2, s * P:(s + 1) * P],
                                                 v[:, s, f:f + HD], start=(s == 0), stop=(s == t))
                        else:
                            pe.wait_ge(spare_free, l * SPARE_USES + SPARE_USE[("turn_v", U_AZ - 1)] + 3 + FREE)
                            pe.wait_ge(ones_col, l + 1)
                            for s in range(t + 1):
                                last = pe.matmul(ps_o[:, place * 2 * P:place * 2 * P + P + 1], prob_t[:, n % 2, s * P:(s + 1) * P],
                                                 cv[:, s, h, :], start=(s == 0), stop=(s == t))
                        last.then_inc(out_full, 1)
                    elif kind in ("z_a", "z_b", "z_c"):
                        use_spare(l, step)
                        if kind == "z_c":
                            pe.wait_ge(normed, l + 1)
                        else:
                            pe.wait_ge(out_free, l * GROUPS + (8 if kind == "z_a" else 16) + FREE)
                        for t in range(NT):
                            last = pe.transpose(spare[:, t * P:(t + 1) * P], att[kind[2]][:, t, n * P:(n + 1) * P], ident)
                        last.then_inc(spare_full, 1)
                    elif kind == "turn_c":
                        use_spare(l, step)
                        pe.wait_ge(floor_ready, l + 1)
                        hold(pe, "pe")
                        for t in range(NT):
                            pe.transpose(spare[:, t * CH:(t + 1) * CH], source[:, t * P:(t + 1) * P], ident[0:CH, 0:CH])
                            last = pe.transpose(spare[:, (NT + t) * CH:(NT + t + 1) * CH], run_max[:, t * P:(t + 1) * P],
                                                ident[0:CH, 0:CH])
                        last.then_inc(spare_full, 1)
                    elif kind == "out_gate":
                        use_spare(l, step)
                        pe.wait_ge(evac, evacs(l, U_CO + n))
                        for t in range(NT):
                            last = pe.transpose(spare[:, t * P:(t + 1) * P], (z_tanh, z)[n % 2][:, t * P:(t + 1) * P], ident)
                        last.then_inc(spare_full, 1)
                with pe.Fori(0, DC) as j:
                    for b in range(3):
                        product(l, j * 6 + (PROJ + b), b % 2, j * 3 + (PROJ // 2 + b // 2), h_hi, h_lo, DC)
                    for b, (hi, lo) in enumerate(((ya_hi, ya_lo), (yb_hi, yb_lo), (yc_hi, yc_lo))):
                        pe.wait_ge(y_ready, l * 12 + 4 * b + 4)
                        product(l, j * 6 + (PROJ + 3 + b), (3 + b) % 2, j * 3 + (PROJ // 2 + (3 + b) // 2), hi, lo, BR)
                product(l, U_OUT, 0, U_OUT // 2, merged_hi, merged_lo, DC, per_chunk=
                        lambda k: pe.wait_ge(mix_ready, l * DC + (k + 1 + FREE)))
                product(l, U_OUT + 1, 1, U_OUT // 2, merged_hi, merged_lo, DC)
                with pe.Fori(1, DC // 2) as i:
                    for b in range(2):
                        product(l, i * 2 + (U_OUT + b), b, i + U_OUT // 2, merged_hi, merged_lo, DC)
            norm_sum(DEPTH)
            for half in range(2):
                pe.wait_ge(post_f[half], DC // 2)
            for n in range(2 * NT):
                t, half = n // 2, n % 2
                if n >= 4:
                    pe.wait_ge(post_x[half], t - 1)
                for c in range(4):
                    last = pe.transpose((ps_s, ps_t)[t % 2][half][:, c * P:(c + 1) * P], xT[:, half * 4 + c, t * P:(t + 1) * P], ident)
                last.then_inc(post_t, 1)

        @block.scalar
        def _(act):
            act.dma_start(consts[:, P:KCOLS], consts_in[:, P:KCOLS]).then_inc(consts_in_s[1], 16)
            act.wait_ge(consts_in_s[2], 16)
            for c in range(DC):
                act.wait_ge(pre_t, c + 1)
                act.activation(xT[:, c, :], ps_s[c % 2][:, :], ACT.Copy).then_inc(x_step, 1)
                if c < DC - 1:
                    act.wait_ge(x_step, c + 1)
                    act.activation(xg_hi[:, c, :], xT[:, c, :], ACT.Copy, scale=gains[:, c:c + 1]).then_inc(xg_hi_done, 1)
            act.wait_ge(consts_in_s[1], 16)
            act.activation(ident_b[:, :], ident, ACT.Copy).then_inc(const_ready, 1)
            act.activation(causal_b[:, :], consts[:, K_CAUSAL:K_CAUSAL + P], ACT.Copy).then_inc(const_ready, 1)

            act.activation(sel_r[:, :], consts[0:36, K_SEL:K_SEL + CH * P], ACT.Copy).then_inc(const_ready, 1)

            def high_part(l, first, uses, b, nk=DC):
                raw, slot = b % RAW, b % SLOTS
                act.wait_ge(raw_full[raw], (l * RAW_USES[raw] + uses + (b // RAW + 1)) * 16)
                act.wait_ge(acc_full, l * UNITS + first + (b + 1))
                act.activation(w_hi[:, slot, 0:nk, :], w_raw[:, raw, 0:nk, :], ACT.Copy).then_inc(w_hi_done, 1)

            with act.Fori(0, DEPTH) as l:
                high_part(l, 0, 0, 0)
                act.wait_ge(x_step, l * DC + DC)
                act.activation(xg_hi[:, DC - 1, :], xT[:, DC - 1, :], ACT.Copy, scale=gains[:, bass.ds(l * DC + (DC - 1), 1)])\
                   .then_inc(xg_hi_done, 1)
                high_part(l, 0, 0, 1)
                def z_tile(zn, which):
                    return ((z_tanh[:, :], z[:, :]) if zn < 8 or zn % 2 == 0 else (prob[:, 0, :], prob[:, 1, :]))[which]

                def read_sums(n):
                    act.wait_ge(acc_full, l * UNITS + n + (SLOTS + 1))
                    src, free = acc[n % 2][:, :], acc_free[n % 2]
                    bias, half = par[:, n:n + 1], par_half[:, n:n + 1]
                    if U_AZ <= n < U_CO or n >= U_CZ:
                        zn = n - U_AZ if n < U_CO else n - U_CZ + 2 * BR
                        before = zn - (1 if n <= U_CZ else 2)
                        if before >= 0:
                            act.wait_ge(gated_ready, l * 12 + before + 1)
                        if n == U_CZ:
                            act.wait_ge(og_used, l * CH + CH)
                        act.activation(z_tile(zn, 0), src, ACT.Tanh, bias=half, scale=0.5)
                        act.activation(z_tile(zn, 1), src, ACT.Identity, bias=bias).then_inc(z_ready, 1)
                        act.wait_ge(z_ready, l * 12 + zn + 1)
                        act.sem_inc(free, 1)
                        act.sem_inc(evac, 1)
                        return
                    if U_CO <= n < U_CZ:
                        act.wait_ge(gated_ready, l * 12 + 8)
                        if n >= U_CO + 2:
                            act.wait_ge(og_used, l * CH + n - U_CO - 1)
                        act.activation((z_tanh, z)[n % 2][:, :], src, ACT.Tanh, bias=half, scale=0.5).then_inc(evac, 1)
                        act.wait_ge(evac, evacs(l, n))
                        act.sem_inc(free, 1)
                        return
                    scale = 1.0
                    if n < XG_UNITS:
                        act.activation(iq[:, n, :] if n < U_IK else ik[:, :], src, ACT.Copy).then_inc(evac, 1)
                        act.wait_ge(evac, evacs(l, n))
                        act.sem_inc(free, 1)
                        return
                    if n == U_AK:
                        dst = ak[:, :]
                    elif U_AQ <= n < U_BQ:
                        dst, scale, bias = aq[:, n - U_AQ, :], HD ** -0.5, par_eighth[:, n:n + 1]
                    elif U_BQ <= n < U_BK:
                        dst, scale, bias = bq[:, n - U_BQ, :], HD ** -0.5, par_eighth[:, n:n + 1]
                    elif U_BK <= n < U_BV:
                        dst = bk[:, n - U_BK, :]
                    else:
                        dst = pad[:, n % 2, 3:3 + SEQ]
                        if n == U_AV:
                            act.wait_ge(h_even, (l + 1) * (DC // 2))
                            act.wait_ge(h_odd, (l + 1) * (DC // 2))
                        elif U_CQ <= n - 2 < U_CV:
                            act.wait_ge(conv_sum, l * 8 + n - 2 - U_CQ + 1)
                        elif n - 2 >= U_BV:
                            act.wait_ge(spare_full, l * SPARE_USES + SPARE_USE[("turn_v", n - 2)] + 3)
                    act.activation(dst, src, ACT.Identity, bias=bias, scale=scale).then_inc(evac, 1)
                    act.wait_ge(evac, evacs(l, n))
                    act.sem_inc(free, 1)

                for kind, n in SEQUENCE:
                    step = (kind, n)
                    if kind == "unit":
                        if n != U_SMALL:
                            read_sums(n)
                        high_part(l, 0, 0, n + 2)
                    elif kind == "norm_sum":
                        act.wait_ge(params_in_s, l * 16 + 16)
                        act.wait_ge(mean_ready, l + 1)
                        act.activation(tok[:, :], tok[:, :], ACT.Sqrt).then_inc(std_ready, 1)
                        act.activation(par[:, :], par_next[:, :], ACT.Copy).then_inc(par_done, 1)
                        act.activation(par_half[:, :], par_next[:, :], ACT.Copy, scale=0.5).then_inc(par_done, 1)
                        act.activation(par_eighth[:, :], par_next[:, :], ACT.Copy, scale=HD ** -0.5).then_inc(par_done, 1)
                        act.wait_ge(par_done, l * 3 + 3 + FREE)
                    elif kind == "h":
                        act.wait_ge(hf_ready, l * DC + n + 1)
                        act.activation(h_hi[:, n, :], pad[:, n % 2, 3:3 + SEQ], ACT.Copy).then_inc(h_hi_ready, 1)
                    elif kind == "turn_v":
                        act.wait_ge(spare_full, l * SPARE_USES + SPARE_USE[step] + 3)
                        if n == U_AV:
                            dst = av[:, :, :]
                        else:
                            dst = bv[:, :, (n - U_BV) * P:(n - U_BV + 1) * P] if n < U_CQ else cv[:, :, n - U_CV, 0:P]
                        act.activation(dst, spare[:, :].rearrange("p (t c) -> p t c", t=NT), ACT.Copy).then_inc(spare_free, 1)
                    elif kind == "conv_gate":
                        act.wait_ge(conv_sum, l * 8 + n + 1)
                        act.activation(z_tanh[:, :], turn[:, :], ACT.Tanh, scale=0.5).then_inc(conv_tanh, 1)
                    elif kind == "index":
                        t, h = n
                        use = SCORE_USE[step]
                        act.wait_ge(score_full, l * SCORE_USES + use + 1)
                        if (t, h) > (1, 1):
                            act.wait_ge(score_part, l * 12 + (t - 1) * 4 + h - 1)
                        act.activation(prob[:, h % 2, 0:(t + 1) * P], ps_s[use % 2][:, 0:(t + 1) * P], ACT.Relu)\
                           .then_inc(score_free[use % 2], 1)
                    elif kind == "rel_bias":
                        if n >= 2:
                            act.wait_ge(max_ready, l * 64 + 32 + 4 * (n - 1))
                        act.dma_start(rel[:, n % 2, :], rel_in[bass.ds(l * HEADS + n, 1), :, :].rearrange("a p k -> (a p) k"))\
                           .then_inc(rel_in_s[n % 2], 16)
                    elif kind == "exp":
                        branch, h, t = item(n)
                        if branch != "c":
                            act.wait_ge(max_ready, l * 64 + n + 1)
                            act.activation(prob[:, n % 3, 0:(t + 1) * P], prob[:, n % 3, 0:(t + 1) * P], ACT.Exp,
                                           bias=neg_max[:, n % 4:n % 4 + 1], scale=-1.0,
                                           accum_out=row_sum[:, n % 8:n % 8 + 1]).then_inc(prob_ready, 1)
                        else:
                            use = SCORE_USE[("scores", n)]
                            act.wait_ge(score_full, l * SCORE_USES + use + 1)
                            if n < 67:
                                act.wait_ge(turn_full, l * ITEMS + n - 2)
                            else:
                                act.wait_ge(turn_free[(n - 3) % 2], l * (ITEMS // 2) + (n - 3) // 2 + 1 + FREE)
                            if n == 64:
                                act.wait_ge(spare_free, l * SPARE_USES + SPARE_USE[("turn_c", 0)] + 3 + FREE)
                            for s in range(t + 1):
                                last = act.activation(prob[:, n % 3, s * P:(s + 1) * P], ps_s[use % 2][:, s * P:(s + 1) * P],
                                                      ACT.Exp, bias=source_t[:, s, h:h + 1])
                            last.then_inc(prob_ready, 1)
                            act.wait_ge(prob_ready, l * ITEMS + n + 1)
                            act.sem_inc(score_free[use % 2], 1)
                    elif kind == "turn_p":
                        branch, h, t = item(n)
                        if branch != "c":
                            act.wait_ge(turn_full, l * ITEMS + n + 1)
                            if n >= 2:
                                act.wait_ge(out_full, l * ITEMS + n - 1)
                            act.activation(prob_t[:, n % 2, 0:(t + 1) * P], ps_t[n % 2][:, 0:(t + 1) * P], ACT.Copy)\
                               .then_inc(turn_free[n % 2], 1)
                    elif kind == "y_split":
                        act.wait_ge(gated_ready, l * 12 + n + 1)
                        act.activation((ya_hi, yb_hi, yc_hi)[n // BR][:, n % BR, :], gated[:, :], ACT.Copy).then_inc(y_hi_ready, 1)
                    elif step == ("rows", 0):
                        act.wait_ge(neg_abs, l + 1)
                        act.activation(log1p, log1p, ACT.Exp).then_inc(log_ready, 1)
                        act.wait_ge(log_ready, l * 2 + 1)
                        act.activation(log1p, log1p, ACT.Ln, bias=ones[0:CH, 0:1]).then_inc(log_ready, 1)
                    elif kind == "row_parts":
                        act.wait_ge(rows_ready, l + 1)
                        act.activation(decay_r[0:CH, :], decay[:, :], ACT.Copy).then_inc(rows_hi, 1)
                        act.activation(run_max[:, :], run_max[:, :], ACT.Exp, scale=-1.0).then_inc(floor_ready, 1)
                    elif kind == "deviation":
                        act.wait_ge(var_ready, l + 1)
                        act.activation(dev[:, :, :], dev[:, :, :], ACT.Sqrt).then_inc(dev_ready, 1)

                act.wait_ge(y_ready, l * 12 + 12)
                with act.Fori(0, DC // 2) as i:
                    for j in range(2):
                        for b in range(3):
                            act.wait_ge(acc_full, l * UNITS + i * 12 + (PROJ + 6 * j + b + SLOTS + 1))
                            if b == 0:
                                act.wait_ge(mix_f, l * DC + i * 2 + (j + FREE))
                            act.activation(prob[:, b, :], acc[b % 2][:, :], ACT.Tanh,
                                           bias=par_half[:, bass.ds(i * 2 + (C_GATE + DC * b + j), 1)], scale=0.5).then_inc(gate_ready, 1)
                            act.wait_ge(gate_ready, l * 24 + i * 6 + (3 * j + b + 1))
                            act.sem_inc(acc_free[b % 2], 1)
                            high_part(l, i * 12, i * 3, PROJ + 6 * j + b + 2, DC if b == 0 else BR)
                        high_part(l, i * 12, i * 3, PROJ + 6 * j + 5, BR)
                        high_part(l, i * 12, i * 3, PROJ + 6 * j + 6)
                        act.wait_ge(mix_f, l * DC + i * 2 + (j + 1 + FREE))
                        act.activation(merged_hi[:, bass.ds(i * 2 + j, 1), :], gated[:, :].rearrange("p (a n) -> p a n", a=1), ACT.Copy,
                                       scale=0.5).then_inc(mix_hi, 1)
                        high_part(l, i * 12, i * 3, PROJ + 6 * j + 7)
                act.activation(tok[:, 0:1], ones[:, 0:1], ACT.Sqrt)
                for c in range(DC):
                    if c + 2 < DC:
                        high_part(l, 0, 0, U_OUT + 2 + c)
                    if c == DC - 1:
                        break
                    act.wait_ge(x_step, l * DC + (DC + c + 1))
                    act.activation(xg_hi[:, c, :], xT[:, c, :], ACT.Copy, scale=gains[:, bass.ds(l * DC + (DC + c), 1)])\
                       .then_inc(xg_hi_done, 1)
            for c in range(DC // 2, DC):
                act.activation(xT[:, c, :], xT[:, c, :], ACT.Copy, scale=gains[:, DEPTH * DC + c:DEPTH * DC + c + 1]).then_inc(post_f[1], 1)
                if c == DC - 3:
                    act.wait_ge(mean_ready, DEPTH + 1)
                    act.activation(tok[:, :], tok[:, :], ACT.Sqrt).then_inc(std_ready, 1)
            act.wait_ge(tok_ready, DEPTH + 1)
            for t in range(NT):
                act.wait_ge(post_t, 2 * t + 2)
                act.activation(stage[:, t, SEQ:2 * SEQ], (ps_s, ps_t)[t % 2][1][:, :], ACT.Copy, scale=tok[:, t:t + 1])\
                   .then_inc(post_x[1], 1)

        @block.vector
        def _(dve):
            count = [0]

            def link(ins):
                count[0] += 1
                ins.then_inc(chain, 1)
                dve.wait_ge(chain, base[0] + count[0])

            base = [0]
            dve.wait_ge(ones_ready, 3)
            dve.wait_ge(consts_in_s[2], 16)
            for c in range(DC):
                dve.wait_ge(x_step, c + 1)
                if c < DC - 1:
                    dve.wait_ge(xg_hi_done, c + 1)
                    dve.scalar_tensor_tensor(xg_lo[:, c, :], xT[:, c, :], gains[:, c:c + 1], xg_hi[:, c, :].bitcast(F32),
                                             ALU.mult, ALU.subtract).then_inc(xg_ready, 1)
                if c == 0:
                    link(dve.tensor_tensor(norm[:, :], xT[:, c, :], xT[:, c, :], ALU.mult))
                else:
                    link(dve.tensor_tensor(turn[:, :], xT[:, c, :], xT[:, c, :], ALU.mult))
                    ins = dve.tensor_tensor(norm[:, :], norm[:, :], turn[:, :], ALU.add)
                    link(ins) if c < DC - 1 else ins.then_inc(sq_ready, 1)
            PRE = count[0]
            count[0] = 0

            def norm_mean(n):
                dve.wait_ge(spare_full, n * SPARE_USES + 1)
                dve.tensor_scalar(tok[:, :], spare[:, 0:NT], 1.0 / D, EPS, ALU.mult, ALU.add).then_inc(mean_ready, 1)

            def norm_factor(n):
                dve.wait_ge(std_ready, n + 1)
                dve.reciprocal(tok[:, :], tok[:, :]).then_inc(tok_ready, 1)
                dve.wait_ge(tok_ready, n + 1)

            def norms(n):
                norm_mean(n)
                norm_factor(n)
                dve.tensor_tensor(turn[:, :].rearrange("p (t q) -> p t q", t=NT), ident.unsqueeze(1).broadcast_to([P, NT, P]),
                                  tok[:, :].unsqueeze(2).broadcast_to([P, NT, P]), ALU.mult).then_inc(spread_ready, 1)
                dve.sem_inc(spare_free, 1)
                dve.wait_ge(spare_full, n * SPARE_USES + 2)

            with dve.Fori(0, DEPTH) as l:
                base[0] = l * DVE_STEPS + PRE
                def h_lo_part(c):
                    dve.wait_ge(h_hi_ready, l * DC + c + 1)
                    dve.tensor_tensor(h_lo[:, c, :], pad[:, 0, 3:3 + SEQ], h_hi[:, c, :].bitcast(F32), ALU.subtract).then_inc(h_even, 1)

                dve.wait_ge(xg_hi_done, l * DC + DC)
                dve.scalar_tensor_tensor(xg_lo[:, DC - 1, :], xT[:, DC - 1, :], gains[:, bass.ds(l * DC + (DC - 1), 1)],
                                         xg_hi[:, DC - 1, :].bitcast(F32), ALU.mult, ALU.subtract).then_inc(xg_ready, 1)
                for kind, n in SEQUENCE:
                    step = (kind, n)
                    if kind == "norm_sum":
                        norms(l)
                        dve.wait_ge(par_done, l * 3 + 1 + FREE)
                    elif kind == "h":
                        if n >= 2:
                            dve.wait_ge((h_even, h_odd)[n % 2], l * (DC // 2) + n // 2)
                        dve.scalar_tensor_tensor(pad[:, n % 2, 3:3 + SEQ], xT[:, n, :], par[:, C_NORM + n:C_NORM + n + 1], spare[:, :],
                                                 ALU.mult, ALU.mult).then_inc(hf_ready, 1)
                        if n % 2:
                            h_lo_part(n - 1)
                    elif kind == "unit" and n == U_SMALL:
                        dve.wait_ge(acc_full, l * UNITS + n + (SLOTS + 1))
                        src = acc[n % 2]
                        dve.wait_ge(par_done, l * 3 + 3 + FREE)
                        dve.tensor_scalar(i_row[:, :], src[32:32 + CH, :], par[32:32 + CH, n:n + 1], None, ALU.add)
                        dve.tensor_scalar(f_row[:, :], src[64:64 + CH, :], par[64:64 + CH, n:n + 1],
                                          par[64:64 + CH, C_FBIAS:C_FBIAS + 1], ALU.add, ALU.add)
                        link(dve.tensor_scalar(iw_row[:, :], src[0:IDX_HEADS, :], par[0:IDX_HEADS, n:n + 1],
                                               HD ** -0.5 * IDX_HEADS ** -0.5, ALU.add, ALU.mult))
                        dve.sem_inc(acc_free[n % 2], 1)
                        dve.sem_inc(small_ready, 1)
                    elif kind == "turn_iw":
                        dve.wait_ge(spare_full, l * SPARE_USES + SPARE_USE[step] + 3)
                        link(dve.tensor_copy(iw[:, :, :], spare[:, 0:NT * IDX_HEADS].rearrange("p (t h) -> p t h", t=NT)))
                        dve.sem_inc(spare_free, 1)
                    elif kind == "rope":
                        dve.wait_ge(evac, evacs(l, n))
                        t = (iq[:, n, :] if n < U_IK else ik[:, :] if n == U_IK else ak[:, :] if n == U_AK else aq[:, n - U_AQ, :])
                        if n < XG_UNITS:
                            link(dve.tensor_tensor(t, t, spare[:, :], ALU.mult))
                            link(dve.tensor_scalar(t, t, par[:, n:n + 1], None, ALU.add))
                            if n == XG_UNITS - 1:
                                dve.wait_ge(hf_ready, l * DC + DC)
                                dve.sem_inc(spare_free, 1)
                        swap = [i + 8 if i < 8 else i - 8 if i < 16 else i for i in range(32)]
                        hold(dve, "dve")
                        link(dve.stream_shuffle(turn[:, :], t, swap))
                        link(dve.tensor_tensor(turn[:, :], turn[:, :], sin, ALU.mult))
                        link(dve.tensor_tensor(t, t, cos, ALU.mult))
                        dve.tensor_tensor(t, t, turn[:, :], ALU.add).then_inc(roped, 1)
                        dve.wait_ge(roped, l * ROPES + ROPE[step] + 1)
                    elif kind == "index":
                        t, h = n
                        use = SCORE_USE[step]
                        w = (t + 1) * P
                        dve.wait_ge(score_free[use % 2], l * (SCORE_USES // 2) + use // 2 + 1 + FREE)
                        dst = score[:, t % 2, 0:w]
                        if h == 0:
                            dve.tensor_scalar(dst, prob[:, h % 2, 0:w], iw[:, t, h:h + 1], None, ALU.mult).then_inc(score_part, 1)
                        else:
                            dve.scalar_tensor_tensor(dst, prob[:, h % 2, 0:w], iw[:, t, h:h + 1], dst, ALU.mult, ALU.add)\
                               .then_inc(score_part, 1)
                        dve.wait_ge(score_part, l * 12 + (t - 1) * 4 + h + 1)
                        if h == IDX_HEADS - 1:
                            link(dve.memset(score[0:P // 2, t % 2, w - P // 2:w], INADMISSIBLE))
                    elif kind == "topk":
                        t, a, b = n
                        s = score[:, t % 2, 0:(t + 1) * P]
                        for _ in range(a, b):
                            hold(dve, "dve")
                            link(dve.max(top8[:, :], s))
                            hold(dve, "dve")
                            link(dve.match_replace(s, top8[:, :], s, TAKEN))
                        if b == TOPK // 8:
                            link(dve.tensor_scalar(key_mask[:, MASK_AT[t]:MASK_AT[t] + (t + 1) * P], s,
                                                   0.5 * (TAKEN + INADMISSIBLE), NEG, ALU.is_gt, ALU.mult))
                    elif kind == "conv":
                        n, part = n
                        dve.wait_ge(evac, evacs(l, U_CQ + n))
                        x = pad[:, n % 2, :]
                        for tap in ((3, 2), (1, 0))[part]:
                            w = par[:, C_CONVW + tap * 8 + n:C_CONVW + tap * 8 + n + 1]
                            if tap == 3:
                                link(dve.tensor_scalar(turn[:, :], x[:, tap:tap + SEQ], w, par[:, C_CONVB + n:C_CONVB + n + 1],
                                                       ALU.mult, ALU.add))
                            else:
                                ins = dve.scalar_tensor_tensor(turn[:, :], x[:, tap:tap + SEQ], w, turn[:, :], ALU.mult, ALU.add)
                                link(ins) if tap else ins.then_inc(conv_sum, 1)
                    elif kind == "conv_gate":
                        dve.wait_ge(conv_tanh, l * 8 + n + 1)
                        dst = cq[:, n, :] if n < CH else ck[:, n - CH, :]
                        dve.scalar_tensor_tensor(dst, z_tanh[:, :], 1.0, turn[:, :], ALU.add, ALU.mult).then_inc(conv_done, 1)
                        dve.wait_ge(conv_done, l * 8 + n + 1)
                    elif kind == "rel_bias":
                        dve.wait_ge(rel_in_s[n % 2], l * 64 + 16 * (n // 2 + 1))
                        link(dve.memset(rel[0:P // 2, n % 2, SEQ - P // 2:SEQ], NEG))
                    elif kind == "scores":
                        branch, h, t = item(n)
                        use = SCORE_USE[step]
                        w = (t + 1) * P
                        if branch != "c":
                            dve.wait_ge(score_full, l * SCORE_USES + use + 1)
                            if n >= 3:
                                dve.wait_ge(turn_full, l * ITEMS + n - 2)
                            if branch == "b":
                                mask = rel[:, h % 2, SEQ - w:SEQ]
                            else:
                                mask = key_mask[:, MASK_AT[t]:MASK_AT[t] + w] if t else consts[:, K_CHUNK:K_CHUNK + P]
                            hold(dve, "dve")
                            dve.tensor_tensor_reduce(out=prob[:, n % 3, 0:w], in0=ps_s[use % 2][:, 0:w], in1=mask, scale=-1.0,
                                                     scalar=3.0e38, op0=ALU.add, op1=ALU.min,
                                                     accum_out=neg_max[:, n % 4:n % 4 + 1]).then_inc(max_ready, 1)
                            dve.wait_ge(max_ready, l * 64 + n + 1)
                            dve.sem_inc(score_free[use % 2], 1)
                    elif kind == "turn_p":
                        branch, h, t = item(n)
                        if branch == "c":
                            dve.wait_ge(turn_full, l * ITEMS + n + 1)
                            dve.wait_ge(prob_ready, l * ITEMS + n + 1)
                            dve.wait_ge(out_full, l * ITEMS + n - 1)
                            w = (t + 1) * P
                            dve.scalar_tensor_tensor(prob_t[:, n % 2, 0:w], ps_t[n % 2][:, 0:w], 0.25 * P ** -0.5, prob[:, n % 3, 0:w],
                                                     ALU.mult, ALU.mult).then_inc(turn_free[n % 2], 1)
                    elif kind == "values":
                        branch, h, t = item(n)
                        dve.wait_ge(out_full, l * ITEMS + n + 1)
                        g, place, size = group(n)
                        if place < size - 1:
                            continue
                        dve.wait_ge(out_free, l * GROUPS + g + FREE)
                        if branch != "c":
                            o = n % 8 - 3
                            link(dve.reciprocal(row_inv[:, :], row_sum[:, o:o + 4]))
                            dst = (att["a"][:, t, (h - 3) * HD:(h + 1) * HD].rearrange("p (g d) -> p g d", g=4) if branch == "a"
                                   else att["b"][:, :, h * HD:(h + 1) * HD])
                            dve.tensor_tensor(dst, ps_o[:, 0:4 * HD].rearrange("p (g d) -> p g d", g=4),
                                              row_inv[:, :].unsqueeze(2).broadcast_to([P, 4, HD]), ALU.mult).then_inc(out_free, 1)
                        else:
                            pair = ps_o[:, :].rearrange("p (g c) -> p g c", g=2)
                            inv = row_inv[:, 0:2].unsqueeze(2)
                            link(dve.scalar_tensor_tensor(inv, pair[:, :, P:P + 1], -1.0, floor_t[:, t - 1:t + 1, h:h + 1],
                                                          ALU.mult, ALU.max))
                            link(dve.tensor_tensor(inv, inv, pair[:, :, P:P + 1], ALU.max))
                            link(dve.reciprocal(inv, inv))
                            dve.tensor_tensor(att["c"][:, t - 1:t + 1, h * P:(h + 1) * P], pair[:, :, 0:P],
                                              inv.broadcast_to([P, 2, P]), ALU.mult).then_inc(out_free, 1)
                    elif kind in ("z_a", "z_b", "z_c"):
                        zn = "abc".index(kind[2]) * BR + n
                        tanh, zt = (z_tanh[:, :], z[:, :]) if zn < 8 or zn % 2 == 0 else (prob[:, 0, :], prob[:, 1, :])
                        dve.wait_ge(z_ready, l * 12 + zn + 1)
                        link(dve.scalar_tensor_tensor(zt, tanh, 1.0, zt, ALU.add, ALU.mult))
                        half = par_half[:, C_CNORM + n:C_CNORM + n + 1] if kind == "z_c" else 0.5
                        dve.wait_ge(spare_full, l * SPARE_USES + SPARE_USE[step] + 3)
                        dve.scalar_tensor_tensor(gated[:, :], zt, half, spare[:, :], ALU.mult, ALU.mult).then_inc(gated_ready, 1)
                        dve.wait_ge(gated_ready, l * 12 + zn + 1)
                        dve.sem_inc(spare_free, 1)
                    elif kind == "y_split":
                        dve.wait_ge(y_hi_ready, l * 12 + n + 1)
                        dve.tensor_tensor((ya_lo, yb_lo, yc_lo)[n // BR][:, n % BR, :], gated[:, :],
                                          (ya_hi, yb_hi, yc_hi)[n // BR][:, n % BR, :].bitcast(F32), ALU.subtract).then_inc(y_ready, 1)
                        dve.wait_ge(y_ready, l * 12 + n + 1)
                    elif step == ("rows", 0):
                        dve.scalar_tensor_tensor(log1p, f_row[:, :], -1.0, f_row[:, :], ALU.mult, ALU.min).then_inc(neg_abs, 1)
                    elif step == ("rows", 1):
                        dve.wait_ge(log_ready, l * 2 + 2)
                        link(dve.scalar_tensor_tensor(f_row[:, :], f_row[:, :], 0.0, log1p, ALU.min, ALU.subtract))
                        link(dve.tensor_tensor_scan(run_max[:, :], f_row[:, :], i_row[:, :], 0.0, ALU.add, ALU.max))
                    elif kind == "rows":
                        s = n - 2
                        w = SEQ - s * P
                        link(dve.tensor_tensor_scan(decay[:, SUM_AT[s]:SUM_AT[s] + w], ones[0:CH, 0:w], f_row[:, s * P:SEQ], 0.0,
                                                    ALU.mult, ALU.add))
                        link(dve.tensor_tensor(source[:, s * P:(s + 1) * P], i_row[:, s * P:(s + 1) * P],
                                               decay[:, SUM_AT[s]:SUM_AT[s] + P], ALU.subtract))
                        link(dve.tensor_tensor(decay[:, SUM_AT[s]:SUM_AT[s] + w], decay[:, SUM_AT[s]:SUM_AT[s] + w],
                                               run_max[:, s * P:SEQ], ALU.subtract))
                        if s == NT - 1:
                            dve.sem_inc(rows_ready, 1)
                            dve.memset(cv[:, :, :, P:P + 1], 1.0).then_inc(ones_col, 1)
                    elif kind == "turn_c":
                        dve.wait_ge(spare_full, l * SPARE_USES + SPARE_USE[step] + 3)
                        link(dve.tensor_copy(source_t[:, :, :], spare[:, 0:NT * CH].rearrange("p (t h) -> p t h", t=NT)))
                        link(dve.tensor_copy(floor_t[:, :, :], spare[:, NT * CH:2 * NT * CH].rearrange("p (t h) -> p t h", t=NT)))
                        dve.sem_inc(spare_free, 1)
                        dve.wait_ge(rows_hi, l + 1)
                        dve.tensor_tensor(decay_r[32:32 + CH, :], decay[:, :], decay_r[0:CH, :].bitcast(F32), ALU.subtract)\
                           .then_inc(decay_ready, 1)
                    elif kind == "out_gate":
                        dve.wait_ge(spare_full, l * SPARE_USES + SPARE_USE[step] + 3)
                        y = att["c"][:, :, n * P:(n + 1) * P]
                        dve.scalar_tensor_tensor(y, spare[:, :].rearrange("p (t q) -> p t q", t=NT), 1.0, y, ALU.add, ALU.mult)\
                           .then_inc(og_used, 1)
                        dve.wait_ge(og_used, l * CH + n + 1)
                        dve.sem_inc(spare_free, 1)
                        for t in range(NT):
                            link(dve.bn_stats(stats[:, t, :], y[:, t, :]))
                            hold(dve, "dve")
                            link(dve.bn_aggr(moments[:, t, n, :], stats[:, t, :]))
                    elif kind == "deviation":
                        dve.tensor_scalar(dev[:, :, :], moments[:, :, :, 1], 4.0 * EPS, None, ALU.add).then_inc(var_ready, 1)
                        dve.wait_ge(dev_ready, l + 1)
                        link(dve.reciprocal(dev[:, :, :], dev[:, :, :]))
                        for t in range(NT):
                            for h in range(CH):
                                y = att["c"][:, t, h * P:(h + 1) * P]
                                last = dve.tensor_scalar(y, y, moments[:, t, h, 0:1], dev[:, t, h:h + 1], ALU.subtract, ALU.mult)
                        last.then_inc(normed, 1)
                assert count[0] == DVE_STEPS, count[0]
                hold(dve, "dve")

                with dve.Fori(0, DC) as j:
                    for b in range(3):
                        dve.wait_ge(acc_full, l * UNITS + j * 6 + (PROJ + 3 + b + SLOTS + 1))
                        dve.wait_ge(gate_ready, l * 24 + j * 3 + (b + 1))
                        if b == 0:
                            dve.wait_ge(mix_ready, l * DC + j + FREE)
                        dve.scalar_tensor_tensor((gated, z, z)[b][:, :], prob[:, b, :], 1.0, acc[(3 + b) % 2][:, :], ALU.add, ALU.mult)\
                           .then_inc(chain_mix, 1)
                        dve.wait_ge(chain_mix, l * (4 * DC) + j * 4 + ((1, 2, 4)[b]))
                        dve.sem_inc(acc_free[(3 + b) % 2], 1)
                        if b == 1:
                            dve.tensor_tensor(gated[:, :], gated[:, :], z[:, :], ALU.add).then_inc(chain_mix, 1)
                            dve.wait_ge(chain_mix, l * (4 * DC) + j * 4 + 3)
                    dve.tensor_tensor(gated[:, :], gated[:, :], z[:, :], ALU.add).then_inc(mix_f, 1)
                    dve.wait_ge(mix_hi, l * DC + j + 1)
                    dve.scalar_tensor_tensor(merged_lo[:, bass.ds(j, 1), :], gated[:, :].rearrange("p (a n) -> p a n", a=1), 0.5,
                                             merged_hi[:, bass.ds(j, 1), :].bitcast(F32), ALU.mult, ALU.subtract).then_inc(mix_ready, 1)

                dve.memset(norm[:, :], 0.0).then_inc(chain_out, 1)
                dve.wait_ge(chain_out, l * (2 * DC + 1) + 1)
                hold(dve, "dve")
                def x_update(c, chunk, slot):
                    xc, part = xT[:, chunk, :], "p (a n) -> p a n"
                    dve.wait_ge(acc_full, l * UNITS + c + (U_OUT + SLOTS + 1))
                    dve.tensor_tensor(xc, xc, acc[slot][:, :].rearrange(part, a=1), ALU.add).then_inc(x_step, 1)
                    dve.wait_ge(x_step, l * DC + c + (DC + 1))
                    dve.sem_inc(acc_free[slot], 1)
                    dve.tensor_tensor(turn[:, :].rearrange(part, a=1), xc, xc, ALU.mult).then_inc(chain_out, 1)
                    dve.wait_ge(chain_out, l * (2 * DC + 1) + c * 2 + 2)
                    dve.tensor_tensor(norm[:, :], norm[:, :], turn[:, :], ALU.add).then_inc(chain_out, 1)
                    dve.wait_ge(chain_out, l * (2 * DC + 1) + c * 2 + 3)

                def xg_low(c, chunk, gain):
                    dve.wait_ge(xg_hi_done, l * DC + c + (DC + 1))
                    dve.scalar_tensor_tensor(xg_lo[:, chunk, :], xT[:, chunk, :], gain, xg_hi[:, chunk, :].bitcast(F32),
                                             ALU.mult, ALU.subtract).then_inc(xg_ready, 1)

                with dve.Fori(0, DC // 2 - 1) as i:
                    for b in range(2):
                        x_update(i * 2 + b, bass.ds(i * 2 + b, 1), b)
                        xg_low(i * 2 + b, bass.ds(i * 2 + b, 1), gains[:, bass.ds(l * DC + i * 2 + (DC + b), 1)])
                x_update(DC - 2, slice(DC - 2, DC - 1), 0)
                xg_low(DC - 2, slice(DC - 2, DC - 1), gains[:, bass.ds(l * DC + (2 * DC - 2), 1)])
                x_update(DC - 1, slice(DC - 1, DC), 1)
                dve.sem_inc(sq_ready, 1)
            for c in range(DC // 2):
                dve.tensor_scalar(xT[:, c, :], xT[:, c, :], gains[:, DEPTH * DC + c:DEPTH * DC + c + 1], None, ALU.mult)\
                   .then_inc(post_f[0], 1)
                if c == 1:
                    norm_mean(DEPTH)
            norm_factor(DEPTH)
            for t in range(NT):
                dve.wait_ge(post_t, 2 * t + 1)
                dve.tensor_scalar(stage[:, t, 0:SEQ], (ps_s, ps_t)[t % 2][0][:, :], tok[:, t:t + 1], None, ALU.mult).then_inc(post_x[0], 1)


def kernel(**inputs):
    import numpy as np
    import concourse.bacc as bacc
    from concourse.bass_utils import run_bass_kernel_spmd

    a = {k: np.ascontiguousarray(v) for k, v in inputs.items()}
    f32 = a["x"].dtype
    w, b = a["w_in"], a["b_in"]
    half = np.arange(HD)

    def cols(start):
        return np.arange(start, start + P)

    offs = {"aq": 0, "ak": 512, "av": 640, "iq": 768, "ik": 1024, "iw": 1088, "az": 1092, "bq": 1604, "bk": 2116, "bv": 2628,
            "bz": 3140, "cq": 3652, "ck": 4164, "cv": 4676, "ci": 5188, "cf": 5192, "co": 5196, "cz": 5708, "gates": 6220}
    small = np.full(P, -1)
    for at_, name in ((0, "iw"), (32, "ci"), (64, "cf")):
        small[at_:at_ + 4] = offs[name] + np.arange(4)
    units = [cols(offs["iq"]), cols(offs["iq"] + P), np.concatenate([offs["ik"] + half] * 2), small, cols(offs["ak"]), cols(offs["av"])]
    units += [np.concatenate([offs["aq"] + j * HD + half, offs["aq"] + (j + 4) * HD + half]) for j in range(4)]
    for name in ("bq", "bk", "bv", "cq", "ck", "cv", "az", "bz", "co", "cz"):
        units += [cols(offs[name] + j * P) for j in range(4)]
    gate_units = [cols(offs["gates"] + n * D + j * P) for j in range(DC) for n in range(3)]

    def take(m, c):
        padded = np.concatenate([m, np.zeros(m.shape[:-1] + (1,), f32)], axis=-1)
        return padded[..., c]

    def unit(m, c):
        t = take(m, c)
        return t.reshape(DEPTH, -1, P, P).transpose(0, 2, 1, 3).reshape(DEPTH, P, -1)

    wo_units = [unit(a["w_out"], cols(j * P)) for j in range(DC)]
    w_full = np.stack([unit(w, c) for c in units + gate_units] + wo_units, axis=1).reshape(-1, P, D)
    wb = a["w_branch"]
    w_mix = np.stack([unit(wb[:, n], cols(j * P)) for j in range(DC) for n in range(3)], axis=1).reshape(-1, P, BR * P)

    def chunks(m):
        return m.reshape(DEPTH, -1, P).transpose(0, 2, 1)

    fcol = np.zeros((DEPTH, P, 2), f32)
    fcol[:, 64:68, 0] = a["f_bias"]
    params = np.concatenate([np.stack([take(b, c) for c in units], axis=2), chunks(b[:, offs["gates"]:]), chunks(a["norm_g"]),
                             chunks(a["conv_b"]), chunks(a["conv_w"].reshape(DEPTH, -1)), chunks(a["c_norm_w"]), fcol], axis=2)
    dist = np.clip(SEQ - P + np.arange(P)[:, None] - np.arange(SEQ)[None, :], -128, 128) + 128
    rel = a["rel_bias"][:, :, dist].reshape(-1, P, SEQ)

    consts = np.zeros((P, KCOLS), f32)
    consts[:, K_ID:K_ID + P] = np.eye(P)
    p, q = np.arange(P)[:, None], np.arange(P)[None, :]
    consts[:, K_CHUNK:K_CHUNK + P] = np.where(q // 64 <= p // 64, 0.0, NEG)
    consts[:, K_CAUSAL:K_CAUSAL + P] = np.where(p <= q, 0.0, NEG)
    inv = (1.0 / (np.float32(500000.0) ** (np.arange(8, dtype=f32) * np.float32(2.0) / np.float32(16)))).astype(f32)
    ang = np.arange(SEQ, dtype=f32)[None, :] * inv[:, None]
    for s in (0, 64):
        consts[s:s + 64, K_COS:K_COS + SEQ] = 1.0
        for r, sign in ((0, -1.0), (8, 1.0)):
            consts[s + r:s + r + 8, K_COS:K_COS + SEQ] = np.cos(ang)
            consts[s + r:s + r + 8, K_SIN:K_SIN + SEQ] = sign * np.sin(ang)
    for h in range(CH):
        for r in (0, 32):
            consts[r + h, K_SEL + h * P:K_SEL + (h + 1) * P] = 1.0

    arrays = {"x": a["x"].reshape(SEQ, D), "w_full": w_full, "w_mix": w_mix, "params": params, "rel": rel,
              "gains": np.concatenate([a["norm_g"].reshape(-1, P), a["final_g"].reshape(-1, P)]).T, "consts": consts}
    arrays = {k: np.ascontiguousarray(v) for k, v in arrays.items()}
    nc = bacc.Bacc("TRN2", target_bir_lowering=False, num_devices=1, dynamic_dma_scratch_size=1024)
    args = [nc.dram_tensor(k, v.shape, mybir.dt.from_np(v.dtype), kind="ExternalInput").ap() for k, v in arrays.items()]
    out = nc.dram_tensor("out", (SEQ, D), F32, kind="ExternalOutput").ap()
    build(nc, *args, out)
    got = run_bass_kernel_spmd(nc, [arrays], core_ids=[0])
    return got.results[0]["out"].reshape(1, SEQ, D)
```
